# Optimizing a Trainium2 kernel written in Bass

```python
import jax, jax.numpy as jnp
from jax import lax
import numpy as np

D_MODEL = 1024
BATCH = 1
SEQ = 1024
DEPTH = 1
DEC_BATCH = 1
DEC_SEQ = 64
PAST_LEN = 1024

CHUNK = 64
N_META = 16
HEAD_DIM = 64
A_HEADS = D_MODEL // HEAD_DIM
A_KV_HEADS = A_HEADS // 8
WINDOW = 128
WIN_CHUNKS = WINDOW // CHUNK
B_HEADS = D_MODEL // HEAD_DIM
B_KV_HEADS = 1
IDX_HEADS = 8
IDX_DIM = 64
TOPK_MAX = 256
Q_BLOCK = 128
INDEX_SCALE = (IDX_HEADS * IDX_DIM) ** -0.5
D_FF = 4 * D_MODEL
META_SLOTS = 2 * A_KV_HEADS + 2 * B_KV_HEADS
SPLIT_SIZES = (A_HEADS * HEAD_DIM, A_KV_HEADS * HEAD_DIM, A_KV_HEADS * HEAD_DIM,
               B_HEADS * HEAD_DIM, B_KV_HEADS * HEAD_DIM, B_KV_HEADS * HEAD_DIM,
               IDX_HEADS * IDX_DIM, IDX_DIM, IDX_HEADS, D_MODEL, D_MODEL)
D_IN = (A_HEADS + 2 * A_KV_HEADS + B_HEADS + 2 * B_KV_HEADS) * HEAD_DIM + IDX_HEADS * IDX_DIM + IDX_DIM + IDX_HEADS + 2 * D_MODEL
EPS = 1e-6

kernel_name = "hybrid_swa_sink_dsa_stream_step"

def rms_norm(x, g):
    xf = x.astype(jnp.float32)
    y = xf * lax.rsqrt(jnp.mean(xf * xf, axis=-1, keepdims=True) + EPS)
    return (y * g.astype(jnp.float32)).astype(x.dtype)

def alibi_slopes(n_heads, n_kv):
    h = jnp.arange(1, n_heads + 1, dtype=jnp.float32)
    return (2.0 ** (-8.0 * h / n_heads)).reshape(n_kv, n_heads // n_kv)

def project(x, g_pre, w_in):
    p = rms_norm(x, g_pre) @ w_in
    lead = p.shape[:-1]
    offs = [int(o) for o in np.cumsum(SPLIT_SIZES)[:-1]]
    qa, ka, va, qb, kb, vb, qi, ki, wi, ga, gb = jnp.split(p, offs, axis=-1)
    hd = lambda t, n: t.reshape(*lead, n, -1)
    return (hd(qa, A_HEADS), hd(ka, A_KV_HEADS), hd(va, A_KV_HEADS),
            hd(qb, B_HEADS), hd(kb, B_KV_HEADS), hd(vb, B_KV_HEADS),
            hd(qi, IDX_HEADS), ki, wi, ga, gb)

def to_blocks(a, size):
    b, t = a.shape[:2]
    return jnp.moveaxis(a.reshape(b, t // size, size, *a.shape[2:]), 1, 0)

def from_blocks(a):
    nb, b, s = a.shape[:3]
    return jnp.moveaxis(a, 0, 1).reshape(b, nb * s, *a.shape[3:])

def swa_attend(q, k, v, q_pos, k_pos, mk, mv, sinks, slopes):
    b, nq, h, d = q.shape
    s_len, kvh = k.shape[1], k.shape[2]
    g = h // kvh
    qg = q.reshape(b, nq, kvh, g, d) * (d ** -0.5)
    s = jnp.einsum('bqkgd,bskd->bkgqs', qg, k).astype(jnp.float32)
    sm = jnp.einsum('bqkgd,bmkd->bkgqm', qg, mk).astype(jnp.float32)
    qc, kc = q_pos // CHUNK, k_pos // CHUNK
    ok = (k_pos[None, :] >= 0) & (kc[None, :] <= qc[:, None]) & (kc[None, :] >= qc[:, None] - WIN_CHUNKS)
    dist = jnp.abs(q_pos[:, None] - k_pos[None, :]).astype(jnp.float32)
    s = jnp.where(ok, s - slopes[None, :, :, None, None] * dist, -jnp.inf)
    sink = jnp.broadcast_to(sinks.astype(jnp.float32).reshape(kvh, g, 1, 1), (b, kvh, g, nq, 1))
    p = jax.nn.softmax(jnp.concatenate([s, sm, sink], axis=-1), axis=-1).astype(v.dtype)
    out = (jnp.einsum('bkgqs,bskd->bqkgd', p[..., :s_len], v)
           + jnp.einsum('bkgqm,bmkd->bqkgd', p[..., s_len:s_len + mk.shape[1]], mv))
    return out.reshape(b, nq, h * d)

def swa_prompt(q, k, v, mk, mv, sinks, slopes):
    b, t = q.shape[:2]
    nc = t // CHUNK
    pad = ((0, 0), (WIN_CHUNKS, 0), (0, 0), (0, 0), (0, 0))
    kp = jnp.pad(k.reshape(b, nc, CHUNK, *k.shape[2:]), pad)
    vp = jnp.pad(v.reshape(b, nc, CHUNK, *v.shape[2:]), pad)
    k_band = jnp.concatenate([kp[:, j:j + nc] for j in range(WIN_CHUNKS + 1)], axis=2)
    v_band = jnp.concatenate([vp[:, j:j + nc] for j in range(WIN_CHUNKS + 1)], axis=2)
    band_len = (WIN_CHUNKS + 1) * CHUNK

    def step(args):
        q_c, k_c, v_c, c = args
        q_pos = c * CHUNK + jnp.arange(CHUNK)
        k_pos = (c - WIN_CHUNKS) * CHUNK + jnp.arange(band_len)
        return swa_attend(q_c, k_c, v_c, q_pos, k_pos, mk, mv, sinks, slopes)

    out = lax.map(step, (to_blocks(q, CHUNK), jnp.moveaxis(k_band, 1, 0),
                         jnp.moveaxis(v_band, 1, 0), jnp.arange(nc)))
    return from_blocks(out)

def dsa_attend(q, qi, wi, q_pos, k, v, ki, mk, mv, slopes, n_sel):
    b, nq, h, d = q.shape
    s_len, kvh = k.shape[1], k.shape[2]
    g = h // kvh
    rel = jax.nn.relu(jnp.einsum('bqhd,bsd->bqhs', qi, ki).astype(jnp.float32))
    score = jnp.einsum('bqh,bqhs->bqs', wi.astype(jnp.float32), rel) * INDEX_SCALE
    admissible = (jnp.arange(s_len) // CHUNK)[None, :] <= (q_pos // CHUNK)[:, None]
    score = jnp.where(admissible[None], score, -jnp.inf)
    top_val, top_idx = lax.top_k(score, n_sel)
    valid = top_val > -jnp.inf
    gather = jax.vmap(lambda rows, i: rows[i])
    k_sel = gather(k, top_idx)
    v_sel = gather(v, top_idx)
    qg = q.reshape(b, nq, kvh, g, d) * (d ** -0.5)
    s = jnp.einsum('bqkgd,bqnkd->bkgqn', qg, k_sel).astype(jnp.float32)
    dist = jnp.abs(q_pos[None, :, None] - top_idx).astype(jnp.float32)
    s = jnp.where(valid[:, None, None], s - slopes[None, :, :, None, None] * dist[:, None, None], -jnp.inf)
    sm = jnp.einsum('bqkgd,bmkd->bkgqm', qg, mk).astype(jnp.float32)
    p = jax.nn.softmax(jnp.concatenate([s, sm], axis=-1), axis=-1).astype(v.dtype)
    out = (jnp.einsum('bkgqn,bqnkd->bqkgd', p[..., :n_sel], v_sel)
           + jnp.einsum('bkgqm,bmkd->bqkgd', p[..., n_sel:], mv))
    return out.reshape(b, nq, h * d)

def dsa_prompt(q, qi, wi, k, v, ki, mk, mv, slopes, n_sel):
    nb = q.shape[1] // Q_BLOCK

    def step(args):
        q_b, qi_b, wi_b, blk = args
        q_pos = blk * Q_BLOCK + jnp.arange(Q_BLOCK)
        return dsa_attend(q_b, qi_b, wi_b, q_pos, k, v, ki, mk, mv, slopes, n_sel)

    out = lax.map(step, (to_blocks(q, Q_BLOCK), to_blocks(qi, Q_BLOCK),
                         to_blocks(wi, Q_BLOCK), jnp.arange(nb)))
    return from_blocks(out)

def meta_attend(q, k, v, sinks=None):
    m, h, d = q.shape
    kvh = k.shape[1]
    g = h // kvh
    s = jnp.einsum('qkgd,skd->kgqs', q.reshape(m, kvh, g, d) * (d ** -0.5), k).astype(jnp.float32)
    if sinks is not None:
        s = jnp.concatenate([s, jnp.broadcast_to(sinks.astype(jnp.float32).reshape(kvh, g, 1, 1), (kvh, g, m, 1))], -1)
    p = jax.nn.softmax(s, axis=-1)[..., :m].astype(v.dtype)
    return jnp.einsum('kgqs,skd->qkgd', p, v).reshape(m, h * d)

def merge_and_mlp(x, o_a, o_b, g_a, g_b, w_o, g_post_mix, g_pre_mlp, w_up, w_down, g_post_mlp):
    mix = (jax.nn.sigmoid(g_a) * o_a + jax.nn.sigmoid(g_b) * o_b) @ w_o
    x = x + rms_norm(mix, g_post_mix)
    hid = jnp.square(jax.nn.relu(rms_norm(x, g_pre_mlp) @ w_up))
    return x + rms_norm(hid @ w_down, g_post_mlp)

def setup_inputs(seed: int = 0) -> dict:
    key = jax.random.key(seed)
    ks = jax.random.split(key, 20)
    f32 = jnp.float32
    win = min(WINDOW, PAST_LEN)
    nrm = lambda k, shape, sc=1.0: jax.random.normal(k, shape, f32) * sc
    gain = lambda k: 1.0 + 0.05 * jax.random.normal(k, (DEPTH, D_MODEL), f32)
    return {
        "x_prompt": nrm(ks[0], (BATCH, SEQ, D_MODEL)),
        "x_sample": nrm(ks[1], (DEC_BATCH, DEC_SEQ, D_MODEL)),
        "cache_k_a": nrm(ks[2], (DEPTH, DEC_BATCH, win, A_KV_HEADS, HEAD_DIM)),
        "cache_v_a": nrm(ks[3], (DEPTH, DEC_BATCH, win, A_KV_HEADS, HEAD_DIM)),
        "cache_k_b": nrm(ks[4], (DEPTH, DEC_BATCH, PAST_LEN, B_KV_HEADS, HEAD_DIM)),
        "cache_v_b": nrm(ks[5], (DEPTH, DEC_BATCH, PAST_LEN, B_KV_HEADS, HEAD_DIM)),
        "cache_ki_b": nrm(ks[6], (DEPTH, DEC_BATCH, PAST_LEN, IDX_DIM)),
        "cache_meta": nrm(ks[7], (DEPTH, DEC_BATCH, N_META, META_SLOTS, HEAD_DIM)),
        "meta_tokens": nrm(ks[8], (N_META, D_MODEL)),
        "g_pre_mix": gain(ks[9]),
        "w_in": nrm(ks[10], (DEPTH, D_MODEL, D_IN), D_MODEL ** -0.5),
        "attn_sinks": nrm(ks[11], (DEPTH, A_HEADS), 0.5),
        "w_o": nrm(ks[12], (DEPTH, D_MODEL, D_MODEL), D_MODEL ** -0.5),
        "g_post_mix": gain(ks[13]),
        "g_pre_mlp": gain(ks[14]),
        "w_up": nrm(ks[15], (DEPTH, D_MODEL, D_FF), D_MODEL ** -0.5),
        "w_down": nrm(ks[16], (DEPTH, D_FF, D_MODEL), D_FF ** -0.5),
        "g_post_mlp": gain(ks[17]),
    }

def reference(x_prompt, x_sample, cache_k_a, cache_v_a, cache_k_b, cache_v_b, cache_ki_b, cache_meta,
              meta_tokens, g_pre_mix, w_in, attn_sinks, w_o, g_post_mix, g_pre_mlp, w_up, w_down, g_post_mlp):
    xp, xs, meta = x_prompt, x_sample, meta_tokens
    bp, t_p = xp.shape[:2]
    bs, t_s = xs.shape[:2]
    past = cache_k_b.shape[2]
    win = cache_k_a.shape[2]
    win_p = min(WINDOW, t_p)
    slopes_a = alibi_slopes(A_HEADS, A_KV_HEADS)
    slopes_b = alibi_slopes(B_HEADS, B_KV_HEADS)
    n_sel_p = min(TOPK_MAX, t_p // 4)
    n_sel_s = min(TOPK_MAX, (past + t_s) // 4)
    A2 = 2 * A_KV_HEADS
    kap, vap, kbp, vbp, kip, metap, kas, vas, kbs, vbs, kis = ([] for _ in range(11))
    for l in range(DEPTH):
        lw = (w_o[l], g_post_mix[l], g_pre_mlp[l], w_up[l], w_down[l], g_post_mlp[l])
        mq_a, mk_a, mv_a, mq_b, mk_b, mv_b, _, _, _, mg_a, mg_b = project(meta, g_pre_mix[l], w_in[l])
        meta_rows = jnp.concatenate([mk_a, mv_a, mk_b, mv_b], axis=1)
        bc = lambda a, n: jnp.broadcast_to(a, (n,) + a.shape)

        qa, ka, va, qb, kb, vb, qi, ki, wi, ga, gb = project(xp, g_pre_mix[l], w_in[l])
        o_a = swa_prompt(qa, ka, va, bc(mk_a, bp), bc(mv_a, bp), attn_sinks[l], slopes_a)
        o_b = dsa_prompt(qb, qi, wi, kb, vb, ki, bc(mk_b, bp), bc(mv_b, bp), slopes_b, n_sel_p)
        kap.append(ka[:, t_p - win_p:]); vap.append(va[:, t_p - win_p:])
        kbp.append(kb); vbp.append(vb); kip.append(ki); metap.append(bc(meta_rows, bp))
        xp_next = merge_and_mlp(xp, o_a, o_b, ga, gb, *lw)

        cm = cache_meta[l]
        smk_a, smv_a = cm[:, :, :A_KV_HEADS], cm[:, :, A_KV_HEADS:A2]
        smk_b, smv_b = cm[:, :, A2:A2 + B_KV_HEADS], cm[:, :, A2 + B_KV_HEADS:]
        qa, ka, va, qb, kb, vb, qi, ki, wi, ga, gb = project(xs, g_pre_mix[l], w_in[l])
        q_pos = past + jnp.arange(t_s)
        k_band = jnp.concatenate([cache_k_a[l], ka], axis=1)
        v_band = jnp.concatenate([cache_v_a[l], va], axis=1)
        k_pos = past - win + jnp.arange(win + t_s)
        o_a = swa_attend(qa, k_band, v_band, q_pos, k_pos, smk_a, smv_a, attn_sinks[l], slopes_a)
        k_all = jnp.concatenate([cache_k_b[l], kb], axis=1)
        v_all = jnp.concatenate([cache_v_b[l], vb], axis=1)
        ki_all = jnp.concatenate([cache_ki_b[l], ki], axis=1)
        o_b = dsa_attend(qb, qi, wi, q_pos, k_all, v_all, ki_all, smk_b, smv_b, slopes_b, n_sel_s)
        kas.append(k_band[:, t_s:]); vas.append(v_band[:, t_s:])
        kbs.append(kb); vbs.append(vb); kis.append(ki)
        xs_next = merge_and_mlp(xs, o_a, o_b, ga, gb, *lw)

        if l + 1 < DEPTH:
            mo_a = meta_attend(mq_a, mk_a, mv_a, attn_sinks[l])
            mo_b = meta_attend(mq_b, mk_b, mv_b)
            meta = merge_and_mlp(meta, mo_a, mo_b, mg_a, mg_b, *lw)
        xp, xs = xp_next, xs_next
    return (xp, xs,
            jnp.stack(kap), jnp.stack(vap), jnp.stack(kbp), jnp.stack(vbp), jnp.stack(kip), jnp.stack(metap),
            jnp.stack(kas), jnp.stack(vas), jnp.stack(kbs), jnp.stack(vbs), jnp.stack(kis))


_drawn_inputs = setup_inputs


def setup_inputs(seed=0):
    import zlib

    import numpy as np

    out = dict(_drawn_inputs(seed))
    spreads = {}
    factors = {'attn_sinks': 6.13}
    for name, (base, spread) in spreads.items():
        noise = np.random.default_rng([zlib.crc32(name.encode()), seed]).standard_normal(out[name].shape)
        drawn = base * np.exp(spread * noise) if base else spread * noise
        out[name] = __import__('jax').numpy.asarray(drawn.astype(out[name].dtype))
    for name, factor in factors.items():
        out[name] = (out[name] * factor).astype(out[name].dtype)
    return out
```

```python
from contextlib import ExitStack

import concourse.bass as bass
from concourse import mybir

F32 = mybir.dt.float32
F32R = mybir.dt.float32r
ALU = mybir.AluOpType
ACT = mybir.ActivationFunctionType

P = 128
D = 1024
KT = D // P
HD = 64
HEADS = 16
CHUNK = 64
N_PROMPT, N_SAMPLE, N_META = 1024, 64, 16
N_QUERY = N_PROMPT + N_SAMPLE
N_TOK = N_QUERY + N_META
TILES = 9
SAMPLE_TILE = 8
PAST = 1024
WINDOW = 128
IDX_HEADS = 8
TOPK = 256
D_FF = 4 * D
EPS = 1e-6
INDEX_SCALE = (IDX_HEADS * HD) ** -0.5

QA, KA, QB, QI, KI, GA, D_IN = 0, 1024, 1280, 2432, 2944, 3016, 5064
KB = 2304
T_COLS = [(KA, 256), (KB, 128), (KI, 72)]
T_WIDTH = sum(n for _, n in T_COLS)
T_KA, T_VA, T_KB, T_VB, T_KI, T_WI = 0, 128, 256, 320, 384, 448

FAR = 1e30
TAKEN = -3.4e38
UNSEEN = -3.0e38


def slope(h):
    return 2.0 ** (-8.0 * (h + 1) / HEADS)


def tile_rows(t):
    return P if t < SAMPLE_TILE else N_SAMPLE


def tile_tokens(t):
    return P if t < SAMPLE_TILE else N_SAMPLE + N_META


def constants(sb):
    c = {}
    c["ident"] = sb("ident", [P, P])
    c["fold"] = sb("fold", [P, HD])
    c["eps"] = sb("eps", [P, 1])
    c["q_scale"] = sb("q_scale", [P, KT])
    return c


def refine_rstd(dve, step, n, out, rstd, mean_sq, work):
    dve.tensor_scalar(work, rstd, rstd, mean_sq, ALU.mult, ALU.mult).then_inc(step, 1)
    dve.wait_ge(step, n + 1)
    dve.tensor_scalar(work, work, -0.5, 1.5, ALU.mult, ALU.add).then_inc(step, 1)
    dve.wait_ge(step, n + 2)
    dve.tensor_tensor(out, rstd, work, ALU.mult).then_inc(step, 1)
    dve.wait_ge(step, n + 3)


def input_norm(nc, top, c, xT, ps, x_prompt, x_sample, meta_tokens, g_pre_mix):
    xT_hi, xT_lo = xT
    with ExitStack() as ctx:
        sb = lambda n, s, d=F32: ctx.enter_context(nc.sbuf_tensor(n, s, d))
        sem = lambda n: top.enter_context(nc.semaphore(n))
        x_in = sb("x_in", [P, 2, D])
        x_norm = sb("x_norm", [P, 2, D])
        squares = sb("squares", [P, D])
        sum_sq = sb("sum_sq", [P, TILES])
        std = sb("std", [P, TILES])
        mean_sq = sb("mean_sq", [P, TILES])
        rstd_0 = sb("rstd_0", [P, TILES])
        rstd = sb("rstd", [P, TILES])
        newton = sb("newton", [P, TILES])
        gain = sb("gain", [P, D])
        refined = sem("p1_refined")

        zeroed, const_ready = sem("p1_zeroed"), sem("p1_const_ready")
        gains_loaded = sem("p1_gains_loaded")
        x_loaded = [sem("p1_x_loaded0"), sem("p1_x_loaded1")]
        squared, std_ready, rstd_ready = sem("p1_squared"), sem("p1_std_ready"), sem("p1_rstd_ready")
        normed, transposed = sem("p1_normed"), sem("p1_transposed")
        hi_done, lo_done = sem("p1_hi_done"), sem("p1_lo_done")

        def x_loads(t):
            return 16 * (t // 2 + 1 + (t == SAMPLE_TILE))

        def toks(t):
            return slice(t * P, t * P + tile_tokens(t))

        with nc.Block() as block:

            @block.sync
            def _(sp):
                sp.dma_start(gain[:], g_pre_mix[0:1, :].to_broadcast([P, D])).then_inc(gains_loaded, 16)
                for t in range(TILES):
                    if t >= 2:
                        sp.wait_ge(normed, t - 1)
                    dst = x_in[:, t % 2, :]
                    if t < SAMPLE_TILE:
                        sp.dma_start(dst, x_prompt[0, t * P:(t + 1) * P, :]).then_inc(x_loaded[t % 2], 16)
                    else:
                        sp.dma_start(dst[0:N_SAMPLE], x_sample[0]).then_inc(x_loaded[t % 2], 16)
                        sp.dma_start(dst[N_SAMPLE:N_SAMPLE + N_META], meta_tokens).then_inc(x_loaded[t % 2], 16)

            @block.gpsimd
            def _(pool):
                pool.memset(c["ident"][:], 0.0).then_inc(zeroed, 1)
                pool.memset(c["fold"][:], 0.0).then_inc(zeroed, 1)
                pool.memset(c["eps"][:], EPS).then_inc(const_ready, 1)
                pool.wait_ge(zeroed, 2)
                pool.affine_select(out=c["ident"][:], in_=c["ident"][:], compare_op=ALU.not_equal, fill=1.0, base=0,
                                   pattern=[[-1, P]], channel_multiplier=1).then_inc(const_ready, 1)
                pool.affine_select(out=c["fold"][:], in_=c["fold"][:], compare_op=ALU.not_equal, fill=1.0, base=0,
                                   pattern=[[-1, HD]], channel_multiplier=1).then_inc(zeroed, 1)
                pool.wait_ge(zeroed, 3)
                pool.affine_select(out=c["fold"][:], in_=c["fold"][:], compare_op=ALU.not_equal, fill=1.0, base=-HD,
                                   pattern=[[-1, HD]], channel_multiplier=1).then_inc(const_ready, 1)

            @block.scalar
            def _(act):
                def split_hi(t):
                    for g in range(2):
                        act.wait_ge(transposed, 2 * t + g + 1)
                        n = tile_tokens(t)
                        src = ps[:, (2 * t + g) % 4, :].rearrange("p (k n) -> p k n", k=4)[:, :, 0:n]
                        act.activation(xT_hi[:, 4 * g:4 * g + 4, toks(t)], src, ACT.Copy).then_inc(hi_done, 1)

                act.wait_ge(const_ready, 1)
                for t in range(TILES):
                    n = tile_tokens(t)
                    act.wait_ge(x_loaded[t % 2], x_loads(t))
                    act.activation(squares[:n], x_in[:n, t % 2, :], ACT.Square,
                                   accum_out=sum_sq[:n, t:t + 1]).then_inc(squared, 1)
                    act.wait_ge(squared, t + 1)
                    act.activation(std[:n, t:t + 1], sum_sq[:n, t:t + 1], ACT.Sqrt, bias=c["eps"][:n, :],
                                   scale=1.0 / D).then_inc(std_ready, 1)
                    if t >= 1:
                        split_hi(t - 1)
                split_hi(TILES - 1)

            @block.vector
            def _(dve):
                for f in range(KT):
                    for half in range(2):
                        dve.memset(c["q_scale"][half * HD:(half + 1) * HD, f:f + 1], HD ** -0.5 / slope(2 * f + half))

                def split_lo(t):
                    for g in range(2):
                        dve.wait_ge(hi_done, 2 * t + g + 1)
                        n = tile_tokens(t)
                        src = ps[:, (2 * t + g) % 4, :].rearrange("p (k n) -> p k n", k=4)[:, :, 0:n]
                        dst = (slice(None), slice(4 * g, 4 * g + 4), toks(t))
                        dve.tensor_tensor(xT_lo[dst], src, xT_hi[dst].bitcast(F32), ALU.subtract).then_inc(lo_done, 1)

                for t in range(TILES):
                    n = tile_tokens(t)
                    dve.wait_ge(std_ready, t + 1)
                    dve.reciprocal(rstd_0[:n, t:t + 1], std[:n, t:t + 1]).then_inc(rstd_ready, 1)
                    dve.tensor_scalar(mean_sq[:n, t:t + 1], sum_sq[:n, t:t + 1], 1.0 / D, EPS, ALU.mult, ALU.add).then_inc(rstd_ready, 1)
                    dve.wait_ge(rstd_ready, 2 * t + 2)
                    refine_rstd(dve, refined, 3 * t, rstd[:n, t:t + 1], rstd_0[:n, t:t + 1], mean_sq[:n, t:t + 1],
                                newton[:n, t:t + 1])
                    if t == 0:
                        dve.wait_ge(gains_loaded, 16)
                    if t >= 2:
                        dve.wait_ge(transposed, 2 * t - 2)
                    dve.scalar_tensor_tensor(out=x_norm[:n, t % 2, :], in0=x_in[:n, t % 2, :], scalar=rstd[:n, t:t + 1],
                                             in1=gain[:n, :], op0=ALU.mult, op1=ALU.mult).then_inc(normed, 1)
                    if t >= 1:
                        split_lo(t - 1)
                split_lo(TILES - 1)

            @block.tensor
            def _(pe):
                pe.wait_ge(const_ready, 2)
                for t in range(TILES):
                    n = tile_tokens(t)
                    pe.wait_ge(normed, t + 1)
                    for g in range(2):
                        u = 2 * t + g
                        if u >= 4:
                            pe.wait_ge(lo_done, u - 3)
                        for k in range(4):
                            last = pe.transpose(ps[:, u % 4, k * P:k * P + n],
                                                x_norm[:n, t % 2, (4 * g + k) * P:(4 * g + k + 1) * P],
                                                c["ident"][:n, :n])
                        last.then_inc(transposed, 1)


TOKEN_MAJOR, GATE, FEATURE_MAJOR = "token-major", "gate", "feature-major"
CHUNKS = [(TOKEN_MAJOR, T_COLS)]
CHUNKS += [(FEATURE_MAJOR, [(QI, 512)])]
CHUNKS += [(FEATURE_MAJOR, [(QB + 512 * j, 512)]) for j in range(2)]
CHUNKS += [(FEATURE_MAJOR, [(QA + 512 * j, 512)]) for j in range(2)]
CHUNKS += [(GATE, [(GA + 512 * j, 512)]) for j in range(4)]
QT_ROW = {QA: 0, QA + 512: 512, QB: 1024, QB + 512: 1536, QI: 2048}
TOK_BLOCKS = [(0, 364), (364, 362), (726, 362)]
INDEX_TILES = [8, 7, 6, 5, 4, 3, 2]
INDEX_CHUNK = 2


def keys_seen(t):
    return P * (t + 1) if t < SAMPLE_TILE else PAST + N_SAMPLE


def groups_of(c):
    kind = CHUNKS[c][0]
    if kind == FEATURE_MAJOR:
        return [(f, t0, n) for f in range(4) for t0, n in TOK_BLOCKS]
    rows = tile_tokens if kind == TOKEN_MAJOR else tile_rows
    return [(None, t * P, rows(t)) for t in range(TILES)]


GROUP_BASE = [sum(len(groups_of(i)) for i in range(c)) for c in range(len(CHUNKS) + 1)]


def projection(nc, top, c, xT, ps, w_in, cache_ki_b, t_scr, q_scr, gate_scr, dist_scr):
    xT_hi, xT_lo = xT
    RAW, STAGE, BANKS = 4, 3, 4
    N_CH = len(CHUNKS)
    with ExitStack() as ctx:
        sb = lambda n, s, d=F32: ctx.enter_context(nc.sbuf_tensor(n, s, d))
        sem = lambda n: top.enter_context(nc.semaphore(n))
        w_raw = sb("w_raw", [P, RAW, 512])
        w_hi = sb("w_hi", [P, 2, KT, 512], F32R)
        w_lo = sb("w_lo", [P, 2, KT, 512], F32R)
        stage = sb("stage", [P, STAGE, 512])
        w_idx = sb("w_idx", [P, TILES, IDX_HEADS])
        kp = sb("kp", [P, 2, N_PROMPT], F32R)
        ks = sb("ks", [P, 2, N_QUERY], F32R)
        rel = sb("rel", [P, 2, N_QUERY])
        k_raw = rel[:].rearrange("p a b -> p (a b)").rearrange("p (j u d) -> p j u d", u=2, d=HD)
        q_raw = sb("q_raw", [P, IDX_HEADS, P])
        q_st = sb("q_st", [P, IDX_HEADS, P], F32R)
        score = sb("score", [P, 2, N_QUERY])
        top8 = sb("top8", [P, 8])
        dist = sb("dist", [P, N_PROMPT + P])
        masked = sb("masked", [P, 2, N_META + N_QUERY])
        ps_idx = ps[:, 5:8, :].rearrange("p b n -> p (b n)")

        w_loaded = [sem(f"p2_w_loaded{i}") for i in range(RAW)]
        w_hi_done, w_lo_done = sem("p2_w_hi_done"), sem("p2_w_lo_done")
        group_done, group_out = sem("p2_group_done"), sem("p2_group_out")
        wi_copied = sem("p2_wi_copied")
        stored = [sem(f"p2_stored{i}") for i in range(STAGE)]
        k_loaded, k_turned, k_hi_done, k_lo_done = (sem(f"p2_k_{n}") for n in ("loaded", "turned", "hi_done", "lo_done"))
        q_loaded, q_hi_done, q_lo_done = sem("p2_q_loaded"), sem("p2_q_hi_done"), sem("p2_q_lo_done")
        idx_done, rel_done, weighted, added = sem("p2_idx_done"), sem("p2_rel_done"), sem("p2_weighted"), sem("p2_added")
        dist_iota, dist_ready = sem("p2_dist_iota"), sem("p2_dist_ready")
        dve_step = sem("p2_dve_step")
        mask_ready = sem("p2_mask_ready")
        mask_stored = [sem("p2_mask_stored0"), sem("p2_mask_stored1")]

        def w_loads(n):
            first = sum(16 * len(T_COLS) for m in range(n % RAW, min(n + 1, KT), RAW))
            return first + sum(16 for m in range(n % RAW, n + 1, RAW) if m >= KT)

        def stores(u):
            return 16 * (u // STAGE + 1)

        def unit_cols(ch):
            return sum(n for _, n in CHUNKS[ch][1])

        K_GROUPS = [(0, 4, P, kp, 0), (4, 4, P, kp, 512), (8, 4, P, ks, 0), (12, 4, P, ks, 512), (16, 1, N_SAMPLE, ks, PAST)]

        with nc.Block() as block:

            @block.sync
            def _(sp):
                def store(ch, g):
                    kind, segs = CHUNKS[ch]
                    f, t0, n = groups_of(ch)[g]
                    u = GROUP_BASE[ch] + g
                    sp.wait_ge(group_out, u + 1)
                    src = stage[:, u % STAGE, :]
                    if kind == TOKEN_MAJOR:
                        sp.dma_start(t_scr[t0:t0 + n, :], src[:n, 0:T_WIDTH]).then_inc(stored[u % STAGE], 16)
                    elif kind == GATE:
                        col = segs[0][0] - GA
                        sp.dma_start(gate_scr[t0:t0 + n, col:col + 512], src[:n, :]).then_inc(stored[u % STAGE], 16)
                    else:
                        row = QT_ROW[segs[0][0]] + f * P
                        sp.dma_start(q_scr[row:row + P, t0:t0 + n], src[:, 0:n]).then_inc(stored[u % STAGE], 16)

                def all_stored(ch):
                    for u in range(GROUP_BASE[ch + 1] - STAGE, GROUP_BASE[ch + 1]):
                        sp.wait_ge(stored[u % STAGE], stores(u))

                def load_q(i):
                    t = INDEX_TILES[i]
                    r = tile_rows(t)
                    src = q_scr[2048:2560, t * P:t * P + r].rearrange("(h d) n -> d h n", d=HD)
                    for half in range(2):
                        sp.dma_start(q_raw[half * HD:(half + 1) * HD, :, 0:r], src).then_inc(q_loaded, 16)

                def store_mask(n, t):
                    sp.wait_ge(mask_ready, n + 1)
                    w = N_META + keys_seen(t)
                    sp.dma_start(dist_scr[t, 0:tile_rows(t), 0:w], masked[:tile_rows(t), n % 2, 0:w]).then_inc(mask_stored[n % 2], 16)

                store_mask(0, 0)
                store_mask(1, 1)
                mask_at = {4: [0], 6: [1], 7: [2], 8: [3], 9: [4, 5, 6]}
                for ch in range(N_CH):
                    for g in range(len(groups_of(ch))):
                        store(ch, g)
                        if INDEX_CHUNK <= ch < INDEX_CHUNK + len(INDEX_TILES) - 1 and g == 3:
                            i = ch - INDEX_CHUNK + 1
                            sp.wait_ge(q_lo_done, i)
                            load_q(i)
                    if ch == 0:
                        all_stored(0)
                        for half in range(2):
                            sp.dma_start(k_raw[:, 0:8, half, :],
                                         t_scr[0:N_PROMPT, T_KI:T_KI + HD].rearrange("(j p) d -> p j d", p=P)).then_inc(k_loaded, 16)
                            sp.dma_start(k_raw[:, 8:16, half, :],
                                         cache_ki_b[0, 0].rearrange("(j p) d -> p j d", p=P)).then_inc(k_loaded, 16)
                            sp.dma_start(k_raw[0:N_SAMPLE, 16, half, :],
                                         t_scr[N_PROMPT:N_QUERY, T_KI:T_KI + HD]).then_inc(k_loaded, 16)
                    if ch == 1:
                        all_stored(1)
                        load_q(0)
                    for i in mask_at.get(ch, []):
                        store_mask(i + 2, INDEX_TILES[i])
                all_stored(N_CH - 1)
                sp.wait_ge(mask_stored[0], 16 * 5)
                sp.wait_ge(mask_stored[1], 16 * 4)

            @block.scalar
            def _(act):
                def load_unit(n):
                    ch, k = divmod(n, KT)
                    if n >= RAW:
                        act.wait_ge(w_lo_done, n - RAW + 1)
                    col = 0
                    for c0, w in CHUNKS[ch][1]:
                        act.dma_start(w_raw[:, n % RAW, col:col + w], w_in[0, k * P:(k + 1) * P, c0:c0 + w])\
                           .then_inc(w_loaded[n % RAW], 16)
                        col += w

                def split_hi(n):
                    ch, k = divmod(n, KT)
                    w = unit_cols(ch)
                    act.wait_ge(w_loaded[n % RAW], w_loads(n))
                    if ch >= 2:
                        act.wait_ge(group_done, GROUP_BASE[ch - 1])
                    act.activation(w_hi[:, ch % 2, k, 0:w], w_raw[:, n % RAW, 0:w], ACT.Copy).then_inc(w_hi_done, 1)
                    if n + RAW - 1 < N_CH * KT and n >= 1:
                        load_unit(n + RAW - 1)

                def evacuate(ch, g):
                    kind, segs = CHUNKS[ch]
                    f, t0, n = groups_of(ch)[g]
                    u = GROUP_BASE[ch] + g
                    act.wait_ge(group_done, u + 1)
                    if u >= STAGE:
                        act.wait_ge(stored[u % STAGE], stores(u - STAGE))
                    dst = stage[:, u % STAGE, :]
                    bank = ps[:, u % BANKS, :]
                    if kind == TOKEN_MAJOR:
                        t = t0 // P
                        act.activation(w_idx[:n, t, :], bank[:n, T_WI:T_WI + IDX_HEADS], ACT.Copy, scale=INDEX_SCALE)\
                           .then_inc(wi_copied, 1)
                        act.activation(dst[:n, 0:T_WIDTH], bank[:n, 0:T_WIDTH], ACT.Copy).then_inc(group_out, 1)
                    elif kind == GATE:
                        act.activation(dst[:n, :], bank[:n, :], ACT.Sigmoid).then_inc(group_out, 1)
                    elif segs[0][0] == QI:
                        act.activation(dst[:, 0:n], bank[:, 0:n], ACT.Copy).then_inc(group_out, 1)
                    else:
                        pair = (QT_ROW[segs[0][0]] % D) // P + f
                        act.activation(dst[:, 0:n], bank[:, 0:n], ACT.Copy,
                                       scale=c["q_scale"][:, pair:pair + 1]).then_inc(group_out, 1)

                def keys_hi(j):
                    _, tiles, n, dst, col = K_GROUPS[j]
                    act.wait_ge(k_turned, j + 1)
                    act.activation(dst[:, 0, col:col + tiles * n], ps[:, 4, 0:tiles * n], ACT.Copy).then_inc(k_hi_done, 1)

                def queries_hi(i):
                    r = tile_rows(INDEX_TILES[i])
                    act.wait_ge(q_loaded, 32 * (i + 1))
                    if i >= 1:
                        act.wait_ge(idx_done, IDX_HEADS * i)
                    act.activation(q_st[:, :, 0:r], q_raw[:, :, 0:r], ACT.Copy).then_inc(q_hi_done, 1)

                def relu(i, h):
                    n, r = keys_seen(INDEX_TILES[i]), tile_rows(INDEX_TILES[i])
                    v = IDX_HEADS * i + h
                    act.wait_ge(idx_done, v + 1)
                    if v >= 2:
                        act.wait_ge(added, v - 1)
                    act.activation(rel[:r, v % 2, 0:n], ps_idx[:r, 0:n], ACT.Relu).then_inc(rel_done, 1)
                    act.wait_ge(wi_copied, TILES)
                    act.wait_ge(rel_done, v + 1)
                    act.activation(rel[:r, v % 2, 0:n], rel[:r, v % 2, 0:n], ACT.Copy,
                                   scale=w_idx[:r, INDEX_TILES[i], h:h + 1]).then_inc(weighted, 1)

                for n in range(RAW):
                    load_unit(n)
                for n in range(KT):
                    split_hi(n)
                for ch in range(N_CH):
                    i = ch - INDEX_CHUNK
                    if 0 <= i < len(INDEX_TILES):
                        queries_hi(i)
                    for g in range(len(groups_of(ch))):
                        evacuate(ch, g)
                        if g < KT and ch + 1 < N_CH:
                            split_hi((ch + 1) * KT + g)
                        if ch == 1 and 1 <= g <= len(K_GROUPS):
                            keys_hi(g - 1)
                        if 0 <= i < len(INDEX_TILES) and 1 <= g <= IDX_HEADS:
                            relu(i, g - 1)

            @block.gpsimd
            def _(pool):
                def split_lo(n):
                    ch, k = divmod(n, KT)
                    w = unit_cols(ch)
                    pool.wait_ge(w_hi_done, n + 1)
                    i = ch - 1 - INDEX_CHUNK
                    if 0 <= i < len(INDEX_TILES):
                        pool.wait_ge(added, IDX_HEADS * i + max(k - 1, 0))
                        pool.wait_ge(q_lo_done, i + 1)
                    pool.tensor_tensor(w_lo[:, ch % 2, k, 0:w], w_raw[:, n % RAW, 0:w], w_hi[:, ch % 2, k, 0:w].bitcast(F32),
                                       ALU.subtract).then_inc(w_lo_done, 1)

                def queries_lo(i):
                    r = tile_rows(INDEX_TILES[i])
                    pool.wait_ge(q_hi_done, i + 1)
                    pool.wait_ge(w_lo_done, KT * (i + INDEX_CHUNK + 1))
                    pool.wait_ge(added, IDX_HEADS * i)
                    pool.tensor_tensor(q_st[HD:, :, 0:r], q_raw[HD:, :, 0:r], q_st[HD:, :, 0:r].bitcast(F32),
                                       ALU.subtract).then_inc(q_lo_done, 1)

                def add_head(i, h):
                    t = INDEX_TILES[i]
                    n, r = keys_seen(t), tile_rows(t)
                    v = IDX_HEADS * i + h
                    pool.wait_ge(weighted, v + 1)
                    pool.wait_ge(w_lo_done, KT * (i + INDEX_CHUNK + 1) + min(h + 2, KT))
                    pool.wait_ge(q_lo_done, i + 1)
                    out = score[:r, i % 2, 0:n]
                    if h == 0:
                        if i >= 2:
                            pool.wait_ge(mask_ready, i + 1)
                        pool.tensor_copy(out, rel[:r, v % 2, 0:n]).then_inc(added, 1)
                    else:
                        pool.wait_ge(added, v)
                        pool.tensor_tensor(out, out, rel[:r, v % 2, 0:n], ALU.add).then_inc(added, 1)

                pool.iota(dist[:], pattern=[[-1, N_PROMPT + P]], base=N_PROMPT, channel_multiplier=1,
                          allow_small_or_imprecise_dtypes=True).then_inc(dist_iota, 1)
                for n in range(KT):
                    split_lo(n)
                for ch in range(N_CH):
                    i = ch - INDEX_CHUNK
                    if 0 <= i < len(INDEX_TILES):
                        queries_lo(i)
                    for g in range(IDX_HEADS + 1):
                        if g < KT and ch + 1 < N_CH:
                            split_lo((ch + 1) * KT + g)
                        if 0 <= i < len(INDEX_TILES) and 1 <= g:
                            add_head(i, g - 1)

            @block.vector
            def _(dve):
                dve.wait_ge(dist_iota, 1)
                dve.scalar_tensor_tensor(out=dist[:], in0=dist[:], scalar=-1.0, in1=dist[:], op0=ALU.mult,
                                         op1=ALU.max).then_inc(dist_ready, 1)
                dve.memset(masked[:, :, 0:N_META], 0.0).then_inc(dist_ready, 1)
                dve.wait_ge(dist_ready, 2)
                for t in range(2):
                    n = keys_seen(t)
                    dve.tensor_copy(masked[:, t, N_META:N_META + n], dist[:, N_PROMPT - t * P:N_PROMPT - t * P + n]).then_inc(dve_step, 1)
                    dve.wait_ge(dve_step, t + 1)
                    dve.memset(masked[0:CHUNK, t, N_META + n - CHUNK:N_META + n], FAR).then_inc(mask_ready, 1)
                for j, (_, tiles, n, dst, col) in enumerate(K_GROUPS):
                    dve.wait_ge(k_hi_done, j + 1)
                    dve.tensor_tensor(dst[:, 1, col:col + tiles * n], ps[:, 4, 0:tiles * n],
                                      dst[:, 0, col:col + tiles * n].bitcast(F32), ALU.subtract).then_inc(k_lo_done, 1)
                steps = 2
                for i, t in enumerate(INDEX_TILES):
                    n, r = keys_seen(t), tile_rows(t)
                    work = score[:r, i % 2, 0:n]
                    dve.wait_ge(added, IDX_HEADS * (i + 1))
                    if t < SAMPLE_TILE:
                        dve.memset(score[0:CHUNK, i % 2, n - CHUNK:n], UNSEEN).then_inc(dve_step, 1)
                        steps += 1
                        dve.wait_ge(dve_step, steps)
                    for _ in range(TOPK // 8):
                        dve.max(top8[:r], work).then_inc(dve_step, 1)
                        dve.wait_ge(dve_step, steps + 1)
                        dve.match_replace(work, top8[:r], work, TAKEN).then_inc(dve_step, 1)
                        dve.wait_ge(dve_step, steps + 2)
                        steps += 2
                    dve.tensor_scalar(work, work, TAKEN, FAR, ALU.not_equal, ALU.mult).then_inc(dve_step, 1)
                    steps += 1
                    dve.wait_ge(dve_step, steps)
                    dve.wait_ge(mask_stored[i % 2], 16 * (i // 2 + 1))
                    c0 = N_PROMPT - t * P
                    dve.tensor_tensor(masked[:r, i % 2, N_META:N_META + n], work, dist[:r, c0:c0 + n], ALU.max).then_inc(mask_ready, 1)

            @block.tensor
            def _(pe):
                def group(ch, g):
                    kind = CHUNKS[ch][0]
                    f, t0, n = groups_of(ch)[g]
                    u = GROUP_BASE[ch] + g
                    if u >= BANKS:
                        pe.wait_ge(group_out, u - BANKS + 1)
                    for k in range(KT):
                        x_hi, x_lo = xT_hi[:, k, t0:t0 + n], xT_lo[:, k, t0:t0 + n]
                        if kind == FEATURE_MAJOR:
                            wh, wl = w_hi[:, ch % 2, k, f * P:(f + 1) * P], w_lo[:, ch % 2, k, f * P:(f + 1) * P]
                            out, terms = ps[:, u % BANKS, 0:n], ((wh, x_hi), (wh, x_lo), (wl, x_hi))
                        else:
                            w = unit_cols(ch)
                            wh, wl = w_hi[:, ch % 2, k, 0:w], w_lo[:, ch % 2, k, 0:w]
                            out, terms = ps[:n, u % BANKS, 0:w], ((x_hi, wh), (x_hi, wl), (x_lo, wh))
                        for j, (a, b) in enumerate(terms):
                            last = pe.matmul(out, a, b, start=(k == 0 and j == 0), stop=(k == KT - 1 and j == 2))
                    last.then_inc(group_done, 1)

                def turn_keys(j):
                    first, tiles, n, _, _ = K_GROUPS[j]
                    if j == 0:
                        pe.wait_ge(k_loaded, 16 * 6)
                    if j >= 1:
                        pe.wait_ge(k_lo_done, j)
                    for a in range(tiles):
                        last = pe.transpose(ps[:, 4, a * n:(a + 1) * n],
                                            k_raw[:n, first + a, :, :].rearrange("p u d -> p (u d)"), c["ident"][:n, :n])
                    last.then_inc(k_turned, 1)

                def index_scores(i, h):
                    t = INDEX_TILES[i]
                    n, r = keys_seen(t), tile_rows(t)
                    v = IDX_HEADS * i + h
                    if h == 0:
                        pe.wait_ge(q_lo_done, i + 1)
                    if i == 0 and h == 0:
                        pe.wait_ge(k_lo_done, len(K_GROUPS))
                    if v >= 1:
                        pe.wait_ge(rel_done, v)
                    keys = kp if t < SAMPLE_TILE else ks
                    for n0 in range(0, n, 512):
                        n1 = min(n, n0 + 512)
                        for part in range(2):
                            last = pe.matmul(ps_idx[:r, n0:n1], q_st[:, h, 0:r], keys[:, part, n0:n1],
                                             start=(part == 0), stop=(part == 1))
                    last.then_inc(idx_done, 1)

                for ch in range(N_CH):
                    pe.wait_ge(w_lo_done, KT * (ch + 1))
                    i = ch - INDEX_CHUNK
                    for g in range(len(groups_of(ch))):
                        group(ch, g)
                        if ch == 1 and 1 <= g <= len(K_GROUPS):
                            turn_keys(g - 1)
                        if 0 <= i < len(INDEX_TILES) and 1 <= g <= IDX_HEADS:
                            index_scores(i, g - 1)


def band_width(t):
    return P if t == 0 else (2 * P if t < SAMPLE_TILE else WINDOW + N_SAMPLE)


def key_columns(branch, t):
    return N_META + (band_width(t) if branch == 0 else keys_seen(t))


def key_tiles(branch, t):
    w = key_columns(branch, t)
    tiles = [(0, N_META, 0)]
    if branch == 0 and t == SAMPLE_TILE:
        return tiles + [(N_META, P, 1), (w - P, P, 2)]
    if branch == 0:
        return tiles + [(N_META + P * j, P, t + j + 1 - (t > 0)) for j in range(band_width(t) // P)]
    if t == SAMPLE_TILE:
        return tiles + [(N_META + P * j, P, j + 1) for j in range(8)] + [(w - P, P, 9)]
    return tiles + [(N_META + P * j, P, j + 1) for j in range(t + 1)]


KV_COPIES = 13


def attention_operands(nc, top, c, ps, kv, t_scr, caches, attn_sinks):
    cache_k_a, cache_v_a, cache_k_b, cache_v_b, cache_meta = caches
    with ExitStack() as ctx:
        sb = lambda n, s, d=F32: ctx.enter_context(nc.sbuf_tensor(n, s, d))
        sem = lambda n: top.enter_context(nc.semaphore(n))
        prompt = slice(0, N_PROMPT)
        new = slice(N_PROMPT, N_QUERY)
        meta = slice(N_QUERY, N_TOK)
        tiled = lambda a: a.rearrange("(j p) d -> p j d", p=P)
        T_KV = T_KI
        raw_p = sb("raw_p", [P, 8, T_KV])
        raw_m = sb("raw_m", [N_META, T_KV])
        raw_cm = sb("raw_cm", [N_META, T_KV])
        raw_n = sb("raw_n", [P, T_KV])
        raw_ca = sb("raw_ca", [P, 2, 2 * HD])
        raw_cb = sb("raw_cb", [P, 2, 8, HD])
        k_twice = sb("k_twice", [P, 43, 2, HD])
        SETS = []

        def add_set(k, v, tiles, k_col, v_col, cached=None):
            cols = (slice(k_col, k_col + HD), slice(v_col, v_col + HD))
            if cached is None:
                SETS.append((k, v, tiles, None, [(raw_m[:, q], raw_p[:, :, q], None) for q in cols]))
            else:
                SETS.append((k, v, tiles, N_SAMPLE, [(raw_cm[:, q], cached[i], raw_n[:, q]) for i, q in enumerate(cols)]))

        for g in range(2):
            add_set(kv["k_a_p"][:, g], kv["v_a_p"][:, g], 8, T_KA + HD * g, T_VA + HD * g)
        add_set(kv["k_b_p"][:], kv["v_b_p"][:], 8, T_KB, T_VB)
        for g in range(2):
            add_set(kv["k_a_s"][:, g], kv["v_a_s"][:, g], 1, T_KA + HD * g, T_VA + HD * g,
                    [raw_ca[:, i:i + 1, HD * g:HD * (g + 1)] for i in range(2)])
        add_set(kv["k_b_s"][:], kv["v_b_s"][:], 8, T_KB, T_VB, [raw_cb[:, i] for i in range(2)])
        GROUPS = []
        for s, (_, _, m, last, _) in enumerate(SETS):
            GROUPS.append((s, 0, 1, N_META, 0))
            for j in range(0, m, 4):
                GROUPS.append((s, 1 + j, min(4, m - j), P, N_META + P * j))
            if last:
                GROUPS.append((s, 1 + m, 1, last, N_META + P * m))
        SLOT_BASE = [sum(g[2] for g in GROUPS[:j]) for j in range(len(GROUPS))]
        keys_doubled = sem("p3_keys_doubled")
        prompt_loaded, sample_loaded = sem("p3_prompt_loaded"), sem("p3_sample_loaded")
        PROMPT_LOADS, SAMPLE_LOADS = 3, 7
        k_turned, k_hi_done, k_lo_done = sem("p3_k_turned"), sem("p3_k_hi_done"), sem("p3_k_lo_done")
        v_zeroed, v_hi_done = sem("p3_v_zeroed"), sem("p3_v_hi_done")
        sinks_loaded, dist_iota, dist_step = sem("p3_sinks_loaded"), sem("p3_dist_iota"), sem("p3_dist_step")

        def value_parts(s):
            _, _, m, last, (_, (v_meta, v_tiles, v_new)) = SETS[s]
            parts = [(slice(0, N_META), 0, 1, v_meta.unsqueeze(1)), (slice(0, P), 1, m, v_tiles)]
            if last:
                parts.append((slice(HD, P), 1 + m, 1, v_new[HD:P].unsqueeze(1)))
            return parts

        with nc.Block() as block:

            def set_loaded(eng, s):
                eng.wait_ge(prompt_loaded, 16 * PROMPT_LOADS)
                if SETS[s][3]:
                    eng.wait_ge(sample_loaded, 16 * SAMPLE_LOADS)

            @block.sync
            def _(sp):
                for j in range(0, 8, 4):
                    sp.dma_start(raw_p[:, j:j + 4, :], t_scr[P * j:P * (j + 4), 0:T_KV].rearrange("(j p) d -> p j d", p=P))\
                      .then_inc(prompt_loaded, 16)
                sp.dma_start(raw_m[:], t_scr[meta, 0:T_KV]).then_inc(prompt_loaded, 16)
                sp.dma_start(raw_n[0:HD], t_scr[new, 0:T_KV]).then_inc(sample_loaded, 16)
                sp.dma_start(raw_n[HD:P], t_scr[new, 0:T_KV]).then_inc(sample_loaded, 16)
                sp.dma_start(kv["sinks"][:], attn_sinks[0:1, :].to_broadcast([P, HEADS])).then_inc(sinks_loaded, 16)

            @block.gpsimd
            def _(pool):
                pool.iota(kv["dist_a"][:, N_META:], pattern=[[-1, 2 * P]], base=P, channel_multiplier=1,
                          allow_small_or_imprecise_dtypes=True).then_inc(dist_iota, 1)
                for j, (s, first, n, rows, col) in enumerate(GROUPS):
                    if first == 0:
                        set_loaded(pool, s)
                    k_meta, k_tiles, k_new = SETS[s][4][0]
                    if first == 0:
                        src = k_meta.unsqueeze(1)
                    elif first <= SETS[s][2]:
                        src = k_tiles[:, first - 1:first - 1 + n]
                    else:
                        src = k_new[0:rows].unsqueeze(1)
                    pool.tensor_copy(k_twice[0:rows, SLOT_BASE[j]:SLOT_BASE[j] + n],
                                     src.unsqueeze(2).to_broadcast([rows, n, 2, HD])).then_inc(keys_doubled, 1)

            @block.scalar
            def _(act):
                act.dma_start(raw_cm[:], cache_meta[0, 0].rearrange("m s d -> m (s d)")).then_inc(sample_loaded, 16)
                for i, cache in enumerate((cache_k_a, cache_v_a)):
                    act.dma_start(raw_ca[:, i, :], cache[0, 0].rearrange("n h d -> n (h d)")).then_inc(sample_loaded, 16)
                for i, cache in enumerate((cache_k_b, cache_v_b)):
                    act.dma_start(raw_cb[:, i], cache[0, 0, :, 0, :].rearrange("(j p) d -> p j d", p=P)).then_inc(sample_loaded, 16)
                for j, (s, first, n, rows, col) in enumerate(GROUPS):
                    act.wait_ge(k_turned, j + 1)
                    act.activation(SETS[s][0][:, 0, col:col + n * rows], ps[:, j % 8, 0:n * rows], ACT.Copy).then_inc(k_hi_done, 1)
                for s in range(len(SETS)):
                    set_loaded(act, s)
                    for rows, slot, n, src in value_parts(s):
                        act.activation(SETS[s][1][rows, slot:slot + n, 0:HD], src, ACT.Copy).then_inc(v_hi_done, 1)

            @block.vector
            def _(dve):
                for s in range(len(SETS)):
                    if SETS[s][3]:
                        dve.memset(SETS[s][1][0:HD, 1 + SETS[s][2], :].bitcast(F32), 0.0)
                da, da0, sinks = kv["dist_a"], kv["dist_a0"], kv["sinks"]
                dve.wait_ge(dist_iota, 1)
                dve.scalar_tensor_tensor(out=da[:, N_META:], in0=da[:, N_META:], scalar=-1.0, in1=da[:, N_META:],
                                         op0=ALU.mult, op1=ALU.max).then_inc(dist_step, 1)
                dve.memset(da[:, 0:N_META], 0.0).then_inc(dist_step, 1)
                dve.memset(da0[:, 0:N_META], 0.0).then_inc(dist_step, 1)
                dve.wait_ge(dist_step, 3)
                dve.memset(da[0:CHUNK, N_META + 3 * CHUNK:N_META + 4 * CHUNK], FAR).then_inc(dist_step, 1)
                dve.memset(da[CHUNK:P, N_META:N_META + CHUNK], FAR).then_inc(dist_step, 1)
                dve.wait_ge(dist_step, 5)
                dve.tensor_copy(da0[:, N_META:], da[:, N_META + P:])
                dve.wait_ge(sinks_loaded, 16)
                for h in range(HEADS):
                    dve.tensor_scalar(kv["sinks_scaled"][:, h:h + 1], sinks[:, h:h + 1], 1.0 / slope(h), None, ALU.mult)
                for j, (s, first, n, rows, col) in enumerate(GROUPS):
                    dve.wait_ge(k_hi_done, j + 1)
                    dve.tensor_tensor(SETS[s][0][:, 1, col:col + n * rows], ps[:, j % 8, 0:n * rows],
                                      SETS[s][0][:, 0, col:col + n * rows].bitcast(F32), ALU.subtract).then_inc(k_lo_done, 1)
                done = 0
                for s in range(len(SETS)):
                    for rows, slot, n, src in value_parts(s):
                        done += 1
                        dve.wait_ge(v_hi_done, done)
                        dve.tensor_tensor(SETS[s][1][rows, slot:slot + n, HD:P], src,
                                          SETS[s][1][rows, slot:slot + n, 0:HD].bitcast(F32), ALU.subtract)

            @block.tensor
            def _(pe):
                for j, (s, first, n, rows, col) in enumerate(GROUPS):
                    pe.wait_ge(keys_doubled, j + 1)
                    if j >= 8:
                        pe.wait_ge(k_lo_done, j - 7)
                    for a in range(n):
                        last = pe.transpose(ps[:, j % 8, a * rows:(a + 1) * rows],
                                            k_twice[0:rows, SLOT_BASE[j] + a].rearrange("p t d -> p (t d)"),
                                            c["ident"][0:rows, 0:rows])
                    last.then_inc(k_turned, 1)


def attention(nc, top, c, ps, kv, q_scr, gate_scr, dist_scr, merged_scr, t_scr, caches, outs):
    with ExitStack() as ctx:
        sb = lambda n, s, d=F32: ctx.enter_context(nc.sbuf_tensor(n, s, d))
        sem = lambda n: top.enter_context(nc.semaphore(n))
        SECTIONS = [(t, branch) for t in range(TILES) for branch in range(2)]
        UNITS = len(SECTIONS) * HEADS
        MAX_W = N_META + N_QUERY
        q_raw = sb("q_raw3", [P, HEADS, P])
        q_st = sb("q_st3", [P, 2, HEADS, P], F32R)
        probs = sb("probs", [P, 3, MAX_W])
        pt_hi = sb("pt_hi", [P, 2, 10, 2, P], F32R)
        pt_lo = sb("pt_lo", [P, 2, 10, 2, P], F32R)
        dist_b = sb("dist_b", [P, 2, MAX_W])
        top_neg = sb("top_neg", [P, 2, HEADS])
        top_val = sb("top_val", [P, 2, 3])
        top_all = sb("top_all", [P, 3])
        sums = sb("sums", [P, 2, HEADS])
        sink_e = sb("sink_e", [P, 2, HEADS])
        inv = sb("inv", [P, 2, HEADS])
        out_t = sb("out_t", [P, 2, 2 * P])
        mixed = sb("mixed", [P, 2, D])
        gates = sb("gates", [P, 2 * D])
        merged = sb("merged", [P, D])
        T_BANK, PV_BANK, O_BANK = 3, 6, 7

        q_loaded, q_hi_done, q_lo_done = sem("p3_q_loaded"), sem("p3_q_hi_done"), sem("p3_q_lo_done")
        dist_loaded = [sem("p3_dist_loaded0"), sem("p3_dist_loaded1")]
        gates_loaded = sem("p3_gates_loaded")
        scored, topped, neg_ready, exped = sem("p3_scored"), sem("p3_topped"), sem("p3_neg_ready"), sem("p3_exped")
        turned, hi_done, lo_done = sem("p3_turned"), sem("p3_hi_done"), sem("p3_lo_done")
        valued, out_copied, folded = sem("p3_valued"), sem("p3_out_copied"), sem("p3_folded")
        sink_in, sink_done, sum_ready, inv_ready = sem("p3_sink_in"), sem("p3_sink_done"), sem("p3_sum_ready"), sem("p3_inv_ready")
        normed = sem("p3_normed")
        merge_step, merged_stored = sem("p3_merge_step"), sem("p3_merged_stored")

        def section(u):
            return SECTIONS[u // HEADS]

        def tiles_of(u):
            t, branch = section(u)
            return key_tiles(branch, t)

        def groups(u):
            n = len(tiles_of(u))
            return [(a, min(4, n - a)) for a in range(0, n, 4)]

        GROUPS = [0]
        for u in range(UNITS):
            GROUPS.append(GROUPS[-1] + len(groups(u)))

        def score_chunks(u):
            t, branch = section(u)
            w = key_columns(branch, t)
            n = -(-w // 512)
            size = -(-w // (2 * n)) * 2
            return [(i, min(w, i + size)) for i in range(0, w, size)]

        CHUNK_BASE = [0]
        for u in range(UNITS):
            CHUNK_BASE.append(CHUNK_BASE[-1] + len(score_chunks(u)))

        def keys(t, branch, h):
            if branch == 1:
                k = kv["k_b_p"] if t < SAMPLE_TILE else kv["k_b_s"]
                return [(k[:], 0, 0, key_columns(1, t))]
            g = h // 8
            if t == SAMPLE_TILE:
                return [(kv["k_a_s"][:, g], 0, 0, key_columns(0, t))]
            band0 = N_META + P * max(t - 1, 0)
            return [(kv["k_a_p"][:, g], 0, 0, N_META), (kv["k_a_p"][:, g], band0, N_META, band_width(t))]

        def values(t, branch, h):
            if branch == 1:
                return kv["v_b_p"][:] if t < SAMPLE_TILE else kv["v_b_s"][:]
            return (kv["v_a_p"] if t < SAMPLE_TILE else kv["v_a_s"])[:, h // 8]

        with nc.Block() as block:

            @block.sync
            def _(sp):
                def load_q(s):
                    t, branch = SECTIONS[s]
                    r = tile_rows(t)
                    if s >= 1:
                        sp.wait_ge(q_lo_done, s)
                    src = q_scr[branch * D:(branch + 1) * D, t * P:t * P + r].rearrange("(h d) n -> d h n", d=HD)
                    for half in range(2):
                        sp.dma_start(q_raw[half * HD:(half + 1) * HD, :, 0:r], src).then_inc(q_loaded, 16)

                def load_dist(t):
                    if t >= 2:
                        sp.wait_ge(topped, CHUNK_BASE[HEADS * 2 * (t - 1)])
                    r, w = tile_rows(t), key_columns(1, t)
                    sp.dma_start(dist_b[:r, t % 2, 0:w], dist_scr[t, 0:r, 0:w]).then_inc(dist_loaded[t % 2], 16)

                def load_gates(t):
                    r = tile_rows(t)
                    sp.dma_start(gates[:r, :], gate_scr[t * P:t * P + r, :]).then_inc(gates_loaded, 16)

                def store_merged(t):
                    r = tile_rows(t)
                    sp.wait_ge(merge_step, 3 * (t + 1))
                    sp.dma_start(merged_scr[t * P:t * P + r, :], merged[:r, :]).then_inc(merged_stored, 16)

                load_q(0)
                load_dist(0)
                load_gates(0)
                copy = lambda dst, src: sp.dma_start(dst, src).then_inc(kv["stored"], 16)
                tail = slice(N_PROMPT - WINDOW, N_PROMPT)
                flat = lambda a: a[0, 0].rearrange("n h d -> n (h d)")
                copy(flat(outs["k_a_prompt"]), t_scr[tail, T_KA:T_KA + 2 * HD])
                copy(flat(outs["v_a_prompt"]), t_scr[tail, T_VA:T_VA + 2 * HD])
                copy(flat(outs["k_b_prompt"]), t_scr[0:N_PROMPT, T_KB:T_KB + HD])
                copy(flat(outs["v_b_prompt"]), t_scr[0:N_PROMPT, T_VB:T_VB + HD])
                copy(outs["ki_b_prompt"][0, 0], t_scr[0:N_PROMPT, T_KI:T_KI + HD])
                copy(flat(outs["meta_prompt"]), t_scr[N_QUERY:N_TOK, 0:T_KI])
                copy(outs["k_a_sample"][0, 0, 0:WINDOW - N_SAMPLE], caches[0][0, 0, N_SAMPLE:WINDOW])
                copy(outs["v_a_sample"][0, 0, 0:WINDOW - N_SAMPLE], caches[1][0, 0, N_SAMPLE:WINDOW])
                copy(flat(outs["k_a_sample"])[WINDOW - N_SAMPLE:], t_scr[N_PROMPT:N_QUERY, T_KA:T_KA + 2 * HD])
                copy(flat(outs["v_a_sample"])[WINDOW - N_SAMPLE:], t_scr[N_PROMPT:N_QUERY, T_VA:T_VA + 2 * HD])
                copy(flat(outs["k_b_sample"]), t_scr[N_PROMPT:N_QUERY, T_KB:T_KB + HD])
                copy(flat(outs["v_b_sample"]), t_scr[N_PROMPT:N_QUERY, T_VB:T_VB + HD])
                copy(outs["ki_b_sample"][0, 0], t_scr[N_PROMPT:N_QUERY, T_KI:T_KI + HD])
                for s, (t, branch) in enumerate(SECTIONS):
                    if s + 1 < len(SECTIONS):
                        load_q(s + 1)
                    if branch == 0:
                        if t >= 1:
                            store_merged(t - 1)
                            load_gates(t)
                        if t + 1 < TILES:
                            load_dist(t + 1)
                store_merged(TILES - 1)
                sp.wait_ge(merged_stored, 16 * TILES)
                sp.wait_ge(kv["stored"], 16 * KV_COPIES)

            @block.gpsimd
            def _(pool):
                def queries_lo(s):
                    t, branch = SECTIONS[s]
                    r = tile_rows(t)
                    pool.wait_ge(q_hi_done, s + 1)
                    st = q_st[HD:, branch, :, 0:r]
                    pool.tensor_tensor(st, q_raw[HD:, :, 0:r], st.bitcast(F32), ALU.subtract).then_inc(q_lo_done, 1)
                    pool.wait_ge(q_lo_done, s + 1)

                def merge(t):
                    r = tile_rows(t)
                    pool.wait_ge(normed, 4 * (t + 1))
                    pool.wait_ge(gates_loaded, 16 * (t + 1))
                    if t >= 1:
                        pool.wait_ge(merged_stored, 16 * t)
                    pool.tensor_tensor(merged[:r, :], mixed[:r, 0, :], gates[:r, 0:D], ALU.mult).then_inc(merge_step, 1)
                    pool.wait_ge(merge_step, 3 * t + 1)
                    pool.tensor_tensor(mixed[:r, 1, :], mixed[:r, 1, :], gates[:r, D:], ALU.mult).then_inc(merge_step, 1)
                    pool.wait_ge(merge_step, 3 * t + 2)
                    pool.tensor_tensor(merged[:r, :], merged[:r, :], mixed[:r, 1, :], ALU.add).then_inc(merge_step, 1)
                    pool.wait_ge(merge_step, 3 * t + 3)

                queries_lo(0)
                for s, (t, branch) in enumerate(SECTIONS):
                    if s + 1 < len(SECTIONS):
                        queries_lo(s + 1)
                    if branch == 0 and t >= 1:
                        merge(t - 1)
                merge(TILES - 1)

            @block.scalar
            def _(act):
                def queries_hi(s):
                    t, branch = SECTIONS[s]
                    r = tile_rows(t)
                    act.wait_ge(q_loaded, 32 * (s + 1))
                    if s >= 2:
                        act.wait_ge(scored, CHUNK_BASE[HEADS * (s - 1)])
                    act.activation(q_st[:, branch, :, 0:r], q_raw[:, :, 0:r], ACT.Copy).then_inc(q_hi_done, 1)

                def split_hi(u):
                    t, branch = section(u)
                    r = tile_rows(t)
                    if u % 2 == 0 and u >= 4:
                        act.wait_ge(valued, u // 2 - 1)
                    for j, (a, n) in enumerate(groups(u)):
                        x = GROUPS[u] + j
                        act.wait_ge(turned, x + 1)
                        src = ps[:, T_BANK + x % 3, :].rearrange("p (k n) -> p k n", k=4)[:, 0:n, 0:r]
                        act.activation(pt_hi[:, (u // 2) % 2, a:a + n, u % 2, 0:r], src, ACT.Copy).then_inc(hi_done, 1)

                def exp(u):
                    t, branch = section(u)
                    r, w, h = tile_rows(t), key_columns(branch, t), u % HEADS
                    act.wait_ge(neg_ready, u + 1)
                    act.activation(probs[:r, u % 3, 0:w], probs[:r, u % 3, 0:w], ACT.Exp, bias=top_neg[:r, branch, h:h + 1],
                                   scale=slope(h), accum_out=sums[:r, branch, h:h + 1]).then_inc(exped, 1)

                def copy_out(p):
                    r = tile_rows(section(2 * p)[0])
                    act.wait_ge(valued, p + 1)
                    if p >= 2:
                        act.wait_ge(folded, p - 1)
                    act.activation(out_t[:, p % 2, 0:2 * r], ps[:, PV_BANK, 0:2 * r], ACT.Copy).then_inc(out_copied, 1)

                def sink_exp(half, done):
                    t, _ = section(8 * half)
                    r, hs = tile_rows(t), slice(8 * (half % 2), 8 * (half % 2) + 8)
                    act.wait_ge(sink_in, done + 1)
                    act.activation(sink_e[:r, 0, hs], sink_e[:r, 0, hs], ACT.Exp).then_inc(sink_done, 1)

                sinks = 0
                queries_hi(0)
                for u in range(UNITS + 6):
                    if u >= 2 and u - 2 < UNITS:
                        split_hi(u - 2)
                    if u < UNITS:
                        exp(u)
                    if u >= 4 and u % 2 == 0 and (u - 4) // 2 < UNITS // 2:
                        copy_out((u - 4) // 2)
                    if u % HEADS == 2 and u // HEADS + 1 < len(SECTIONS):
                        queries_hi(u // HEADS + 1)
                    if u >= 8 and u % 8 == 0 and u <= UNITS and section(u - 8)[1] == 0:
                        sink_exp(u // 8 - 1, sinks)
                        sinks += 1

            @block.vector
            def _(dve):
                def subtract_distance(u):
                    t, branch = section(u)
                    r, w, h = tile_rows(t), key_columns(branch, t), u % HEADS
                    if branch == 1 and h == 0:
                        dve.wait_ge(dist_loaded[t % 2], 16 * (t // 2 + 1))
                    if u >= 3:
                        dve.wait_ge(turned, GROUPS[u - 2])
                    if branch == 1:
                        dist, start = dist_b[:r, t % 2, :], UNSEEN
                    else:
                        dist = (kv["dist_a0"] if t == 0 else kv["dist_a"])[:r, :]
                        start = kv["sinks_scaled"][:r, h:h + 1]
                    chunks = score_chunks(u)
                    for j, (c0, c1) in enumerate(chunks):
                        x = CHUNK_BASE[u] + j
                        dve.wait_ge(scored, x + 1)
                        dve.tensor_tensor_reduce(probs[:r, u % 3, c0:c1], ps[:r, x % 3, 0:c1 - c0], dist[:, c0:c1], 1.0, start,
                                                 ALU.subtract, ALU.max, top_val[:r, u % 2, j:j + 1]).then_inc(topped, 1)
                    dve.wait_ge(topped, CHUNK_BASE[u + 1])
                    neg = top_neg[:r, branch, h:h + 1]
                    if len(chunks) == 1:
                        dve.tensor_scalar(neg, top_val[:r, u % 2, 0:1], -slope(h), None, ALU.mult).then_inc(neg_ready, 1)
                    else:
                        n = len(chunks)
                        dve.tensor_scalar(top_all[:r, 0:n], top_val[:r, u % 2, 0:n], -slope(h), None, ALU.mult, ALU.min,
                                          accum_out=neg).then_inc(neg_ready, 1)

                def split_lo(u):
                    t, branch = section(u)
                    r = tile_rows(t)
                    for j, (a, n) in enumerate(groups(u)):
                        x = GROUPS[u] + j
                        dve.wait_ge(hi_done, x + 1)
                        src = ps[:, T_BANK + x % 3, :].rearrange("p (k n) -> p k n", k=4)[:, 0:n, 0:r]
                        at = (slice(None), (u // 2) % 2, slice(a, a + n), u % 2, slice(0, r))
                        dve.tensor_tensor(pt_lo[at], src, pt_hi[at].bitcast(F32), ALU.subtract).then_inc(lo_done, 1)

                def sink_argument(half):
                    t, _ = section(8 * half)
                    r, hs = tile_rows(t), slice(8 * (half % 2), 8 * (half % 2) + 8)
                    dve.wait_ge(neg_ready, 8 * half + 8)
                    dve.tensor_tensor(sink_e[:r, 0, hs], kv["sinks"][:r, hs], top_neg[:r, 0, hs], ALU.add).then_inc(sink_in, 1)

                def invert(half, sinks):
                    t, branch = section(8 * half)
                    r, hs = tile_rows(t), slice(8 * (half % 2), 8 * (half % 2) + 8)
                    dve.wait_ge(exped, 8 * half + 8)
                    if branch == 0:
                        dve.wait_ge(sink_done, sinks)
                        dve.tensor_tensor(sums[:r, 0, hs], sums[:r, 0, hs], sink_e[:r, 0, hs], ALU.add).then_inc(sum_ready, 1)
                        dve.wait_ge(sum_ready, sinks)
                    dve.reciprocal(inv[:r, branch, hs], sums[:r, branch, hs]).then_inc(inv_ready, 1)

                def normalise(half):
                    t, branch = section(8 * half)
                    r, hs = tile_rows(t), slice(8 * (half % 2), 8 * (half % 2) + 8)
                    dve.wait_ge(folded, 4 * half + 4)
                    dve.wait_ge(inv_ready, half + 1)
                    if t >= 1:
                        dve.wait_ge(merge_step, 3 * t)
                    out = mixed[:r, branch, 512 * (half % 2):512 * (half % 2) + 512].rearrange("p (h d) -> p h d", d=HD)
                    src = ps[:r, O_BANK, :].rearrange("p (h d) -> p h d", d=HD)
                    scale = inv[:r, branch, hs].unsqueeze(2).to_broadcast([r, 8, HD])
                    dve.tensor_tensor(out, src, scale, ALU.mult).then_inc(normed, 1)

                sinks = 0
                for u in range(UNITS + 6):
                    if u < UNITS:
                        subtract_distance(u)
                    if u >= 12 and u % 8 == 4 and (u - 12) // 8 < UNITS // 8:
                        normalise((u - 12) // 8)
                    if u >= 2 and u - 2 < UNITS:
                        split_lo(u - 2)
                    if u >= 8 and u % 8 == 0 and u <= UNITS and section(u - 8)[1] == 0:
                        sink_argument(u // 8 - 1)
                        sinks += 1
                    if u >= 8 and u % 8 == 2 and (u - 10) // 8 < UNITS // 8:
                        invert((u - 10) // 8, sinks)


            @block.tensor
            def _(pe):
                def score(u):
                    t, branch = section(u)
                    r, h, s = tile_rows(t), u % HEADS, u // HEADS
                    if h == 0:
                        pe.wait_ge(q_lo_done, s + 1)
                    for j, (c0, c1) in enumerate(score_chunks(u)):
                        x = CHUNK_BASE[u] + j
                        if x >= 3:
                            pe.wait_ge(topped, x - 2)
                        for k, k0, at, n in keys(t, branch, h):
                            a, b = max(at, c0), min(at + n, c1)
                            if a >= b:
                                continue
                            for part in range(2):
                                last = pe.matmul(ps[:r, x % 3, a - c0:b - c0], q_st[:, branch, h, 0:r],
                                                 k[:, part, k0 + a - at:k0 + b - at], start=(part == 0), stop=(part == 1))
                        last.then_inc(scored, 1)

                def turn(u):
                    t, branch = section(u)
                    r, tiles = tile_rows(t), tiles_of(u)
                    pe.wait_ge(exped, u + 1)
                    for j, (a, n) in enumerate(groups(u)):
                        x = GROUPS[u] + j
                        if x >= 3:
                            pe.wait_ge(lo_done, x - 2)
                        for b in range(n):
                            col = tiles[a + b][0]
                            last = pe.transpose(ps[:, T_BANK + x % 3, b * P:b * P + r], probs[:r, u % 3, col:col + P],
                                                c["ident"][:r, :r])
                        last.then_inc(turned, 1)

                def weigh_values(p):
                    u = 2 * p
                    t, branch = section(u)
                    r, tiles = tile_rows(t), tiles_of(u)
                    pe.wait_ge(lo_done, GROUPS[u + 2])
                    if p >= 1:
                        pe.wait_ge(out_copied, p)
                    v = values(t, branch, u % HEADS)
                    for j, (_, rows, slot) in enumerate(tiles):
                        for part, pt in enumerate((pt_hi, pt_lo)):
                            last = pe.matmul(ps[:, PV_BANK, 0:2 * r], v[0:rows, slot, :], pt[0:rows, p % 2, j, :, 0:r],
                                             start=(j == 0 and part == 0), stop=(j == len(tiles) - 1 and part == 1))
                    last.then_inc(valued, 1)

                def fold(p):
                    t, _ = section(2 * p)
                    r, half = tile_rows(t), p // 4
                    pe.wait_ge(out_copied, p + 1)
                    if p % 4 == 0 and half >= 1:
                        pe.wait_ge(normed, half)
                    for b in range(2):
                        h = (2 * p + b) % 8
                        last = pe.matmul(ps[:r, O_BANK, h * HD:(h + 1) * HD], out_t[:, p % 2, b * r:(b + 1) * r],
                                         c["fold"][:], start=True, stop=True)
                    last.then_inc(folded, 1)

                for u in range(UNITS + 6):
                    if u < UNITS:
                        score(u)
                    if u >= 2 and u - 2 < UNITS:
                        turn(u - 2)
                    if u >= 4 and u % 2 == 0 and (u - 4) // 2 < UNITS // 2:
                        weigh_values((u - 4) // 2)
                    if u >= 5 and u % 2 == 1 and (u - 5) // 2 < UNITS // 2:
                        fold((u - 5) // 2)


def attention_buffers(ctx, top, nc):
    sb = lambda n, s, d=F32: ctx.enter_context(nc.sbuf_tensor(n, s, d))
    return {
        "stored": top.enter_context(nc.semaphore("p3_kv_stored")),
        "k_b_p": sb("k_b_p", [P, 2, N_META + N_PROMPT], F32R), "k_b_s": sb("k_b_s", [P, 2, N_META + N_QUERY], F32R),
        "k_a_p": sb("k_a_p", [P, 2, 2, N_META + N_PROMPT], F32R),
        "k_a_s": sb("k_a_s", [P, 2, 2, N_META + WINDOW + N_SAMPLE], F32R),
        "v_b_p": sb("v_b_p", [P, 9, P], F32R), "v_b_s": sb("v_b_s", [P, 10, P], F32R),
        "v_a_p": sb("v_a_p", [P, 2, 9, P], F32R), "v_a_s": sb("v_a_s", [P, 2, 3, P], F32R),
        "dist_a": sb("dist_a", [P, N_META + 2 * P]), "dist_a0": sb("dist_a0", [P, N_META + P]),
        "sinks": sb("sinks", [P, HEADS]), "sinks_scaled": sb("sinks_scaled", [P, HEADS]),
    }


def output_mix(nc, top, c, x2T, ps, merged_scr, w_o, x_prompt, x_sample, g_post_mix, g_pre_mlp, x1_scr):
    x2T_hi, x2T_lo = x2T
    RAW = 4
    UNITS = 2 * KT
    with ExitStack() as ctx:
        sb = lambda n, s, d=F32: ctx.enter_context(nc.sbuf_tensor(n, s, d))
        sem = lambda n: top.enter_context(nc.semaphore(n))
        w_raw = sb("wo_raw", [P, RAW, 512])
        w_hi = sb("wo_hi", [P, KT, D], F32R)
        w_lo = sb("wo_lo", [P, KT, D], F32R)
        m_in = sb("m_in", [P, 2, D])
        mT_hi = sb("mT_hi", [P, 2, KT, P], F32R)
        mT_lo = sb("mT_lo", [P, 2, KT, P], F32R)
        x_in = sb("x_in4", [P, 2, D])
        x1 = sb("x1", [P, 2, D])
        x_norm = sb("x_norm4", [P, 2, D])
        squares = sb("squares4", [P, D])
        g_post = sb("g_post", [P, D])
        g_pre = sb("g_pre", [P, D])
        col = {n: sb("p4_" + n, [P, 2 * TILES]) for n in ("sum_sq", "std", "mean_sq", "rstd_0", "rstd", "newton")}

        w_loaded = [sem(f"p4_w_loaded{i}") for i in range(RAW)]
        w_hi_done, w_lo_done = sem("p4_w_hi_done"), sem("p4_w_lo_done")
        gains_loaded = sem("p4_gains_loaded")
        m_loaded = [sem("p4_m_loaded0"), sem("p4_m_loaded1")]
        x_loaded = [sem("p4_x_loaded0"), sem("p4_x_loaded1")]
        m_turned, m_hi_done, m_lo_done = sem("p4_m_turned"), sem("p4_m_hi_done"), sem("p4_m_lo_done")
        product_done = sem("p4_product_done")
        squared, std_ready, rstd_ready, refined = sem("p4_squared"), sem("p4_std_ready"), sem("p4_rstd_ready"), sem("p4_refined")
        scaled, x1_ready = sem("p4_scaled"), sem("p4_x1_ready")
        x1_stored = [sem("p4_x1_stored0"), sem("p4_x1_stored1")]
        normed, x_turned, x_hi_done, x_lo_done = sem("p4_normed"), sem("p4_x_turned"), sem("p4_x_hi_done"), sem("p4_x_lo_done")

        def toks(t):
            return slice(t * P, t * P + tile_rows(t))

        def product(t):
            return ps[:, 4 + 2 * (t % 2):6 + 2 * (t % 2), :].rearrange("p b n -> p (b n)")[:tile_rows(t)]

        def four(bank, t):
            return ps[:, bank, :].rearrange("p (k n) -> p k n", k=4)[:, :, 0:tile_rows(t)]

        with nc.Block() as block:

            @block.sync
            def _(sp):
                def load_merged(t):
                    if t >= 2:
                        sp.wait_ge(m_turned, 2 * t - 2)
                    sp.dma_start(m_in[:tile_rows(t), t % 2, :], merged_scr[toks(t), :]).then_inc(m_loaded[t % 2], 16)

                def load_x(t):
                    r = tile_rows(t)
                    if t >= 2:
                        sp.wait_ge(x1_ready, t - 1)
                    src = x_prompt[0, toks(t), :] if t < SAMPLE_TILE else x_sample[0]
                    sp.dma_start(x_in[:r, t % 2, :], src).then_inc(x_loaded[t % 2], 16)

                load_merged(0)
                load_merged(1)
                load_x(0)
                load_x(1)
                sp.dma_start(g_post[:], g_post_mix[0:1, :].to_broadcast([P, D])).then_inc(gains_loaded, 16)
                sp.dma_start(g_pre[:], g_pre_mlp[0:1, :].to_broadcast([P, D])).then_inc(gains_loaded, 16)
                for t in range(TILES):
                    if t + 2 < TILES:
                        load_merged(t + 2)
                    sp.wait_ge(x1_ready, t + 1)
                    sp.dma_start(x1_scr[toks(t), :], x1[:tile_rows(t), t % 2, :]).then_inc(x1_stored[t % 2], 16)
                    if t + 2 < TILES:
                        load_x(t + 2)
                sp.wait_ge(x1_stored[0], 16 * 5)
                sp.wait_ge(x1_stored[1], 16 * 4)

            @block.gpsimd
            def _(pool):
                for n in range(UNITS):
                    k, half = n % KT, n // KT
                    at = (slice(None), k, slice(512 * half, 512 * half + 512))
                    pool.wait_ge(w_hi_done, n + 1)
                    pool.tensor_tensor(w_lo[at], w_raw[:, n % RAW, :], w_hi[at].bitcast(F32), ALU.subtract).then_inc(w_lo_done, 1)
                    pool.wait_ge(w_lo_done, n + 1)
                for t in range(TILES):
                    r = tile_rows(t)
                    pool.wait_ge(scaled, t + 1)
                    pool.wait_ge(x_loaded[t % 2], 16 * (t // 2 + 1))
                    pool.tensor_tensor(x1[:r, t % 2, :], x1[:r, t % 2, :], x_in[:r, t % 2, :], ALU.add).then_inc(x1_ready, 1)
                    pool.wait_ge(x1_ready, t + 1)

            @block.scalar
            def _(act):
                def load_w(n):
                    k, half = n % KT, n // KT
                    if n >= RAW:
                        act.wait_ge(w_lo_done, n - RAW + 1)
                    act.dma_start(w_raw[:, n % RAW, :], w_o[0, k * P:(k + 1) * P, 512 * half:512 * half + 512])\
                       .then_inc(w_loaded[n % RAW], 16)

                def norm_statistics(t, which, src):
                    j, r = 2 * t + which, tile_rows(t)
                    act.activation(squares[:r], src, ACT.Square, accum_out=col["sum_sq"][:r, j:j + 1]).then_inc(squared, 1)
                    act.wait_ge(squared, j + 1)
                    act.activation(col["std"][:r, j:j + 1], col["sum_sq"][:r, j:j + 1], ACT.Sqrt, bias=c["eps"][:r, :],
                                   scale=1.0 / D).then_inc(std_ready, 1)

                def merged_hi(t):
                    for g in range(2):
                        act.wait_ge(m_turned, 2 * t + g + 1)
                        if t >= 2:
                            act.wait_ge(product_done, t - 1)
                        act.activation(mT_hi[:, t % 2, 4 * g:4 * g + 4, 0:tile_rows(t)], four(g, t), ACT.Copy).then_inc(m_hi_done, 1)

                def normed_hi(t):
                    for g in range(2):
                        act.wait_ge(x_turned, 2 * t + g + 1)
                        act.activation(x2T_hi[:, 4 * g:4 * g + 4, toks(t)], four(2 + g, t), ACT.Copy).then_inc(x_hi_done, 1)

                for n in range(RAW):
                    load_w(n)
                merged_hi(0)
                for n in range(UNITS):
                    act.wait_ge(w_loaded[n % RAW], 16 * (n // RAW + 1))
                    k, half = n % KT, n // KT
                    act.activation(w_hi[:, k, 512 * half:512 * half + 512], w_raw[:, n % RAW, :], ACT.Copy).then_inc(w_hi_done, 1)
                    if 1 <= n and n + RAW - 1 < UNITS:
                        load_w(n + RAW - 1)
                for t in range(1, TILES + 2):
                    if t < TILES:
                        merged_hi(t)
                    if t - 1 < TILES:
                        act.wait_ge(product_done, t)
                        norm_statistics(t - 1, 0, product(t - 1))
                    if t - 1 < TILES:
                        act.wait_ge(x1_ready, t)
                        norm_statistics(t - 1, 1, x1[:tile_rows(t - 1), (t - 1) % 2, :])
                    if 0 <= t - 2:
                        normed_hi(t - 2)

            @block.vector
            def _(dve):
                def rstd(t, which):
                    j, r = 2 * t + which, tile_rows(t)
                    one = lambda n: col[n][:r, j:j + 1]
                    dve.wait_ge(std_ready, j + 1)
                    dve.reciprocal(one("rstd_0"), one("std")).then_inc(rstd_ready, 1)
                    dve.tensor_scalar(one("mean_sq"), one("sum_sq"), 1.0 / D, EPS, ALU.mult, ALU.add).then_inc(rstd_ready, 1)
                    dve.wait_ge(rstd_ready, 2 * j + 2)
                    refine_rstd(dve, refined, 3 * j, one("rstd"), one("rstd_0"), one("mean_sq"), one("newton"))
                    return one("rstd")

                def merged_lo(t):
                    for g in range(2):
                        dve.wait_ge(m_hi_done, 2 * t + g + 1)
                        at = (slice(None), t % 2, slice(4 * g, 4 * g + 4), slice(0, tile_rows(t)))
                        dve.tensor_tensor(mT_lo[at], four(g, t), mT_hi[at].bitcast(F32), ALU.subtract).then_inc(m_lo_done, 1)

                def normed_lo(t):
                    for g in range(2):
                        dve.wait_ge(x_hi_done, 2 * t + g + 1)
                        at = (slice(None), slice(4 * g, 4 * g + 4), toks(t))
                        dve.tensor_tensor(x2T_lo[at], four(2 + g, t), x2T_hi[at].bitcast(F32), ALU.subtract).then_inc(x_lo_done, 1)

                def scale_product(t):
                    r = tile_rows(t)
                    s = rstd(t, 0)
                    if t >= 2:
                        dve.wait_ge(x1_stored[t % 2], 16 * (t // 2))
                        dve.wait_ge(normed, t - 1)
                    dve.scalar_tensor_tensor(out=x1[:r, t % 2, :], in0=product(t), scalar=s, in1=g_post[:r, :],
                                             op0=ALU.mult, op1=ALU.mult).then_inc(scaled, 1)

                def norm_x1(t):
                    r = tile_rows(t)
                    s = rstd(t, 1)
                    if t >= 2:
                        dve.wait_ge(x_turned, 2 * t - 2)
                    dve.scalar_tensor_tensor(out=x_norm[:r, t % 2, :], in0=x1[:r, t % 2, :], scalar=s, in1=g_pre[:r, :],
                                             op0=ALU.mult, op1=ALU.mult).then_inc(normed, 1)

                merged_lo(0)
                dve.wait_ge(gains_loaded, 32)
                for t in range(1, TILES + 2):
                    if t < TILES:
                        merged_lo(t)
                    if t - 1 < TILES:
                        scale_product(t - 1)
                    if t - 1 < TILES:
                        norm_x1(t - 1)
                    if 0 <= t - 2:
                        normed_lo(t - 2)

            @block.tensor
            def _(pe):
                def turn_merged(t):
                    pe.wait_ge(m_loaded[t % 2], 16 * (t // 2 + 1))
                    for g in range(2):
                        if t >= 1:
                            pe.wait_ge(m_lo_done, 2 * t + g - 1)
                        for k in range(4):
                            last = pe.transpose(ps[:, g, k * P:k * P + tile_rows(t)],
                                                m_in[:tile_rows(t), t % 2, (4 * g + k) * P:(4 * g + k + 1) * P],
                                                c["ident"][:tile_rows(t), :tile_rows(t)])
                        last.then_inc(m_turned, 1)

                def turn_normed(t):
                    pe.wait_ge(normed, t + 1)
                    for g in range(2):
                        if t >= 1:
                            pe.wait_ge(x_lo_done, 2 * t + g - 1)
                        for k in range(4):
                            last = pe.transpose(ps[:, 2 + g, k * P:k * P + tile_rows(t)],
                                                x_norm[:tile_rows(t), t % 2, (4 * g + k) * P:(4 * g + k + 1) * P],
                                                c["ident"][:tile_rows(t), :tile_rows(t)])
                        last.then_inc(x_turned, 1)

                def multiply(t):
                    r = tile_rows(t)
                    pe.wait_ge(m_lo_done, 2 * t + 2)
                    if t >= 2:
                        pe.wait_ge(scaled, t - 1)
                    for half in range(2):
                        if t == 0:
                            pe.wait_ge(w_lo_done, KT * (half + 1))
                        out = product(t)[:, 512 * half:512 * half + 512]
                        cols = slice(512 * half, 512 * half + 512)
                        for k in range(KT):
                            m_hi, m_lo = mT_hi[:, t % 2, k, 0:r], mT_lo[:, t % 2, k, 0:r]
                            for j, (a, b) in enumerate(((m_hi, w_hi), (m_hi, w_lo), (m_lo, w_hi))):
                                last = pe.matmul(out, a, b[:, k, cols], start=(k == 0 and j == 0), stop=(k == KT - 1 and j == 2))
                    last.then_inc(product_done, 1)

                turn_merged(0)
                for t in range(1, TILES + 2):
                    if t < TILES:
                        turn_merged(t)
                    if t - 1 < TILES:
                        multiply(t - 1)
                    if 0 <= t - 2:
                        turn_normed(t - 2)


def mlp(nc, top, c, x2T, ps, w_up, w_down, g_post_mlp, x1_scr, y_prompt, y_sample):
    x2T_hi, x2T_lo = x2T
    CH = 256
    FT = CH // P
    N_CH = D_FF // CH
    UP_UNITS, DOWN_UNITS = 4, 4
    UP_GROUPS = [(f, t0, n) for f in range(FT) for t0, n in TOK_BLOCKS]
    DOWN_GROUPS = [(t, half) for t in range(TILES) for half in range(2)]
    N_UP, N_DOWN = len(UP_GROUPS), len(DOWN_GROUPS)
    UP_BANKS = 2
    DOWN_BANKS = 6
    with ExitStack() as ctx:
        sb = lambda n, s, d=F32: ctx.enter_context(nc.sbuf_tensor(n, s, d))
        sem = lambda n: top.enter_context(nc.semaphore(n))
        up_raw = sb("up_raw", [P, UP_UNITS, 2, CH])
        down_raw = sb("down_raw", [P, DOWN_UNITS, 512])
        up_hi = sb("up_hi", [P, KT, CH], F32R)
        up_lo = sb("up_lo", [P, KT, CH], F32R)
        down_hi = sb("down_hi", [P, FT, D], F32R)
        down_lo = sb("down_lo", [P, FT, D], F32R)
        hidden = sb("hidden", [P, 2, 364])
        hid_hi = sb("hid_hi", [P, FT, N_QUERY], F32R)
        hid_lo = sb("hid_lo", [P, FT, N_QUERY], F32R)
        total = sb("total", [P, TILES, D])
        x1_in = sb("x1_in", [P, 2, D])
        squares = sb("squares5", [P, D])
        gain = sb("gain5", [P, D])
        col = {n: sb("p5_" + n, [P, TILES]) for n in ("sum_sq", "std", "mean_sq", "rstd_0", "rstd", "newton")}

        up_loaded = [sem(f"p5_up_loaded{i}") for i in range(UP_UNITS)]
        down_loaded = [sem(f"p5_down_loaded{i}") for i in range(DOWN_UNITS)]
        up_hi_done, up_lo_done = sem("p5_up_hi_done"), sem("p5_up_lo_done")
        down_hi_done, down_lo_done = sem("p5_down_hi_done"), sem("p5_down_lo_done")
        up_done, relu_done, squared_done, hid_hi_done, hid_lo_done = (sem("p5_" + n) for n in ("up_done", "relu_done", "squared_done", "hid_hi_done", "hid_lo_done"))
        down_done, added, cleared = sem("p5_down_done"), sem("p5_added"), sem("p5_cleared")
        gain_loaded = sem("p5_gain_loaded")
        x1_loaded = [sem("p5_x1_loaded0"), sem("p5_x1_loaded1")]
        sq_done, std_ready, rstd_ready, refined = sem("p5_sq_done"), sem("p5_std_ready"), sem("p5_rstd_ready"), sem("p5_refined")
        scaled, y_ready, y_stored = sem("p5_scaled"), sem("p5_y_ready"), sem("p5_y_stored")

        def toks(t):
            return slice(t * P, t * P + tile_rows(t))

        up_src = w_up[0].rearrange("(u k p) f -> u p k f", k=2, p=P)

        with nc.Block() as block:

            def store_y(sp, t):
                r = tile_rows(t)
                sp.wait_ge(y_ready, t + 1)
                dst = y_prompt[0, toks(t), :] if t < SAMPLE_TILE else y_sample[0]
                sp.dma_start(dst, total[:r, t, :]).then_inc(y_stored, 16)

            @block.sync
            def _(sp):
                def load_up(j, first):
                    for u in range(UP_UNITS):
                        if not first:
                            sp.wait_ge(up_lo_done, (j - 1) * KT + (2 * u + 2))
                        sp.dma_start(up_raw[:, u], up_src[u][:, :, bass.ds(j * CH, CH)]).then_inc(up_loaded[u], 16)

                def load_down(j, first):
                    for u in range(DOWN_UNITS):
                        f, half = divmod(u, 2)
                        if not first:
                            sp.wait_ge(down_lo_done, (j - 1) * DOWN_UNITS + (u + 1))
                        src = w_down[0, bass.ds(j * CH + f * P, P), 512 * half:512 * half + 512]
                        sp.dma_start(down_raw[:, u, :], src).then_inc(down_loaded[u], 16)

                load_up(0, True)
                load_down(0, True)
                sp.dma_start(gain[:], g_post_mlp[0:1, :].to_broadcast([P, D])).then_inc(gain_loaded, 16)
                with sp.Fori(1, N_CH) as j:
                    load_up(j, False)
                    load_down(j, False)
                for t in range(TILES):
                    if t >= 2:
                        sp.wait_ge(y_ready, t - 1)
                    sp.dma_start(x1_in[:tile_rows(t), t % 2, :], x1_scr[toks(t), :]).then_inc(x1_loaded[t % 2], 16)
                    if t >= 1:
                        store_y(sp, t - 1)
                store_y(sp, TILES - 1)
                sp.wait_ge(y_stored, 16 * TILES)

            @block.gpsimd
            def _(pool):
                def split_up_lo(j):
                    for k in range(KT):
                        pool.wait_ge(up_hi_done, j * KT + (k + 1))
                        pool.tensor_tensor(up_lo[:, k, :], up_raw[:, k // 2, k % 2, :], up_hi[:, k, :].bitcast(F32),
                                           ALU.subtract).then_inc(up_lo_done, 1)

                def split_down_lo(j):
                    for u in range(DOWN_UNITS):
                        f, half = divmod(u, 2)
                        at = (slice(None), f, slice(512 * half, 512 * half + 512))
                        pool.wait_ge(down_hi_done, j * DOWN_UNITS + (u + 1))
                        pool.tensor_tensor(down_lo[at], down_raw[:, u, :], down_hi[at].bitcast(F32), ALU.subtract).then_inc(down_lo_done, 1)

                split_up_lo(0)
                with pool.Fori(0, N_CH - 1) as j:
                    split_down_lo(j)
                    split_up_lo(j + 1)
                split_down_lo(N_CH - 1)
                pool.wait_ge(down_lo_done, N_CH * DOWN_UNITS)
                for t in range(TILES):
                    r = tile_rows(t)
                    pool.wait_ge(scaled, t + 1)
                    pool.wait_ge(x1_loaded[t % 2], 16 * (t // 2 + 1))
                    pool.tensor_tensor(total[:r, t, :], total[:r, t, :], x1_in[:r, t % 2, :], ALU.add).then_inc(y_ready, 1)
                    pool.wait_ge(y_ready, t + 1)

            @block.scalar
            def _(act):
                def split_up_hi(j, first=False):
                    if not first:
                        act.wait_ge(up_done, j * N_UP)
                    for k in range(KT):
                        act.wait_ge(up_loaded[k // 2], (j + 1) * 16)
                        act.activation(up_hi[:, k, :], up_raw[:, k // 2, k % 2, :], ACT.Copy).then_inc(up_hi_done, 1)

                def chunk(j, first=False):
                    for g in range(N_UP + 1):
                        if g < DOWN_UNITS:
                            fd, half = divmod(g, 2)
                            act.wait_ge(down_done, j * N_DOWN)
                            act.wait_ge(down_loaded[g], (j + 1) * 16)
                            act.activation(down_hi[:, fd, 512 * half:512 * half + 512], down_raw[:, g, :], ACT.Copy)\
                               .then_inc(down_hi_done, 1)
                        if g < N_UP:
                            n = UP_GROUPS[g][2]
                            act.wait_ge(up_done, j * N_UP + (g + 1))
                            if g >= 2:
                                act.wait_ge(hid_lo_done, j * N_UP + (g - 1))
                            elif not first:
                                act.wait_ge(hid_lo_done, j * N_UP)
                            act.activation(hidden[:, g % 2, 0:n], ps[:, g % UP_BANKS, 0:n], ACT.Relu).then_inc(relu_done, 1)
                        if g >= 1:
                            f, t0, n = UP_GROUPS[g - 1]
                            act.wait_ge(squared_done, j * N_UP + g)
                            act.activation(hid_hi[:, f, t0:t0 + n], hidden[:, (g - 1) % 2, 0:n], ACT.Copy).then_inc(hid_hi_done, 1)

                split_up_hi(0, first=True)
                chunk(0, first=True)
                with act.Fori(1, N_CH) as j:
                    split_up_hi(j)
                    chunk(j)
                for t in range(TILES):
                    r = tile_rows(t)
                    act.wait_ge(added, (N_CH - 1) * N_DOWN + 2 * t + 2)
                    act.activation(squares[:r], total[:r, t, :], ACT.Square, accum_out=col["sum_sq"][:r, t:t + 1]).then_inc(sq_done, 1)
                    act.wait_ge(sq_done, t + 1)
                    act.activation(col["std"][:r, t:t + 1], col["sum_sq"][:r, t:t + 1], ACT.Sqrt, bias=c["eps"][:r, :],
                                   scale=1.0 / D).then_inc(std_ready, 1)

            @block.vector
            def _(dve):
                def square_hidden(j):
                    for g in range(N_UP + 1):
                        if g < N_UP:
                            h = hidden[:, g % 2, 0:UP_GROUPS[g][2]]
                            dve.wait_ge(relu_done, j * N_UP + (g + 1))
                            dve.tensor_tensor(h, h, h, ALU.mult).then_inc(squared_done, 1)
                        if g >= 1:
                            f, t0, n = UP_GROUPS[g - 1]
                            dve.wait_ge(hid_hi_done, j * N_UP + g)
                            dve.tensor_tensor(hid_lo[:, f, t0:t0 + n], hidden[:, (g - 1) % 2, 0:n],
                                              hid_hi[:, f, t0:t0 + n].bitcast(F32), ALU.subtract).then_inc(hid_lo_done, 1)

                def add_down(j, g):
                    t, half = DOWN_GROUPS[g]
                    r = tile_rows(t)
                    out = total[:r, t, 512 * half:512 * half + 512]
                    dve.wait_ge(down_done, j * N_DOWN + (g + 1))
                    dve.tensor_tensor(out, out, ps[:r, UP_BANKS + g % DOWN_BANKS, :], ALU.add).then_inc(added, 1)

                def scale_total(t):
                    r = tile_rows(t)
                    one = lambda n: col[n][:r, t:t + 1]
                    dve.wait_ge(std_ready, t + 1)
                    dve.reciprocal(one("rstd_0"), one("std")).then_inc(rstd_ready, 1)
                    dve.tensor_scalar(one("mean_sq"), one("sum_sq"), 1.0 / D, EPS, ALU.mult, ALU.add).then_inc(rstd_ready, 1)
                    dve.wait_ge(rstd_ready, 2 * t + 2)
                    refine_rstd(dve, refined, 3 * t, one("rstd"), one("rstd_0"), one("mean_sq"), one("newton"))
                    dve.scalar_tensor_tensor(out=total[:r, t, :], in0=total[:r, t, :], scalar=one("rstd"), in1=gain[:r, :],
                                             op0=ALU.mult, op1=ALU.mult).then_inc(scaled, 1)

                dve.memset(total[:], 0.0).then_inc(cleared, 1)
                dve.wait_ge(cleared, 1)
                with dve.Fori(0, N_CH - 1) as j:
                    dve.wait_ge(added, j * N_DOWN)
                    square_hidden(j)
                    for g in range(N_DOWN):
                        add_down(j, g)
                dve.wait_ge(added, (N_CH - 1) * N_DOWN)
                square_hidden(N_CH - 1)
                dve.wait_ge(gain_loaded, 16)
                for t in range(TILES):
                    add_down(N_CH - 1, 2 * t)
                    add_down(N_CH - 1, 2 * t + 1)
                    if t >= 2:
                        scale_total(t - 2)
                scale_total(TILES - 2)
                scale_total(TILES - 1)

            @block.tensor
            def _(pe):
                def chunk(j, first=False):
                    pe.wait_ge(up_lo_done, (j + 1) * KT)
                    for g, (f, t0, n) in enumerate(UP_GROUPS):
                        if g >= UP_BANKS:
                            pe.wait_ge(relu_done, j * N_UP + (g - UP_BANKS + 1))
                        elif not first:
                            pe.wait_ge(relu_done, j * N_UP - UP_BANKS + (g + 1))
                        fs = slice(f * P, (f + 1) * P)
                        for k in range(KT):
                            x_hi, x_lo = x2T_hi[:, k, t0:t0 + n], x2T_lo[:, k, t0:t0 + n]
                            for i, (a, b) in enumerate(((up_hi, x_hi), (up_hi, x_lo), (up_lo, x_hi))):
                                last = pe.matmul(ps[:, g % UP_BANKS, 0:n], a[:, k, fs], b, start=(k == 0 and i == 0),
                                                 stop=(k == KT - 1 and i == 2))
                        last.then_inc(up_done, 1)
                    pe.wait_ge(down_lo_done, (j + 1) * DOWN_UNITS)
                    for g, (t, half) in enumerate(DOWN_GROUPS):
                        r = tile_rows(t)
                        block_of = max(b for b, (t0, n) in enumerate(TOK_BLOCKS) if t0 < t * P + r)
                        if half == 0:
                            pe.wait_ge(hid_lo_done, j * N_UP + (len(TOK_BLOCKS) * (FT - 1) + block_of + 1))
                        if g >= DOWN_BANKS:
                            pe.wait_ge(added, j * N_DOWN + (g - DOWN_BANKS + 1))
                        elif not first:
                            pe.wait_ge(added, (j - 1) * N_DOWN + (N_DOWN - DOWN_BANKS + g + 1))
                        cols = slice(512 * half, 512 * half + 512)
                        for f in range(FT):
                            h_hi, h_lo = hid_hi[:, f, toks(t)], hid_lo[:, f, toks(t)]
                            for i, (a, b) in enumerate(((h_hi, down_hi), (h_hi, down_lo), (h_lo, down_hi))):
                                last = pe.matmul(ps[:r, UP_BANKS + g % DOWN_BANKS, :], a, b[:, f, cols],
                                                 start=(f == 0 and i == 0), stop=(f == FT - 1 and i == 2))
                        last.then_inc(down_done, 1)

                chunk(0, first=True)
                with pe.Fori(1, N_CH) as j:
                    chunk(j)


def streaming_step(nc, a, o):
    scratch = lambda name, shape: nc.dram_tensor(name, shape, F32).ap()
    t_scr = scratch("t_scr", (N_TOK, T_WIDTH))
    q_scr = scratch("q_scr", (2 * D + IDX_HEADS * HD, N_QUERY))
    gate_scr = scratch("gate_scr", (N_QUERY, 2 * D))
    dist_scr = scratch("dist_scr", (TILES, P, N_META + N_QUERY))
    merged_scr = scratch("merged_scr", (N_QUERY, D))
    x1_scr = scratch("x1_scr", (N_QUERY, D))
    caches = [a[n] for n in ("cache_k_a", "cache_v_a", "cache_k_b", "cache_v_b", "cache_meta")]
    with ExitStack() as top:
        c = constants(lambda n, s: top.enter_context(nc.sbuf_tensor(n, s, F32)))
        ps = top.enter_context(nc.psum_tensor("ps", [P, 8, 512], F32))
        with ExitStack() as ctx:
            xT = [ctx.enter_context(nc.sbuf_tensor(n, [P, KT, N_TOK], F32R)) for n in ("xT_hi", "xT_lo")]
            input_norm(nc, top, c, xT, ps, a["x_prompt"], a["x_sample"], a["meta_tokens"], a["g_pre_mix"])
            projection(nc, top, c, xT, ps, a["w_in"], a["cache_ki_b"], t_scr, q_scr, gate_scr, dist_scr)
        with ExitStack() as ctx:
            kv = attention_buffers(ctx, top, nc)
            attention_operands(nc, top, c, ps, kv, t_scr, caches, a["attn_sinks"])
            attention(nc, top, c, ps, kv, q_scr, gate_scr, dist_scr, merged_scr, t_scr, caches, o)
        with ExitStack() as ctx:
            x2T = [ctx.enter_context(nc.sbuf_tensor(n, [P, KT, N_QUERY], F32R)) for n in ("x2T_hi", "x2T_lo")]
            output_mix(nc, top, c, x2T, ps, merged_scr, a["w_o"], a["x_prompt"], a["x_sample"], a["g_post_mix"],
                       a["g_pre_mlp"], x1_scr)
            mlp(nc, top, c, x2T, ps, a["w_up"], a["w_down"], a["g_post_mlp"], x1_scr, o["y_prompt"], o["y_sample"])


_INS = ["x_prompt", "x_sample", "cache_k_a", "cache_v_a", "cache_k_b", "cache_v_b", "cache_ki_b", "cache_meta",
        "meta_tokens", "g_pre_mix", "w_in", "attn_sinks", "w_o", "g_post_mix", "g_pre_mlp", "w_up", "w_down", "g_post_mlp"]
_OUTS = [("y_prompt", (1, N_PROMPT, D)), ("y_sample", (1, N_SAMPLE, D)),
         ("k_a_prompt", (1, 1, WINDOW, 2, HD)), ("v_a_prompt", (1, 1, WINDOW, 2, HD)),
         ("k_b_prompt", (1, 1, N_PROMPT, 1, HD)), ("v_b_prompt", (1, 1, N_PROMPT, 1, HD)),
         ("ki_b_prompt", (1, 1, N_PROMPT, HD)), ("meta_prompt", (1, 1, N_META, 6, HD)),
         ("k_a_sample", (1, 1, WINDOW, 2, HD)), ("v_a_sample", (1, 1, WINDOW, 2, HD)),
         ("k_b_sample", (1, 1, N_SAMPLE, 1, HD)), ("v_b_sample", (1, 1, N_SAMPLE, 1, HD)),
         ("ki_b_sample", (1, 1, N_SAMPLE, HD))]


def kernel(**inputs):
    import numpy as np
    import concourse.bacc as bacc
    from concourse.bass_utils import run_bass_kernel_spmd

    nc = bacc.Bacc("TRN2", target_bir_lowering=False, num_devices=1)
    arrays, a, o = {}, {}, {}
    for name in _INS:
        arrays[f"in_{name}"] = np.ascontiguousarray(inputs[name])
        a[name] = nc.dram_tensor(f"in_{name}", arrays[f"in_{name}"].shape, F32, kind="ExternalInput").ap()
    for name, shape in _OUTS:
        o[name] = nc.dram_tensor(f"out_{name}", shape, F32, kind="ExternalOutput").ap()
    streaming_step(nc, a, o)
    r = run_bass_kernel_spmd(nc, [arrays], core_ids=[0])
    return tuple(r.results[0][f"out_{name}"] for name, _ in _OUTS)
```

```python
from contextlib import ExitStack

import concourse.bass as bass
from concourse import mybir

F32 = mybir.dt.float32
F32R = mybir.dt.float32r
ALU = mybir.AluOpType
ACT = mybir.ActivationFunctionType

P = 128
D = 1024
KT = D // P
HD = 64
HEADS = 16
CHUNK = 64
N_PROMPT, N_SAMPLE, N_META = 1024, 64, 16
N_QUERY = N_PROMPT + N_SAMPLE
N_TOK = N_QUERY + N_META
TILES = 9
SAMPLE_TILE = 8
PAST = 1024
WINDOW = 128
IDX_HEADS = 8
TOPK = 256
D_FF = 4 * D
EPS = 1e-6
INDEX_SCALE = (IDX_HEADS * HD) ** -0.5

QA, KA, QB, QI, KI, GA, D_IN = 0, 1024, 1280, 2432, 2944, 3016, 5064
KB = 2304
T_COLS = [(KA, 256), (KB, 128), (KI, 72)]
T_WIDTH = sum(n for _, n in T_COLS)
T_KA, T_VA, T_KB, T_VB, T_KI, T_WI = 0, 128, 256, 320, 384, 448

FAR = 1e30
TAKEN = -3.4e38
UNSEEN = -3.0e38


def slope(h):
    return 2.0 ** (-8.0 * (h + 1) / HEADS)


def tile_rows(t):
    return P if t < SAMPLE_TILE else N_SAMPLE


def tile_tokens(t):
    return P if t < SAMPLE_TILE else N_SAMPLE + N_META


def constants(sb):
    c = {}
    c["ident"] = sb("ident", [P, P])
    c["fold"] = sb("fold", [P, HD])
    c["eps"] = sb("eps", [P, 1])
    c["q_scale"] = sb("q_scale", [P, KT])
    return c


def refine_rstd(dve, step, n, out, rstd, mean_sq, work):
    dve.tensor_scalar(work, rstd, rstd, mean_sq, ALU.mult, ALU.mult).then_inc(step, 1)
    dve.wait_ge(step, n + 1)
    dve.tensor_scalar(work, work, -0.5, 1.5, ALU.mult, ALU.add).then_inc(step, 1)
    dve.wait_ge(step, n + 2)
    dve.tensor_tensor(out, rstd, work, ALU.mult).then_inc(step, 1)
    dve.wait_ge(step, n + 3)


def input_norm(nc, top, c, xT, ps, x_prompt, x_sample, meta_tokens, g_pre_mix):
    xT_hi, xT_lo = xT
    with ExitStack() as ctx:
        sb = lambda n, s, d=F32: ctx.enter_context(nc.sbuf_tensor(n, s, d))
        sem = lambda n: top.enter_context(nc.semaphore(n))
        x_in = sb("x_in", [P, 2, D])
        x_norm = sb("x_norm", [P, 2, D])
        squares = sb("squares", [P, D])
        sum_sq = sb("sum_sq", [P, TILES])
        std = sb("std", [P, TILES])
        mean_sq = sb("mean_sq", [P, TILES])
        rstd_0 = sb("rstd_0", [P, TILES])
        rstd = sb("rstd", [P, TILES])
        newton = sb("newton", [P, TILES])
        gain = sb("gain", [P, D])
        refined = sem("p1_refined")

        zeroed, const_ready = sem("p1_zeroed"), sem("p1_const_ready")
        gains_loaded = sem("p1_gains_loaded")
        x_loaded = [sem("p1_x_loaded0"), sem("p1_x_loaded1")]
        squared, std_ready, rstd_ready = sem("p1_squared"), sem("p1_std_ready"), sem("p1_rstd_ready")
        normed, transposed = sem("p1_normed"), sem("p1_transposed")
        hi_done, lo_done = sem("p1_hi_done"), sem("p1_lo_done")

        def x_loads(t):
            return 16 * (t // 2 + 1 + (t == SAMPLE_TILE))

        def toks(t):
            return slice(t * P, t * P + tile_tokens(t))

        with nc.Block() as block:

            @block.sync
            def _(sp):
                sp.dma_start(gain[:], g_pre_mix[0:1, :].to_broadcast([P, D])).then_inc(gains_loaded, 16)
                for t in range(TILES):
                    if t >= 2:
                        sp.wait_ge(normed, t - 1)
                    dst = x_in[:, t % 2, :]
                    if t < SAMPLE_TILE:
                        sp.dma_start(dst, x_prompt[0, t * P:(t + 1) * P, :]).then_inc(x_loaded[t % 2], 16)
                    else:
                        sp.dma_start(dst[0:N_SAMPLE], x_sample[0]).then_inc(x_loaded[t % 2], 16)
                        sp.dma_start(dst[N_SAMPLE:N_SAMPLE + N_META], meta_tokens).then_inc(x_loaded[t % 2], 16)

            @block.gpsimd
            def _(pool):
                pool.memset(c["ident"][:], 0.0).then_inc(zeroed, 1)
                pool.memset(c["fold"][:], 0.0).then_inc(zeroed, 1)
                pool.memset(c["eps"][:], EPS).then_inc(const_ready, 1)
                pool.wait_ge(zeroed, 2)
                pool.affine_select(out=c["ident"][:], in_=c["ident"][:], compare_op=ALU.not_equal, fill=1.0, base=0,
                                   pattern=[[-1, P]], channel_multiplier=1).then_inc(const_ready, 1)
                pool.affine_select(out=c["fold"][:], in_=c["fold"][:], compare_op=ALU.not_equal, fill=1.0, base=0,
                                   pattern=[[-1, HD]], channel_multiplier=1).then_inc(zeroed, 1)
                pool.wait_ge(zeroed, 3)
                pool.affine_select(out=c["fold"][:], in_=c["fold"][:], compare_op=ALU.not_equal, fill=1.0, base=-HD,
                                   pattern=[[-1, HD]], channel_multiplier=1).then_inc(const_ready, 1)

            @block.scalar
            def _(act):
                def split_hi(t):
                    for g in range(2):
                        act.wait_ge(transposed, 2 * t + g + 1)
                        n = tile_tokens(t)
                        src = ps[:, (2 * t + g) % 4, :].rearrange("p (k n) -> p k n", k=4)[:, :, 0:n]
                        act.activation(xT_hi[:, 4 * g:4 * g + 4, toks(t)], src, ACT.Copy).then_inc(hi_done, 1)

                act.wait_ge(const_ready, 1)
                for t in range(TILES):
                    n = tile_tokens(t)
                    act.wait_ge(x_loaded[t % 2], x_loads(t))
                    act.activation(squares[:n], x_in[:n, t % 2, :], ACT.Square,
                                   accum_out=sum_sq[:n, t:t + 1]).then_inc(squared, 1)
                    act.wait_ge(squared, t + 1)
                    act.activation(std[:n, t:t + 1], sum_sq[:n, t:t + 1], ACT.Sqrt, bias=c["eps"][:n, :],
                                   scale=1.0 / D).then_inc(std_ready, 1)
                    if t >= 1:
                        split_hi(t - 1)
                split_hi(TILES - 1)

            @block.vector
            def _(dve):
                for f in range(KT):
                    for half in range(2):
                        dve.memset(c["q_scale"][half * HD:(half + 1) * HD, f:f + 1], HD ** -0.5 / slope(2 * f + half))

                def split_lo(t):
                    for g in range(2):
                        dve.wait_ge(hi_done, 2 * t + g + 1)
                        n = tile_tokens(t)
                        src = ps[:, (2 * t + g) % 4, :].rearrange("p (k n) -> p k n", k=4)[:, :, 0:n]
                        dst = (slice(None), slice(4 * g, 4 * g + 4), toks(t))
                        dve.tensor_tensor(xT_lo[dst], src, xT_hi[dst].bitcast(F32), ALU.subtract).then_inc(lo_done, 1)

                for t in range(TILES):
                    n = tile_tokens(t)
                    dve.wait_ge(std_ready, t + 1)
                    dve.reciprocal(rstd_0[:n, t:t + 1], std[:n, t:t + 1]).then_inc(rstd_ready, 1)
                    dve.tensor_scalar(mean_sq[:n, t:t + 1], sum_sq[:n, t:t + 1], 1.0 / D, EPS, ALU.mult, ALU.add).then_inc(rstd_ready, 1)
                    dve.wait_ge(rstd_ready, 2 * t + 2)
                    refine_rstd(dve, refined, 3 * t, rstd[:n, t:t + 1], rstd_0[:n, t:t + 1], mean_sq[:n, t:t + 1],
                                newton[:n, t:t + 1])
                    if t == 0:
                        dve.wait_ge(gains_loaded, 16)
                    if t >= 2:
                        dve.wait_ge(transposed, 2 * t - 2)
                    dve.scalar_tensor_tensor(out=x_norm[:n, t % 2, :], in0=x_in[:n, t % 2, :], scalar=rstd[:n, t:t + 1],
                                             in1=gain[:n, :], op0=ALU.mult, op1=ALU.mult).then_inc(normed, 1)
                    if t >= 1:
                        split_lo(t - 1)
                split_lo(TILES - 1)

            @block.tensor
            def _(pe):
                pe.wait_ge(const_ready, 2)
                for t in range(TILES):
                    n = tile_tokens(t)
                    pe.wait_ge(normed, t + 1)
                    for g in range(2):
                        u = 2 * t + g
                        if u >= 4:
                            pe.wait_ge(lo_done, u - 3)
                        for k in range(4):
                            last = pe.transpose(ps[:, u % 4, k * P:k * P + n],
                                                x_norm[:n, t % 2, (4 * g + k) * P:(4 * g + k + 1) * P],
                                                c["ident"][:n, :n])
                        last.then_inc(transposed, 1)


TOKEN_MAJOR, GATE, FEATURE_MAJOR = "token-major", "gate", "feature-major"
CHUNKS = [(TOKEN_MAJOR, T_COLS)]
CHUNKS += [(FEATURE_MAJOR, [(QI, 512)])]
CHUNKS += [(FEATURE_MAJOR, [(QB + 512 * j, 512)]) for j in range(2)]
CHUNKS += [(FEATURE_MAJOR, [(QA + 512 * j, 512)]) for j in range(2)]
CHUNKS += [(GATE, [(GA + 512 * j, 512)]) for j in range(4)]
QT_ROW = {QA: 0, QA + 512: 512, QB: 1024, QB + 512: 1536, QI: 2048}
TOK_BLOCKS = [(0, 364), (364, 362), (726, 362)]
INDEX_TILES = [8, 7, 6, 5, 4, 3, 2]
INDEX_CHUNK = 2


def keys_seen(t):
    return P * (t + 1) if t < SAMPLE_TILE else PAST + N_SAMPLE


def groups_of(c):
    kind = CHUNKS[c][0]
    if kind == FEATURE_MAJOR:
        return [(f, t0, n) for f in range(4) for t0, n in TOK_BLOCKS]
    rows = tile_tokens if kind == TOKEN_MAJOR else tile_rows
    return [(None, t * P, rows(t)) for t in range(TILES)]


GROUP_BASE = [sum(len(groups_of(i)) for i in range(c)) for c in range(len(CHUNKS) + 1)]


def selection_buffers(ctx, nc):
    sb = lambda n, s, d=F32: ctx.enter_context(nc.sbuf_tensor(n, s, d))
    return {
        "score": sb("score", [P, SCORES, N_META + N_QUERY]),
        "top8": sb("top8", [P, 2, 8]),
        "dist": sb("dist", [P, N_PROMPT + P]),
    }


def projection_buffers(ctx, nc):
    sb = lambda n, s, d=F32: ctx.enter_context(nc.sbuf_tensor(n, s, d))
    return {
        "w_raw": sb("w_raw", [P, RAW, 512]),
        "w_hi": sb("w_hi", [P, 2, KT, 512], F32R), "w_lo": sb("w_lo", [P, 2, KT, 512], F32R),
        "stage": sb("stage", [P, STAGE, 512]),
        "w_idx": sb("w_idx", [P, TILES, IDX_HEADS]),
        "kp": sb("kp", [P, 2, N_PROMPT], F32R),
        "ks": sb("ks", [P, 2, N_QUERY], F32R),
        "rel": sb("rel", [P, 2, N_QUERY]),
        "q_raw": sb("q_raw", [P, IDX_HEADS, P]),
        "q_st": sb("q_st", [P, IDX_HEADS, P], F32R),
    }


RAW, STAGE, BANKS, SCORES = 4, 3, 4, 4


def projection(nc, top, c, xT, b2, sel, kv, raw, ps, w_in, caches, cache_ki_b, attn_sinks, t_scr, q_scr, gate_scr, dist_scr):
    xT_hi, xT_lo = xT
    N_CH = len(CHUNKS)
    cache_k_a, cache_v_a, cache_k_b, cache_v_b, cache_meta = caches
    sets = operand_sets(kv, raw)
    GROUPS = key_groups(sets)
    SLOT_BASE = [sum(g[2] for g in GROUPS[:j]) for j in range(len(GROUPS))]
    sem = lambda n: top.enter_context(nc.semaphore(n))
    w_raw, w_hi, w_lo, stage, w_idx, kp, ks, rel, q_raw, q_st = (
        b2[n] for n in ("w_raw", "w_hi", "w_lo", "stage", "w_idx", "kp", "ks", "rel", "q_raw", "q_st"))
    score, top8, dist = sel["score"], sel["top8"], sel["dist"]
    k_raw = rel[:].rearrange("p a b -> p (a b)").rearrange("p (j u d) -> p j u d", u=2, d=HD)
    ps_idx = ps[:, 5:8, :].rearrange("p b n -> p (b n)")

    w_loaded = [sem(f"p2_w_loaded{i}") for i in range(RAW)]
    w_hi_done, w_lo_done = sem("p2_w_hi_done"), sem("p2_w_lo_done")
    group_done, group_out = sem("p2_group_done"), sem("p2_group_out")
    wi_copied = sem("p2_wi_copied")
    stored = [sem(f"p2_stored{i}") for i in range(STAGE)]
    k_loaded, k_turned, k_hi_done, k_lo_done = (sem(f"p2_k_{n}") for n in ("loaded", "turned", "hi_done", "lo_done"))
    q_loaded, q_hi_done, q_lo_done = sem("p2_q_loaded"), sem("p2_q_hi_done"), sem("p2_q_lo_done")
    idx_done, rel_done, weighted, added = sem("p2_idx_done"), sem("p2_rel_done"), sem("p2_weighted"), sem("p2_added")
    dist_iota, dist_ready = sem("p2_dist_iota"), sem("p2_dist_ready")
    first_masks = sem("p2_first_masks")
    select_step = [sem("p2_select_even"), sem("p2_select_odd")]
    mask_ready = sem("p2_mask_ready")
    mask_stored = [sem(f"p2_mask_stored{i}") for i in range(SCORES)]

    def w_loads(n):
        first = sum(16 * len(T_COLS) for m in range(n % RAW, min(n + 1, KT), RAW))
        return first + sum(16 for m in range(n % RAW, n + 1, RAW) if m >= KT)

    def stores(u):
        return 16 * (u // STAGE + 1)

    prompt_loaded, sample_loaded = sem("p3_prompt_loaded"), sem("p3_sample_loaded")
    PROMPT_LOADS, SAMPLE_LOADS = 3, 7
    kt_hi_done, kt_lo_done, kt_turned, kt_copied = (sem(f"p3_k_{n}") for n in ("hi_done", "lo_done", "turned", "copied"))
    v_hi_done, v_lo_done = sem("p3_v_hi_done"), sem("p3_v_lo_done")
    sinks_loaded, band_iota, band_step = sem("p3_sinks_loaded"), sem("p3_band_iota"), sem("p3_band_step")

    def set_loaded(eng, s):
        eng.wait_ge(prompt_loaded, 16 * PROMPT_LOADS)
        if sets[s][3]:
            eng.wait_ge(sample_loaded, 16 * SAMPLE_LOADS)

    MASKS = 2 + len(INDEX_TILES)

    def mask_slot(n):
        return (n + 2) % SCORES

    def slot_free(eng, n):
        if n >= SCORES:
            eng.wait_ge(mask_stored[mask_slot(n)], 16 * (n // SCORES))

    def index_groups(i):
        if i == 0:
            return {g: [2 * (g - 3), 2 * (g - 3) + 1] for g in range(3, 7)}
        return {g: [g - 1] for g in range(1, IDX_HEADS + 1)}

    def unit_cols(ch):
        return sum(n for _, n in CHUNKS[ch][1])

    K_GROUPS = [(0, 4, P, kp, 0), (4, 4, P, kp, 512), (8, 4, P, ks, 0), (12, 4, P, ks, 512), (16, 1, N_SAMPLE, ks, PAST)]

    with nc.Block() as block:

        @block.sync
        def _(sp):
            def store(ch, g):
                kind, segs = CHUNKS[ch]
                f, t0, n = groups_of(ch)[g]
                u = GROUP_BASE[ch] + g
                sp.wait_ge(group_out, u + 1)
                src = stage[:, u % STAGE, :]
                if kind == TOKEN_MAJOR:
                    sp.dma_start(t_scr[t0:t0 + n, :], src[:n, 0:T_WIDTH]).then_inc(stored[u % STAGE], 16)
                elif kind == GATE:
                    col = segs[0][0] - GA
                    sp.dma_start(gate_scr[t0:t0 + n, col:col + 512], src[:n, :]).then_inc(stored[u % STAGE], 16)
                else:
                    row = QT_ROW[segs[0][0]] + f * P
                    sp.dma_start(q_scr[row:row + P, t0:t0 + n], src[:, 0:n]).then_inc(stored[u % STAGE], 16)

            def all_stored(ch):
                for u in range(GROUP_BASE[ch + 1] - STAGE, GROUP_BASE[ch + 1]):
                    sp.wait_ge(stored[u % STAGE], stores(u))

            def load_q(i):
                t = INDEX_TILES[i]
                r = tile_rows(t)
                src = q_scr[2048:2560, t * P:t * P + r].rearrange("(h d) n -> d h n", d=HD)
                for half in range(2):
                    sp.dma_start(q_raw[half * HD:(half + 1) * HD, :, 0:r], src).then_inc(q_loaded, 16)

            def store_mask(n, t):
                sp.wait_ge(mask_ready, n + 1)
                w = N_META + keys_seen(t)
                sp.dma_start(dist_scr[t, 0:tile_rows(t), 0:w], score[:tile_rows(t), mask_slot(n), 0:w])\
                  .then_inc(mask_stored[mask_slot(n)], 16)

            store_mask(0, 0)
            store_mask(1, 1)
            mask_at, LATE_MASKS = {4: [0], 6: [1], 7: [2], 8: [3]}, [4, 5, 6]
            for ch in range(N_CH):
                for g in range(len(groups_of(ch))):
                    store(ch, g)
                    if INDEX_CHUNK <= ch < INDEX_CHUNK + len(INDEX_TILES) - 1 and g == 3:
                        i = ch - INDEX_CHUNK + 1
                        sp.wait_ge(q_lo_done, i)
                        load_q(i)
                if ch == 0:
                    all_stored(0)
                    for half in range(2):
                        sp.dma_start(k_raw[:, 0:8, half, :],
                                     t_scr[0:N_PROMPT, T_KI:T_KI + HD].rearrange("(j p) d -> p j d", p=P)).then_inc(k_loaded, 16)
                        sp.dma_start(k_raw[:, 8:16, half, :],
                                     cache_ki_b[0, 0].rearrange("(j p) d -> p j d", p=P)).then_inc(k_loaded, 16)
                        sp.dma_start(k_raw[0:N_SAMPLE, 16, half, :],
                                     t_scr[N_PROMPT:N_QUERY, T_KI:T_KI + HD]).then_inc(k_loaded, 16)
                if ch == 1:
                    all_stored(1)
                    load_q(0)
                for i in mask_at.get(ch, []):
                    store_mask(i + 2, INDEX_TILES[i])
            all_stored(N_CH - 1)
            sp.wait_ge(group_done, GROUP_BASE[N_CH])
            sp.wait_ge(added, IDX_HEADS * len(INDEX_TILES))
            new = slice(N_PROMPT, N_QUERY)
            T_KV = T_KI
            for j in range(0, 8, 4):
                sp.dma_start(raw["p"][:, j:j + 4, :], t_scr[P * j:P * (j + 4), 0:T_KV].rearrange("(j p) d -> p j d", p=P))\
                  .then_inc(prompt_loaded, 16)
            sp.dma_start(raw["m"][:], t_scr[N_QUERY:N_TOK, 0:T_KV]).then_inc(prompt_loaded, 16)
            sp.dma_start(raw["n"][0:HD], t_scr[new, 0:T_KV]).then_inc(sample_loaded, 16)
            sp.dma_start(raw["n"][HD:P], t_scr[new, 0:T_KV]).then_inc(sample_loaded, 16)
            sp.dma_start(raw["cm"][:], cache_meta[0, 0].rearrange("m s d -> m (s d)")).then_inc(sample_loaded, 16)
            for i, cache in enumerate((cache_k_a, cache_v_a)):
                sp.dma_start(raw["ca"][:, i, :], cache[0, 0].rearrange("n h d -> n (h d)")).then_inc(sample_loaded, 16)
            for i, cache in enumerate((cache_k_b, cache_v_b)):
                sp.dma_start(raw["cb"][:, i], cache[0, 0, :, 0, :].rearrange("(j p) d -> p j d", p=P)).then_inc(sample_loaded, 16)
            sp.dma_start(kv["sinks"][:], attn_sinks[0:1, :].to_broadcast([P, HEADS])).then_inc(sinks_loaded, 16)
            for i in LATE_MASKS:
                store_mask(i + 2, INDEX_TILES[i])
            for n in range(MASKS - SCORES, MASKS):
                sp.wait_ge(mask_stored[mask_slot(n)], 16 * (n // SCORES + 1))

        @block.scalar
        def _(act):
            def load_unit(n):
                ch, k = divmod(n, KT)
                if n >= RAW:
                    act.wait_ge(w_lo_done, n - RAW + 1)
                col = 0
                for c0, w in CHUNKS[ch][1]:
                    act.dma_start(w_raw[:, n % RAW, col:col + w], w_in[0, k * P:(k + 1) * P, c0:c0 + w])\
                       .then_inc(w_loaded[n % RAW], 16)
                    col += w

            def split_hi(n):
                ch, k = divmod(n, KT)
                w = unit_cols(ch)
                act.wait_ge(w_loaded[n % RAW], w_loads(n))
                if ch >= 2:
                    act.wait_ge(group_done, GROUP_BASE[ch - 1])
                act.activation(w_hi[:, ch % 2, k, 0:w], w_raw[:, n % RAW, 0:w], ACT.Copy).then_inc(w_hi_done, 1)
                if n + RAW - 1 < N_CH * KT and n >= 1:
                    load_unit(n + RAW - 1)

            def evacuate(ch, g):
                kind, segs = CHUNKS[ch]
                f, t0, n = groups_of(ch)[g]
                u = GROUP_BASE[ch] + g
                act.wait_ge(group_done, u + 1)
                if u >= STAGE:
                    act.wait_ge(stored[u % STAGE], stores(u - STAGE))
                dst = stage[:, u % STAGE, :]
                bank = ps[:, u % BANKS, :]
                if kind == TOKEN_MAJOR:
                    t = t0 // P
                    act.activation(w_idx[:n, t, :], bank[:n, T_WI:T_WI + IDX_HEADS], ACT.Copy, scale=INDEX_SCALE)\
                       .then_inc(wi_copied, 1)
                    act.activation(dst[:n, 0:T_WIDTH], bank[:n, 0:T_WIDTH], ACT.Copy).then_inc(group_out, 1)
                elif kind == GATE:
                    act.activation(dst[:n, :], bank[:n, :], ACT.Sigmoid).then_inc(group_out, 1)
                elif segs[0][0] == QI:
                    act.activation(dst[:, 0:n], bank[:, 0:n], ACT.Copy).then_inc(group_out, 1)
                else:
                    pair = (QT_ROW[segs[0][0]] % D) // P + f
                    act.activation(dst[:, 0:n], bank[:, 0:n], ACT.Copy,
                                   scale=c["q_scale"][:, pair:pair + 1]).then_inc(group_out, 1)

            def keys_hi(j):
                _, tiles, n, dst, col = K_GROUPS[j]
                act.wait_ge(k_turned, j + 1)
                act.activation(dst[:, 0, col:col + tiles * n], ps[:, 4, 0:tiles * n], ACT.Copy).then_inc(k_hi_done, 1)

            def queries_hi(i):
                r = tile_rows(INDEX_TILES[i])
                act.wait_ge(q_loaded, 32 * (i + 1))
                if i >= 1:
                    act.wait_ge(idx_done, IDX_HEADS * i)
                act.activation(q_st[:, :, 0:r], q_raw[:, :, 0:r], ACT.Copy).then_inc(q_hi_done, 1)

            def relu(i, h):
                n, r = keys_seen(INDEX_TILES[i]), tile_rows(INDEX_TILES[i])
                v = IDX_HEADS * i + h
                act.wait_ge(idx_done, v + 1)
                if v >= 2:
                    act.wait_ge(added, v - 1)
                act.activation(rel[:r, v % 2, 0:n], ps_idx[:r, 0:n], ACT.Relu).then_inc(rel_done, 1)
                if i == 0:
                    return
                act.wait_ge(rel_done, v + 1)
                act.activation(rel[:r, v % 2, 0:n], rel[:r, v % 2, 0:n], ACT.Copy,
                               scale=w_idx[:r, INDEX_TILES[i], h:h + 1]).then_inc(weighted, 1)

            for n in range(RAW):
                load_unit(n)
            for n in range(KT):
                split_hi(n)
            for ch in range(N_CH):
                i = ch - INDEX_CHUNK
                if 0 <= i < len(INDEX_TILES):
                    queries_hi(i)
                for g in range(len(groups_of(ch))):
                    evacuate(ch, g)
                    if g < KT and ch + 1 < N_CH:
                        split_hi((ch + 1) * KT + g)
                    if ch == 1 and 1 <= g <= len(K_GROUPS):
                        keys_hi(g - 1)
                    if 0 <= i < len(INDEX_TILES):
                        for h in index_groups(i).get(g, []):
                            relu(i, h)
            for j, group in enumerate(GROUPS):
                s, first, n, rows, _ = group
                set_loaded(act, s)
                act.activation(raw["k_twice_hi"][0:rows, SLOT_BASE[j]:SLOT_BASE[j] + n], key_source(sets, group), ACT.Copy)\
                   .then_inc(kt_hi_done, 1)
            for s in range(len(sets)):
                for rows, slot, n, src in value_parts(sets, s):
                    act.activation(sets[s][1][rows, slot:slot + n, 0:HD], src, ACT.Copy).then_inc(v_hi_done, 1)
            for j, (s, first, n, rows, col) in enumerate(GROUPS):
                act.wait_ge(kt_turned, j + 1)
                act.activation(sets[s][0][:, :, col:col + n * rows], ps[:, 2 * (j % 4):2 * (j % 4) + 2, 0:n * rows], ACT.Copy)\
                   .then_inc(kt_copied, 1)

        @block.gpsimd
        def _(pool):
            def split_lo(n):
                ch, k = divmod(n, KT)
                w = unit_cols(ch)
                pool.wait_ge(w_hi_done, n + 1)
                i = ch - 1 - INDEX_CHUNK
                if 1 <= i < len(INDEX_TILES):
                    pool.wait_ge(added, IDX_HEADS * i + max(k - 1, 0))
                if 0 <= i < len(INDEX_TILES):
                    pool.wait_ge(q_lo_done, i + 1)
                pool.tensor_tensor(w_lo[:, ch % 2, k, 0:w], w_raw[:, n % RAW, 0:w], w_hi[:, ch % 2, k, 0:w].bitcast(F32),
                                   ALU.subtract).then_inc(w_lo_done, 1)

            def queries_lo(i):
                r = tile_rows(INDEX_TILES[i])
                pool.wait_ge(q_hi_done, i + 1)
                pool.wait_ge(w_lo_done, KT * (i + INDEX_CHUNK + 1))
                pool.wait_ge(added, IDX_HEADS * i)
                pool.tensor_tensor(q_st[HD:, :, 0:r], q_raw[HD:, :, 0:r], q_st[HD:, :, 0:r].bitcast(F32),
                                   ALU.subtract).then_inc(q_lo_done, 1)

            def add_head(i, h):
                t = INDEX_TILES[i]
                n, r = keys_seen(t), tile_rows(t)
                v = IDX_HEADS * i + h
                pool.wait_ge(weighted, v + 1 - IDX_HEADS)
                pool.wait_ge(w_lo_done, KT * (i + INDEX_CHUNK + 1) + min(h + 2, KT))
                pool.wait_ge(q_lo_done, i + 1)
                out = score[:r, mask_slot(i + 2), N_META:N_META + n]
                if h == 0:
                    slot_free(pool, i + 2)
                    pool.tensor_copy(out, rel[:r, v % 2, 0:n]).then_inc(added, 1)
                else:
                    pool.wait_ge(added, v)
                    pool.tensor_tensor(out, out, rel[:r, v % 2, 0:n], ALU.add).then_inc(added, 1)

            pool.iota(dist[:], pattern=[[-1, N_PROMPT + P]], base=N_PROMPT, channel_multiplier=1,
                      allow_small_or_imprecise_dtypes=True).then_inc(dist_iota, 1)
            for n in range(KT):
                split_lo(n)
            for ch in range(N_CH):
                i = ch - INDEX_CHUNK
                if 0 <= i < len(INDEX_TILES):
                    queries_lo(i)
                for g in range(IDX_HEADS + 1):
                    if g < KT and ch + 1 < N_CH:
                        split_lo((ch + 1) * KT + g)
                    if 1 <= i < len(INDEX_TILES) and 1 <= g:
                        add_head(i, g - 1)
            set_loaded(pool, 0)
            for j, group in enumerate(GROUPS):
                s, first, n, rows, _ = group
                set_loaded(pool, s)
                pool.wait_ge(kt_hi_done, j + 1)
                at = (slice(0, rows), slice(SLOT_BASE[j], SLOT_BASE[j] + n))
                pool.tensor_tensor(raw["k_twice_lo"][at], key_source(sets, group), raw["k_twice_hi"][at].bitcast(F32),
                                   ALU.subtract).then_inc(kt_lo_done, 1)
            parts, shifted = 0, False
            for s in range(len(sets)):
                for rows, slot, n, src in value_parts(sets, s):
                    parts += 1
                    pool.wait_ge(v_hi_done, parts)
                    if rows.start or shifted:
                        pool.wait_ge(v_lo_done, parts - 1)
                    shifted = rows.start > 0
                    pool.tensor_tensor(sets[s][1][rows, slot:slot + n, HD:P], src,
                                       sets[s][1][rows, slot:slot + n, 0:HD].bitcast(F32), ALU.subtract).then_inc(v_lo_done, 1)
            pool.wait_ge(v_lo_done, parts)
            pool.iota(kv["dist_a"][:, N_META:], pattern=[[-1, 2 * P]], base=P, channel_multiplier=1,
                      allow_small_or_imprecise_dtypes=True).then_inc(band_iota, 1)

        @block.vector
        def _(dve):
            dve.wait_ge(dist_iota, 1)
            dve.scalar_tensor_tensor(out=dist[:], in0=dist[:], scalar=-1.0, in1=dist[:], op0=ALU.mult,
                                     op1=ALU.max).then_inc(dist_ready, 1)
            dve.memset(score[:, :, 0:N_META], 0.0).then_inc(dist_ready, 1)
            dve.wait_ge(dist_ready, 2)
            for t in range(2):
                n = keys_seen(t)
                dve.tensor_copy(score[:, mask_slot(t), N_META:N_META + n], dist[:, N_PROMPT - t * P:N_PROMPT - t * P + n]).then_inc(first_masks, 1)
                dve.wait_ge(first_masks, t + 1)
                dve.memset(score[0:CHUNK, mask_slot(t), N_META + n - CHUNK:N_META + n], FAR).then_inc(mask_ready, 1)
            for j, (_, tiles, n, dst, col) in enumerate(K_GROUPS):
                dve.wait_ge(k_hi_done, j + 1)
                dve.tensor_tensor(dst[:, 1, col:col + tiles * n], ps[:, 4, 0:tiles * n],
                                  dst[:, 0, col:col + tiles * n].bitcast(F32), ALU.subtract).then_inc(k_lo_done, 1)
            steps = [0, 0]

            def ready(i):
                t = INDEX_TILES[i]
                n, r, slot = keys_seen(t), tile_rows(t), mask_slot(i + 2)
                work = score[:r, slot, N_META:N_META + n]
                if i == 0:
                    dve.wait_ge(wi_copied, TILES)
                    for h in range(IDX_HEADS):
                        dve.wait_ge(rel_done, h + 1)
                        if h == 0:
                            dve.tensor_scalar(work, rel[:r, h % 2, 0:n], w_idx[:r, t, h:h + 1], None, ALU.mult).then_inc(added, 1)
                        else:
                            dve.wait_ge(added, h)
                            dve.scalar_tensor_tensor(out=work, in0=rel[:r, h % 2, 0:n], scalar=w_idx[:r, t, h:h + 1], in1=work,
                                                     op0=ALU.mult, op1=ALU.add).then_inc(added, 1)
                dve.wait_ge(added, IDX_HEADS * (i + 1))
                if t < SAMPLE_TILE:
                    dve.memset(score[0:CHUNK, slot, N_META + n - CHUNK:N_META + n], UNSEEN).then_inc(select_step[i % 2], 1)
                    steps[i % 2] += 1
                return work

            def finish(i, work):
                t = INDEX_TILES[i]
                n, r = keys_seen(t), tile_rows(t)
                dve.wait_ge(select_step[i % 2], steps[i % 2])
                dve.tensor_scalar(work, work, TAKEN, FAR, ALU.not_equal, ALU.mult).then_inc(select_step[i % 2], 1)
                steps[i % 2] += 1
                dve.wait_ge(select_step[i % 2], steps[i % 2])
                c0 = N_PROMPT - t * P
                dve.tensor_tensor(work, work, dist[:r, c0:c0 + n], ALU.max).then_inc(mask_ready, 1)

            ROUNDS = TOPK // 8
            first = [0, ROUNDS, ROUNDS + 12]
            while len(first) < len(INDEX_TILES):
                first.append(first[-2] + ROUNDS)
            works = {}
            for at in range(first[-1] + ROUNDS):
                live = [i for i in range(len(INDEX_TILES)) if first[i] <= at < first[i] + ROUNDS]
                for i in live:
                    if at == first[i]:
                        works[i] = ready(i)
                for i in live:
                    if steps[i % 2]:
                        dve.wait_ge(select_step[i % 2], steps[i % 2])
                    dve.max(top8[:tile_rows(INDEX_TILES[i]), i % 2], works[i]).then_inc(select_step[i % 2], 1)
                    steps[i % 2] += 1
                for i in live:
                    dve.wait_ge(select_step[i % 2], steps[i % 2])
                    dve.match_replace(works[i], top8[:tile_rows(INDEX_TILES[i]), i % 2], works[i], TAKEN)\
                       .then_inc(select_step[i % 2], 1)
                    steps[i % 2] += 1
                for i in live:
                    if at == first[i] + ROUNDS - 1:
                        finish(i, works[i])
            set_loaded(dve, len(sets) - 1)
            for s in range(len(sets)):
                if sets[s][3]:
                    dve.memset(sets[s][1][0:HD, 1 + sets[s][2], :].bitcast(F32), 0.0)
            da, da0, sinks = kv["dist_a"], kv["dist_a0"], kv["sinks"]
            dve.wait_ge(band_iota, 1)
            dve.scalar_tensor_tensor(out=da[:, N_META:], in0=da[:, N_META:], scalar=-1.0, in1=da[:, N_META:],
                                     op0=ALU.mult, op1=ALU.max).then_inc(band_step, 1)
            dve.memset(da[:, 0:N_META], 0.0).then_inc(band_step, 1)
            dve.memset(da0[:, 0:N_META], 0.0).then_inc(band_step, 1)
            dve.wait_ge(band_step, 3)
            dve.memset(da[0:CHUNK, N_META + 3 * CHUNK:N_META + 4 * CHUNK], FAR).then_inc(band_step, 1)
            dve.memset(da[CHUNK:P, N_META:N_META + CHUNK], FAR).then_inc(band_step, 1)
            dve.wait_ge(sinks_loaded, 16)
            for h in range(HEADS):
                dve.tensor_scalar(kv["sinks_scaled"][:, h:h + 1], sinks[:, h:h + 1], 1.0 / slope(h), None, ALU.mult)
            dve.wait_ge(band_step, 5)
            dve.tensor_copy(da0[:, N_META:], da[:, N_META + P:])

        @block.tensor
        def _(pe):
            def group(ch, g):
                kind = CHUNKS[ch][0]
                f, t0, n = groups_of(ch)[g]
                u = GROUP_BASE[ch] + g
                if u >= BANKS:
                    pe.wait_ge(group_out, u - BANKS + 1)
                for k in range(KT):
                    x_hi, x_lo = xT_hi[:, k, t0:t0 + n], xT_lo[:, k, t0:t0 + n]
                    if kind == FEATURE_MAJOR:
                        wh, wl = w_hi[:, ch % 2, k, f * P:(f + 1) * P], w_lo[:, ch % 2, k, f * P:(f + 1) * P]
                        out, terms = ps[:, u % BANKS, 0:n], ((wh, x_hi), (wh, x_lo), (wl, x_hi))
                    else:
                        w = unit_cols(ch)
                        wh, wl = w_hi[:, ch % 2, k, 0:w], w_lo[:, ch % 2, k, 0:w]
                        out, terms = ps[:n, u % BANKS, 0:w], ((x_hi, wh), (x_hi, wl), (x_lo, wh))
                    for j, (a, b) in enumerate(terms):
                        last = pe.matmul(out, a, b, start=(k == 0 and j == 0), stop=(k == KT - 1 and j == 2))
                last.then_inc(group_done, 1)

            def turn_keys(j):
                first, tiles, n, _, _ = K_GROUPS[j]
                if j == 0:
                    pe.wait_ge(k_loaded, 16 * 6)
                if j >= 1:
                    pe.wait_ge(k_lo_done, j)
                for a in range(tiles):
                    last = pe.transpose(ps[:, 4, a * n:(a + 1) * n],
                                        k_raw[:n, first + a, :, :].rearrange("p u d -> p (u d)"), c["ident"][:n, :n])
                last.then_inc(k_turned, 1)

            def index_scores(i, h):
                t = INDEX_TILES[i]
                n, r = keys_seen(t), tile_rows(t)
                v = IDX_HEADS * i + h
                if h == 0:
                    pe.wait_ge(q_lo_done, i + 1)
                if i == 0 and h == 0:
                    pe.wait_ge(k_lo_done, len(K_GROUPS))
                if v >= 1:
                    pe.wait_ge(rel_done, v)
                keys = kp if t < SAMPLE_TILE else ks
                for n0 in range(0, n, 512):
                    n1 = min(n, n0 + 512)
                    for part in range(2):
                        last = pe.matmul(ps_idx[:r, n0:n1], q_st[:, h, 0:r], keys[:, part, n0:n1],
                                         start=(part == 0), stop=(part == 1))
                last.then_inc(idx_done, 1)

            for ch in range(N_CH):
                pe.wait_ge(w_lo_done, KT * (ch + 1))
                i = ch - INDEX_CHUNK
                for g in range(len(groups_of(ch))):
                    group(ch, g)
                    if ch == 1 and 1 <= g <= len(K_GROUPS):
                        turn_keys(g - 1)
                    if 0 <= i < len(INDEX_TILES):
                        for h in index_groups(i).get(g, []):
                            index_scores(i, h)
            pe.wait_ge(group_out, GROUP_BASE[N_CH])
            for j, (s, first, n, rows, _) in enumerate(GROUPS):
                if j >= 4:
                    pe.wait_ge(kt_copied, j - 3)
                for part, (keys, split) in enumerate(((raw["k_twice_hi"], kt_hi_done), (raw["k_twice_lo"], kt_lo_done))):
                    pe.wait_ge(split, j + 1)
                    for a in range(n):
                        src = keys[0:rows, SLOT_BASE[j] + a].rearrange("p t d -> p (t d)")
                        last = pe.transpose(ps[:, 2 * (j % 4) + part, a * rows:(a + 1) * rows],
                                            src.bitcast(F32) if part == 0 else src, c["ident"][0:rows, 0:rows])
                last.then_inc(kt_turned, 1)


def band_width(t):
    return P if t == 0 else (2 * P if t < SAMPLE_TILE else WINDOW + N_SAMPLE)


def key_columns(branch, t):
    return N_META + (band_width(t) if branch == 0 else keys_seen(t))


def key_tiles(branch, t):
    w = key_columns(branch, t)
    tiles = [(0, N_META, 0)]
    if branch == 0 and t == SAMPLE_TILE:
        return tiles + [(N_META, P, 1), (w - P, P, 2)]
    if branch == 0:
        return tiles + [(N_META + P * j, P, t + j + 1 - (t > 0)) for j in range(band_width(t) // P)]
    if t == SAMPLE_TILE:
        return tiles + [(N_META + P * j, P, j + 1) for j in range(8)] + [(w - P, P, 9)]
    return tiles + [(N_META + P * j, P, j + 1) for j in range(t + 1)]


KV_COPIES = 13


def operand_buffers(ctx, nc):
    sb = lambda n, s, d=F32: ctx.enter_context(nc.sbuf_tensor(n, s, d))
    T_KV = T_KI
    return {
        "p": sb("raw_p", [P, 8, T_KV]),
        "m": sb("raw_m", [N_META, T_KV]),
        "cm": sb("raw_cm", [N_META, T_KV]),
        "n": sb("raw_n", [P, T_KV]),
        "ca": sb("raw_ca", [P, 2, 2 * HD]),
        "cb": sb("raw_cb", [P, 2, 8, HD]),
        "k_twice_hi": sb("k_twice_hi", [P, 43, 2, HD], F32R),
        "k_twice_lo": sb("k_twice_lo", [P, 43, 2, HD]),
    }


def operand_sets(kv, raw):
    sets = []

    def add_set(k, v, tiles, k_col, v_col, cached=None):
        cols = (slice(k_col, k_col + HD), slice(v_col, v_col + HD))
        if cached is None:
            sets.append((k, v, tiles, None, [(raw["m"][:, q], raw["p"][:, :, q], None) for q in cols]))
        else:
            sets.append((k, v, tiles, N_SAMPLE, [(raw["cm"][:, q], cached[i], raw["n"][:, q]) for i, q in enumerate(cols)]))

    for g in range(2):
        add_set(kv["k_a_p"][:, g], kv["v_a_p"][:, g], 8, T_KA + HD * g, T_VA + HD * g)
    add_set(kv["k_b_p"][:], kv["v_b_p"][:], 8, T_KB, T_VB)
    for g in range(2):
        add_set(kv["k_a_s"][:, g], kv["v_a_s"][:, g], 1, T_KA + HD * g, T_VA + HD * g,
                [raw["ca"][:, i:i + 1, HD * g:HD * (g + 1)] for i in range(2)])
    add_set(kv["k_b_s"][:], kv["v_b_s"][:], 8, T_KB, T_VB, [raw["cb"][:, i] for i in range(2)])
    return sets


def key_groups(sets):
    out = []
    for s, (_, _, m, last, _) in enumerate(sets):
        out.append((s, 0, 1, N_META, 0))
        for j in range(0, m, 4):
            out.append((s, 1 + j, min(4, m - j), P, N_META + P * j))
        if last:
            out.append((s, 1 + m, 1, last, N_META + P * m))
    return out


def key_source(sets, group):
    s, first, n, rows, _ = group
    k_meta, k_tiles, k_new = sets[s][4][0]
    if first == 0:
        src = k_meta.unsqueeze(1)
    elif first <= sets[s][2]:
        src = k_tiles[:, first - 1:first - 1 + n]
    else:
        src = k_new[0:rows].unsqueeze(1)
    return src.unsqueeze(2).to_broadcast([rows, n, 2, HD])


def value_parts(sets, s):
    _, _, m, last, (_, (v_meta, v_tiles, v_new)) = sets[s]
    parts = [(slice(0, N_META), 0, 1, v_meta.unsqueeze(1)), (slice(0, P), 1, m, v_tiles)]
    if last:
        parts.append((slice(HD, P), 1 + m, 1, v_new[HD:P].unsqueeze(1)))
    return parts


KV_COPIES = 13


def attention(nc, top, c, ps, kv, q_scr, gate_scr, dist_scr, merged_scr, t_scr, caches, outs):
    with ExitStack() as ctx:
        sb = lambda n, s, d=F32: ctx.enter_context(nc.sbuf_tensor(n, s, d))
        sem = lambda n: top.enter_context(nc.semaphore(n))
        SECTIONS = [(t, branch) for t in range(TILES) for branch in range(2)]
        UNITS = len(SECTIONS) * HEADS
        STEPS = UNITS + 9
        MAX_W = N_META + N_QUERY
        q_raw = sb("q_raw3", [P, HEADS, P])
        q_st = sb("q_st3", [P, 2, HEADS, P], F32R)
        probs = sb("probs", [P, 3, MAX_W])
        pt_hi = sb("pt_hi", [P, 2, 10, 2, P], F32R)
        pt_lo = sb("pt_lo", [P, 2, 10, 2, P], F32R)
        dist_b = sb("dist_b", [P, 2, MAX_W])
        top_neg = sb("top_neg", [P, 2, HEADS])
        top_val = sb("top_val", [P, 2, 3])
        top_all = sb("top_all", [P, 3])
        sums = sb("sums", [P, 2, HEADS])
        sink_e = sb("sink_e", [P, 2, HEADS])
        inv = sb("inv", [P, 2, HEADS])
        out_t = sb("out_t", [P, 2, 2 * P])
        mixed = sb("mixed", [P, 2, D])
        gates = sb("gates", [P, 2 * D])
        merged = sb("merged", [P, D])
        T_BANK, PV_BANK, O_BANK = 3, 6, 7

        q_loaded, q_hi_done, q_lo_done = sem("p3_q_loaded"), sem("p3_q_hi_done"), sem("p3_q_lo_done")
        dist_loaded = [sem("p3_dist_loaded0"), sem("p3_dist_loaded1")]
        gates_loaded = sem("p3_gates_loaded")
        scored, topped, neg_ready, exped = sem("p3_scored"), sem("p3_topped"), sem("p3_neg_ready"), sem("p3_exped")
        turned, hi_done, lo_done = sem("p3_turned"), sem("p3_hi_done"), sem("p3_lo_done")
        valued, out_copied, folded = sem("p3_valued"), sem("p3_out_copied"), sem("p3_folded")
        sink_in, sink_done, sum_ready, inv_ready = sem("p3_sink_in"), sem("p3_sink_done"), sem("p3_sum_ready"), sem("p3_inv_ready")
        normed = sem("p3_normed")
        merge_step, merged_stored = sem("p3_merge_step"), sem("p3_merged_stored")

        def section(u):
            return SECTIONS[u // HEADS]

        def tiles_of(u):
            t, branch = section(u)
            return key_tiles(branch, t)

        def groups(u):
            n = len(tiles_of(u))
            return [(a, min(4, n - a)) for a in range(0, n, 4)]

        GROUPS = [0]
        for u in range(UNITS):
            GROUPS.append(GROUPS[-1] + len(groups(u)))

        def score_chunks(u):
            t, branch = section(u)
            w = key_columns(branch, t)
            n = -(-w // 512)
            size = -(-w // (2 * n)) * 2
            return [(i, min(w, i + size)) for i in range(0, w, size)]

        CHUNK_BASE = [0]
        for u in range(UNITS):
            CHUNK_BASE.append(CHUNK_BASE[-1] + len(score_chunks(u)))

        def keys(t, branch, h):
            if branch == 1:
                k = kv["k_b_p"] if t < SAMPLE_TILE else kv["k_b_s"]
                return [(k[:], 0, 0, key_columns(1, t))]
            g = h // 8
            if t == SAMPLE_TILE:
                return [(kv["k_a_s"][:, g], 0, 0, key_columns(0, t))]
            band0 = N_META + P * max(t - 1, 0)
            return [(kv["k_a_p"][:, g], 0, 0, N_META), (kv["k_a_p"][:, g], band0, N_META, band_width(t))]

        def values(t, branch, h):
            if branch == 1:
                return kv["v_b_p"][:] if t < SAMPLE_TILE else kv["v_b_s"][:]
            return (kv["v_a_p"] if t < SAMPLE_TILE else kv["v_a_s"])[:, h // 8]

        with nc.Block() as block:

            @block.sync
            def _(sp):
                def load_q(s):
                    t, branch = SECTIONS[s]
                    r = tile_rows(t)
                    if s >= 1:
                        sp.wait_ge(q_lo_done, s)
                    src = q_scr[branch * D:(branch + 1) * D, t * P:t * P + r].rearrange("(h d) n -> d h n", d=HD)
                    for half in range(2):
                        sp.dma_start(q_raw[half * HD:(half + 1) * HD, :, 0:r], src).then_inc(q_loaded, 16)

                def load_dist(t):
                    if t >= 2:
                        sp.wait_ge(topped, CHUNK_BASE[HEADS * 2 * (t - 1)])
                    r, w = tile_rows(t), key_columns(1, t)
                    sp.dma_start(dist_b[:r, t % 2, 0:w], dist_scr[t, 0:r, 0:w]).then_inc(dist_loaded[t % 2], 16)

                def load_gates(t):
                    r = tile_rows(t)
                    sp.dma_start(gates[:r, :], gate_scr[t * P:t * P + r, :]).then_inc(gates_loaded, 16)

                def store_merged(t):
                    r = tile_rows(t)
                    sp.wait_ge(merge_step, 3 * (t + 1))
                    sp.dma_start(merged_scr[t * P:t * P + r, :], merged[:r, :]).then_inc(merged_stored, 16)

                load_q(0)
                load_dist(0)
                load_gates(0)
                copy = lambda dst, src: sp.dma_start(dst, src).then_inc(kv["stored"], 16)
                tail = slice(N_PROMPT - WINDOW, N_PROMPT)
                flat = lambda a: a[0, 0].rearrange("n h d -> n (h d)")
                copy(flat(outs["k_a_prompt"]), t_scr[tail, T_KA:T_KA + 2 * HD])
                copy(flat(outs["v_a_prompt"]), t_scr[tail, T_VA:T_VA + 2 * HD])
                copy(flat(outs["k_b_prompt"]), t_scr[0:N_PROMPT, T_KB:T_KB + HD])
                copy(flat(outs["v_b_prompt"]), t_scr[0:N_PROMPT, T_VB:T_VB + HD])
                copy(outs["ki_b_prompt"][0, 0], t_scr[0:N_PROMPT, T_KI:T_KI + HD])
                copy(flat(outs["meta_prompt"]), t_scr[N_QUERY:N_TOK, 0:T_KI])
                copy(outs["k_a_sample"][0, 0, 0:WINDOW - N_SAMPLE], caches[0][0, 0, N_SAMPLE:WINDOW])
                copy(outs["v_a_sample"][0, 0, 0:WINDOW - N_SAMPLE], caches[1][0, 0, N_SAMPLE:WINDOW])
                copy(flat(outs["k_a_sample"])[WINDOW - N_SAMPLE:], t_scr[N_PROMPT:N_QUERY, T_KA:T_KA + 2 * HD])
                copy(flat(outs["v_a_sample"])[WINDOW - N_SAMPLE:], t_scr[N_PROMPT:N_QUERY, T_VA:T_VA + 2 * HD])
                copy(flat(outs["k_b_sample"]), t_scr[N_PROMPT:N_QUERY, T_KB:T_KB + HD])
                copy(flat(outs["v_b_sample"]), t_scr[N_PROMPT:N_QUERY, T_VB:T_VB + HD])
                copy(outs["ki_b_sample"][0, 0], t_scr[N_PROMPT:N_QUERY, T_KI:T_KI + HD])
                for s, (t, branch) in enumerate(SECTIONS):
                    if s + 1 < len(SECTIONS):
                        load_q(s + 1)
                    if branch == 0:
                        if t >= 1:
                            store_merged(t - 1)
                            load_gates(t)
                        if t + 1 < TILES:
                            load_dist(t + 1)
                store_merged(TILES - 1)
                sp.wait_ge(merged_stored, 16 * TILES)
                sp.wait_ge(kv["stored"], 16 * KV_COPIES)

            @block.gpsimd
            def _(pool):
                def queries_lo(s):
                    t, branch = SECTIONS[s]
                    r = tile_rows(t)
                    pool.wait_ge(q_hi_done, 4 * (s + 1))
                    st = q_st[HD:, branch, :, 0:r]
                    pool.tensor_tensor(st, q_raw[HD:, :, 0:r], st.bitcast(F32), ALU.subtract).then_inc(q_lo_done, 1)
                    pool.wait_ge(q_lo_done, s + 1)

                def merge(t):
                    r = tile_rows(t)
                    pool.wait_ge(normed, 4 * (t + 1))
                    pool.wait_ge(gates_loaded, 16 * (t + 1))
                    if t >= 1:
                        pool.wait_ge(merged_stored, 16 * t)
                    pool.tensor_tensor(merged[:r, :], mixed[:r, 0, :], gates[:r, 0:D], ALU.mult).then_inc(merge_step, 1)
                    pool.wait_ge(merge_step, 3 * t + 1)
                    pool.tensor_tensor(mixed[:r, 1, :], mixed[:r, 1, :], gates[:r, D:], ALU.mult).then_inc(merge_step, 1)
                    pool.wait_ge(merge_step, 3 * t + 2)
                    pool.tensor_tensor(merged[:r, :], merged[:r, :], mixed[:r, 1, :], ALU.add).then_inc(merge_step, 1)
                    pool.wait_ge(merge_step, 3 * t + 3)

                queries_lo(0)
                for s, (t, branch) in enumerate(SECTIONS):
                    if s + 1 < len(SECTIONS):
                        queries_lo(s + 1)
                    if branch == 0 and t >= 1:
                        merge(t - 1)
                merge(TILES - 1)

            @block.scalar
            def _(act):
                def queries_hi(s, quarter):
                    t, branch = SECTIONS[s]
                    r = tile_rows(t)
                    hs = slice(4 * quarter, 4 * quarter + 4)
                    act.wait_ge(q_loaded, 32 * (s + 1))
                    if s >= 2:
                        act.wait_ge(scored, CHUNK_BASE[HEADS * (s - 1)])
                    act.activation(q_st[:, branch, hs, 0:r], q_raw[:, hs, 0:r], ACT.Copy).then_inc(q_hi_done, 1)

                def split_hi(u):
                    t, branch = section(u)
                    r = tile_rows(t)
                    if u % 2 == 0 and u >= 4:
                        act.wait_ge(valued, u // 2 - 1)
                    for j, (a, n) in enumerate(groups(u)):
                        x = GROUPS[u] + j
                        act.wait_ge(turned, x + 1)
                        src = ps[:, T_BANK + x % 3, :].rearrange("p (k n) -> p k n", k=4)[:, 0:n, 0:r]
                        act.activation(pt_hi[:, (u // 2) % 2, a:a + n, u % 2, 0:r], src, ACT.Copy).then_inc(hi_done, 1)

                def exp(u):
                    t, branch = section(u)
                    r, w, h = tile_rows(t), key_columns(branch, t), u % HEADS
                    act.wait_ge(neg_ready, u + 1)
                    act.activation(probs[:r, u % 3, 0:w], probs[:r, u % 3, 0:w], ACT.Exp, bias=top_neg[:r, branch, h:h + 1],
                                   scale=slope(h), accum_out=sums[:r, branch, h:h + 1]).then_inc(exped, 1)

                def copy_out(p):
                    r = tile_rows(section(2 * p)[0])
                    act.wait_ge(valued, p + 1)
                    if p >= 2:
                        act.wait_ge(folded, p - 1)
                    act.activation(out_t[:, p % 2, 0:2 * r], ps[:, PV_BANK, 0:2 * r], ACT.Copy).then_inc(out_copied, 1)

                def sink_exp(half, done):
                    t, _ = section(8 * half)
                    r, hs = tile_rows(t), slice(8 * (half % 2), 8 * (half % 2) + 8)
                    act.wait_ge(sink_in, done + 1)
                    act.activation(sink_e[:r, 0, hs], sink_e[:r, 0, hs], ACT.Exp).then_inc(sink_done, 1)

                sinks = 0
                for quarter in range(4):
                    queries_hi(0, quarter)
                for u in range(STEPS):
                    if u >= 2 and u - 2 < UNITS:
                        split_hi(u - 2)
                    if u < UNITS:
                        exp(u)
                    if u >= 5 and u % 2 == 1 and (u - 5) // 2 < UNITS // 2:
                        copy_out((u - 5) // 2)
                    quarter = u % HEADS - (1 if u // HEADS % 2 == 0 else 5)
                    if 0 <= quarter < 4 and u // HEADS + 1 < len(SECTIONS):
                        queries_hi(u // HEADS + 1, quarter)
                    if u >= 8 and u % 8 == 0 and u <= UNITS and section(u - 8)[1] == 0:
                        sink_exp(u // 8 - 1, sinks)
                        sinks += 1

            @block.vector
            def _(dve):
                def subtract_distance(u):
                    t, branch = section(u)
                    r, w, h = tile_rows(t), key_columns(branch, t), u % HEADS
                    if branch == 1 and h == 0:
                        dve.wait_ge(dist_loaded[t % 2], 16 * (t // 2 + 1))
                    if u >= 3:
                        dve.wait_ge(turned, GROUPS[u - 2])
                    if branch == 1:
                        dist, start = dist_b[:r, t % 2, :], UNSEEN
                    else:
                        dist = (kv["dist_a0"] if t == 0 else kv["dist_a"])[:r, :]
                        start = kv["sinks_scaled"][:r, h:h + 1]
                    chunks = score_chunks(u)
                    for j, (c0, c1) in enumerate(chunks):
                        x = CHUNK_BASE[u] + j
                        dve.wait_ge(scored, x + 1)
                        dve.tensor_tensor_reduce(probs[:r, u % 3, c0:c1], ps[:r, x % 3, 0:c1 - c0], dist[:, c0:c1], 1.0, start,
                                                 ALU.subtract, ALU.max, top_val[:r, u % 2, j:j + 1]).then_inc(topped, 1)
                    dve.wait_ge(topped, CHUNK_BASE[u + 1])
                    neg = top_neg[:r, branch, h:h + 1]
                    if len(chunks) == 1:
                        dve.tensor_scalar(neg, top_val[:r, u % 2, 0:1], -slope(h), None, ALU.mult).then_inc(neg_ready, 1)
                    else:
                        n = len(chunks)
                        dve.tensor_scalar(top_all[:r, 0:n], top_val[:r, u % 2, 0:n], -slope(h), None, ALU.mult, ALU.min,
                                          accum_out=neg).then_inc(neg_ready, 1)

                def split_lo(u):
                    t, branch = section(u)
                    r = tile_rows(t)
                    for j, (a, n) in enumerate(groups(u)):
                        x = GROUPS[u] + j
                        dve.wait_ge(hi_done, x + 1)
                        src = ps[:, T_BANK + x % 3, :].rearrange("p (k n) -> p k n", k=4)[:, 0:n, 0:r]
                        at = (slice(None), (u // 2) % 2, slice(a, a + n), u % 2, slice(0, r))
                        dve.tensor_tensor(pt_lo[at], src, pt_hi[at].bitcast(F32), ALU.subtract).then_inc(lo_done, 1)

                def sink_argument(half):
                    t, _ = section(8 * half)
                    r, hs = tile_rows(t), slice(8 * (half % 2), 8 * (half % 2) + 8)
                    dve.wait_ge(neg_ready, 8 * half + 8)
                    dve.tensor_tensor(sink_e[:r, 0, hs], kv["sinks"][:r, hs], top_neg[:r, 0, hs], ALU.add).then_inc(sink_in, 1)

                def invert(half, sinks):
                    t, branch = section(8 * half)
                    r, hs = tile_rows(t), slice(8 * (half % 2), 8 * (half % 2) + 8)
                    dve.wait_ge(exped, 8 * half + 8)
                    if branch == 0:
                        dve.wait_ge(sink_done, sinks)
                        dve.tensor_tensor(sums[:r, 0, hs], sums[:r, 0, hs], sink_e[:r, 0, hs], ALU.add).then_inc(sum_ready, 1)
                        dve.wait_ge(sum_ready, sinks)
                    dve.reciprocal(inv[:r, branch, hs], sums[:r, branch, hs]).then_inc(inv_ready, 1)

                def normalise(half):
                    t, branch = section(8 * half)
                    r, hs = tile_rows(t), slice(8 * (half % 2), 8 * (half % 2) + 8)
                    dve.wait_ge(folded, 4 * half + 4)
                    dve.wait_ge(inv_ready, half + 1)
                    if t >= 1:
                        dve.wait_ge(merge_step, 3 * t)
                    out = mixed[:r, branch, 512 * (half % 2):512 * (half % 2) + 512].rearrange("p (h d) -> p h d", d=HD)
                    src = ps[:r, O_BANK, :].rearrange("p (h d) -> p h d", d=HD)
                    scale = inv[:r, branch, hs].unsqueeze(2).to_broadcast([r, 8, HD])
                    dve.tensor_tensor(out, src, scale, ALU.mult).then_inc(normed, 1)

                sinks = 0
                for u in range(STEPS):
                    if u < UNITS:
                        subtract_distance(u)
                    if u >= 14 and u % 8 == 6 and (u - 14) // 8 < UNITS // 8:
                        normalise((u - 14) // 8)
                    if u >= 2 and u - 2 < UNITS:
                        split_lo(u - 2)
                    if u >= 8 and u % 8 == 0 and u <= UNITS and section(u - 8)[1] == 0:
                        sink_argument(u // 8 - 1)
                        sinks += 1
                    if u >= 8 and u % 8 == 2 and (u - 10) // 8 < UNITS // 8:
                        invert((u - 10) // 8, sinks)


            @block.tensor
            def _(pe):
                def score(u):
                    t, branch = section(u)
                    r, h, s = tile_rows(t), u % HEADS, u // HEADS
                    if h == 0:
                        pe.wait_ge(q_lo_done, s + 1)
                    for j, (c0, c1) in enumerate(score_chunks(u)):
                        x = CHUNK_BASE[u] + j
                        if x >= 3:
                            pe.wait_ge(topped, x - 2)
                        for k, k0, at, n in keys(t, branch, h):
                            a, b = max(at, c0), min(at + n, c1)
                            if a >= b:
                                continue
                            for part in range(2):
                                last = pe.matmul(ps[:r, x % 3, a - c0:b - c0], q_st[:, branch, h, 0:r],
                                                 k[:, part, k0 + a - at:k0 + b - at], start=(part == 0), stop=(part == 1))
                        last.then_inc(scored, 1)

                def turn(u):
                    t, branch = section(u)
                    r, tiles = tile_rows(t), tiles_of(u)
                    pe.wait_ge(exped, u + 1)
                    for j, (a, n) in enumerate(groups(u)):
                        x = GROUPS[u] + j
                        if x >= 3:
                            pe.wait_ge(lo_done, x - 2)
                        for b in range(n):
                            col = tiles[a + b][0]
                            last = pe.transpose(ps[:, T_BANK + x % 3, b * P:b * P + r], probs[:r, u % 3, col:col + P],
                                                c["ident"][:r, :r])
                        last.then_inc(turned, 1)

                def weigh_values(p, second):
                    u = 2 * p
                    t, branch = section(u)
                    r, tiles = tile_rows(t), tiles_of(u)
                    cut = len(tiles) // 2 if branch == 1 else 0
                    if second == 0 and cut == 0:
                        return
                    if second == 0 or cut == 0:
                        pe.wait_ge(lo_done, GROUPS[u + 2])
                        if p >= 1:
                            pe.wait_ge(out_copied, p)
                    v = values(t, branch, u % HEADS)
                    for j, (_, rows, slot) in enumerate(tiles):
                        if (j >= cut) != (second == 1):
                            continue
                        for part, pt in enumerate((pt_hi, pt_lo)):
                            last = pe.matmul(ps[:, PV_BANK, 0:2 * r], v[0:rows, slot, :], pt[0:rows, p % 2, j, :, 0:r],
                                             start=(j == 0 and part == 0), stop=(j == len(tiles) - 1 and part == 1))
                    if second == 1:
                        last.then_inc(valued, 1)

                def fold(p):
                    t, _ = section(2 * p)
                    r, half = tile_rows(t), p // 4
                    pe.wait_ge(out_copied, p + 1)
                    if p % 4 == 0 and half >= 1:
                        pe.wait_ge(normed, half)
                    for b in range(2):
                        h = (2 * p + b) % 8
                        last = pe.matmul(ps[:r, O_BANK, h * HD:(h + 1) * HD], out_t[:, p % 2, b * r:(b + 1) * r],
                                         c["fold"][:], start=True, stop=True)
                    last.then_inc(folded, 1)

                score(0)
                for u in range(STEPS):
                    if u >= 2 and u - 2 < UNITS:
                        turn(u - 2)
                    if u + 1 < UNITS:
                        score(u + 1)
                    if u >= 7 and u % 2 == 1 and (u - 7) // 2 < UNITS // 2:
                        fold((u - 7) // 2)
                    if u >= 4 and (u - 4) // 2 < UNITS // 2:
                        weigh_values((u - 4) // 2, u % 2)


def attention_buffers(ctx, top, nc):
    sb = lambda n, s, d=F32: ctx.enter_context(nc.sbuf_tensor(n, s, d))
    return {
        "stored": top.enter_context(nc.semaphore("p3_kv_stored")),
        "k_b_p": sb("k_b_p", [P, 2, N_META + N_PROMPT], F32R), "k_b_s": sb("k_b_s", [P, 2, N_META + N_QUERY], F32R),
        "k_a_p": sb("k_a_p", [P, 2, 2, N_META + N_PROMPT], F32R),
        "k_a_s": sb("k_a_s", [P, 2, 2, N_META + WINDOW + N_SAMPLE], F32R),
        "v_b_p": sb("v_b_p", [P, 9, P], F32R), "v_b_s": sb("v_b_s", [P, 10, P], F32R),
        "v_a_p": sb("v_a_p", [P, 2, 9, P], F32R), "v_a_s": sb("v_a_s", [P, 2, 3, P], F32R),
        "dist_a": sb("dist_a", [P, N_META + 2 * P]), "dist_a0": sb("dist_a0", [P, N_META + P]),
        "sinks": sb("sinks", [P, HEADS]), "sinks_scaled": sb("sinks_scaled", [P, HEADS]),
    }


def output_mix(nc, top, c, x2T, ps, merged_scr, w_o, x_prompt, x_sample, g_post_mix, g_pre_mlp, x1_scr):
    x2T_hi, x2T_lo = x2T
    RAW = 4
    UNITS = 2 * KT
    with ExitStack() as ctx:
        sb = lambda n, s, d=F32: ctx.enter_context(nc.sbuf_tensor(n, s, d))
        sem = lambda n: top.enter_context(nc.semaphore(n))
        w_raw = sb("wo_raw", [P, RAW, 512])
        w_hi = sb("wo_hi", [P, KT, D], F32R)
        w_lo = sb("wo_lo", [P, KT, D], F32R)
        m_in = sb("m_in", [P, 2, D])
        mT_hi = sb("mT_hi", [P, 2, KT, P], F32R)
        mT_lo = sb("mT_lo", [P, 2, KT, P], F32R)
        x_in = sb("x_in4", [P, 2, D])
        x1 = sb("x1", [P, 2, D])
        x_norm = sb("x_norm4", [P, 2, D])
        squares = sb("squares4", [P, D])
        g_post = sb("g_post", [P, D])
        g_pre = sb("g_pre", [P, D])
        col = {n: sb("p4_" + n, [P, 2 * TILES]) for n in ("sum_sq", "std", "mean_sq", "rstd_0", "rstd", "newton")}

        w_loaded = [sem(f"p4_w_loaded{i}") for i in range(RAW)]
        w_hi_done, w_lo_done = sem("p4_w_hi_done"), sem("p4_w_lo_done")
        gains_loaded = sem("p4_gains_loaded")
        m_loaded = [sem("p4_m_loaded0"), sem("p4_m_loaded1")]
        x_loaded = [sem("p4_x_loaded0"), sem("p4_x_loaded1")]
        m_turned, m_hi_done, m_lo_done = sem("p4_m_turned"), sem("p4_m_hi_done"), sem("p4_m_lo_done")
        product_done = sem("p4_product_done")
        squared, std_ready, rstd_ready, refined = sem("p4_squared"), sem("p4_std_ready"), sem("p4_rstd_ready"), sem("p4_refined")
        scaled, x1_ready = sem("p4_scaled"), sem("p4_x1_ready")
        x1_stored = [sem("p4_x1_stored0"), sem("p4_x1_stored1")]
        normed, x_turned, x_hi_done, x_lo_done = sem("p4_normed"), sem("p4_x_turned"), sem("p4_x_hi_done"), sem("p4_x_lo_done")

        def toks(t):
            return slice(t * P, t * P + tile_rows(t))

        def product(t):
            return ps[:, 4 + 2 * (t % 2):6 + 2 * (t % 2), :].rearrange("p b n -> p (b n)")[:tile_rows(t)]

        def four(bank, t):
            return ps[:, bank, :].rearrange("p (k n) -> p k n", k=4)[:, :, 0:tile_rows(t)]

        with nc.Block() as block:

            @block.sync
            def _(sp):
                def load_merged(t):
                    if t >= 2:
                        sp.wait_ge(m_turned, 2 * t - 2)
                    sp.dma_start(m_in[:tile_rows(t), t % 2, :], merged_scr[toks(t), :]).then_inc(m_loaded[t % 2], 16)

                def load_x(t):
                    r = tile_rows(t)
                    if t >= 2:
                        sp.wait_ge(x1_ready, t - 1)
                    src = x_prompt[0, toks(t), :] if t < SAMPLE_TILE else x_sample[0]
                    sp.dma_start(x_in[:r, t % 2, :], src).then_inc(x_loaded[t % 2], 16)

                load_merged(0)
                load_merged(1)
                load_x(0)
                load_x(1)
                sp.dma_start(g_post[:], g_post_mix[0:1, :].to_broadcast([P, D])).then_inc(gains_loaded, 16)
                sp.dma_start(g_pre[:], g_pre_mlp[0:1, :].to_broadcast([P, D])).then_inc(gains_loaded, 16)
                for t in range(TILES):
                    if t + 2 < TILES:
                        load_merged(t + 2)
                    sp.wait_ge(x1_ready, t + 1)
                    sp.dma_start(x1_scr[toks(t), :], x1[:tile_rows(t), t % 2, :]).then_inc(x1_stored[t % 2], 16)
                    if t + 2 < TILES:
                        load_x(t + 2)
                sp.wait_ge(x1_stored[0], 16 * 5)
                sp.wait_ge(x1_stored[1], 16 * 4)

            @block.gpsimd
            def _(pool):
                for n in range(UNITS):
                    k, half = n % KT, n // KT
                    at = (slice(None), k, slice(512 * half, 512 * half + 512))
                    pool.wait_ge(w_hi_done, n + 1)
                    pool.tensor_tensor(w_lo[at], w_raw[:, n % RAW, :], w_hi[at].bitcast(F32), ALU.subtract).then_inc(w_lo_done, 1)
                    pool.wait_ge(w_lo_done, n + 1)
                for t in range(TILES):
                    r = tile_rows(t)
                    pool.wait_ge(scaled, t + 1)
                    pool.wait_ge(x_loaded[t % 2], 16 * (t // 2 + 1))
                    pool.tensor_tensor(x1[:r, t % 2, :], x1[:r, t % 2, :], x_in[:r, t % 2, :], ALU.add).then_inc(x1_ready, 1)
                    pool.wait_ge(x1_ready, t + 1)

            @block.scalar
            def _(act):
                def load_w(n):
                    k, half = n % KT, n // KT
                    if n >= RAW:
                        act.wait_ge(w_lo_done, n - RAW + 1)
                    act.dma_start(w_raw[:, n % RAW, :], w_o[0, k * P:(k + 1) * P, 512 * half:512 * half + 512])\
                       .then_inc(w_loaded[n % RAW], 16)

                def norm_statistics(t, which, src):
                    j, r = 2 * t + which, tile_rows(t)
                    act.activation(squares[:r], src, ACT.Square, accum_out=col["sum_sq"][:r, j:j + 1]).then_inc(squared, 1)
                    act.wait_ge(squared, j + 1)
                    act.activation(col["std"][:r, j:j + 1], col["sum_sq"][:r, j:j + 1], ACT.Sqrt, bias=c["eps"][:r, :],
                                   scale=1.0 / D).then_inc(std_ready, 1)

                def merged_hi(t):
                    for g in range(2):
                        act.wait_ge(m_turned, 2 * t + g + 1)
                        if t >= 2:
                            act.wait_ge(product_done, t - 1)
                        act.activation(mT_hi[:, t % 2, 4 * g:4 * g + 4, 0:tile_rows(t)], four(g, t), ACT.Copy).then_inc(m_hi_done, 1)

                def normed_hi(t):
                    for g in range(2):
                        act.wait_ge(x_turned, 2 * t + g + 1)
                        act.activation(x2T_hi[:, 4 * g:4 * g + 4, toks(t)], four(2 + g, t), ACT.Copy).then_inc(x_hi_done, 1)

                for n in range(RAW):
                    load_w(n)
                merged_hi(0)
                for n in range(UNITS):
                    act.wait_ge(w_loaded[n % RAW], 16 * (n // RAW + 1))
                    k, half = n % KT, n // KT
                    act.activation(w_hi[:, k, 512 * half:512 * half + 512], w_raw[:, n % RAW, :], ACT.Copy).then_inc(w_hi_done, 1)
                    if 1 <= n and n + RAW - 1 < UNITS:
                        load_w(n + RAW - 1)
                for t in range(1, TILES + 2):
                    if t < TILES:
                        merged_hi(t)
                    if t - 1 < TILES:
                        act.wait_ge(product_done, t)
                        norm_statistics(t - 1, 0, product(t - 1))
                    if t - 1 < TILES:
                        act.wait_ge(x1_ready, t)
                        norm_statistics(t - 1, 1, x1[:tile_rows(t - 1), (t - 1) % 2, :])
                    if 0 <= t - 2:
                        normed_hi(t - 2)

            @block.vector
            def _(dve):
                def rstd(t, which):
                    j, r = 2 * t + which, tile_rows(t)
                    one = lambda n: col[n][:r, j:j + 1]
                    dve.wait_ge(std_ready, j + 1)
                    dve.reciprocal(one("rstd_0"), one("std")).then_inc(rstd_ready, 1)
                    dve.tensor_scalar(one("mean_sq"), one("sum_sq"), 1.0 / D, EPS, ALU.mult, ALU.add).then_inc(rstd_ready, 1)
                    dve.wait_ge(rstd_ready, 2 * j + 2)
                    refine_rstd(dve, refined, 3 * j, one("rstd"), one("rstd_0"), one("mean_sq"), one("newton"))
                    return one("rstd")

                def merged_lo(t):
                    for g in range(2):
                        dve.wait_ge(m_hi_done, 2 * t + g + 1)
                        at = (slice(None), t % 2, slice(4 * g, 4 * g + 4), slice(0, tile_rows(t)))
                        dve.tensor_tensor(mT_lo[at], four(g, t), mT_hi[at].bitcast(F32), ALU.subtract).then_inc(m_lo_done, 1)

                def normed_lo(t):
                    for g in range(2):
                        dve.wait_ge(x_hi_done, 2 * t + g + 1)
                        at = (slice(None), slice(4 * g, 4 * g + 4), toks(t))
                        dve.tensor_tensor(x2T_lo[at], four(2 + g, t), x2T_hi[at].bitcast(F32), ALU.subtract).then_inc(x_lo_done, 1)

                def scale_product(t):
                    r = tile_rows(t)
                    s = rstd(t, 0)
                    if t >= 2:
                        dve.wait_ge(x1_stored[t % 2], 16 * (t // 2))
                        dve.wait_ge(normed, t - 1)
                    dve.scalar_tensor_tensor(out=x1[:r, t % 2, :], in0=product(t), scalar=s, in1=g_post[:r, :],
                                             op0=ALU.mult, op1=ALU.mult).then_inc(scaled, 1)

                def norm_x1(t):
                    r = tile_rows(t)
                    s = rstd(t, 1)
                    if t >= 2:
                        dve.wait_ge(x_turned, 2 * t - 2)
                    dve.scalar_tensor_tensor(out=x_norm[:r, t % 2, :], in0=x1[:r, t % 2, :], scalar=s, in1=g_pre[:r, :],
                                             op0=ALU.mult, op1=ALU.mult).then_inc(normed, 1)

                merged_lo(0)
                dve.wait_ge(gains_loaded, 32)
                for t in range(1, TILES + 2):
                    if t < TILES:
                        merged_lo(t)
                    if t - 1 < TILES:
                        scale_product(t - 1)
                    if t - 1 < TILES:
                        norm_x1(t - 1)
                    if 0 <= t - 2:
                        normed_lo(t - 2)

            @block.tensor
            def _(pe):
                def turn_merged(t):
                    pe.wait_ge(m_loaded[t % 2], 16 * (t // 2 + 1))
                    for g in range(2):
                        if t >= 1:
                            pe.wait_ge(m_lo_done, 2 * t + g - 1)
                        for k in range(4):
                            last = pe.transpose(ps[:, g, k * P:k * P + tile_rows(t)],
                                                m_in[:tile_rows(t), t % 2, (4 * g + k) * P:(4 * g + k + 1) * P],
                                                c["ident"][:tile_rows(t), :tile_rows(t)])
                        last.then_inc(m_turned, 1)

                def turn_normed(t):
                    pe.wait_ge(normed, t + 1)
                    for g in range(2):
                        if t >= 1:
                            pe.wait_ge(x_lo_done, 2 * t + g - 1)
                        for k in range(4):
                            last = pe.transpose(ps[:, 2 + g, k * P:k * P + tile_rows(t)],
                                                x_norm[:tile_rows(t), t % 2, (4 * g + k) * P:(4 * g + k + 1) * P],
                                                c["ident"][:tile_rows(t), :tile_rows(t)])
                        last.then_inc(x_turned, 1)

                def multiply(t):
                    r = tile_rows(t)
                    pe.wait_ge(m_lo_done, 2 * t + 2)
                    if t >= 2:
                        pe.wait_ge(scaled, t - 1)
                    for half in range(2):
                        if t == 0:
                            pe.wait_ge(w_lo_done, KT * (half + 1))
                        out = product(t)[:, 512 * half:512 * half + 512]
                        cols = slice(512 * half, 512 * half + 512)
                        for k in range(KT):
                            m_hi, m_lo = mT_hi[:, t % 2, k, 0:r], mT_lo[:, t % 2, k, 0:r]
                            for j, (a, b) in enumerate(((m_hi, w_hi), (m_hi, w_lo), (m_lo, w_hi))):
                                last = pe.matmul(out, a, b[:, k, cols], start=(k == 0 and j == 0), stop=(k == KT - 1 and j == 2))
                    last.then_inc(product_done, 1)

                turn_merged(0)
                for t in range(1, TILES + 2):
                    if t < TILES:
                        turn_merged(t)
                    if t - 1 < TILES:
                        multiply(t - 1)
                    if 0 <= t - 2:
                        turn_normed(t - 2)


def mlp(nc, top, c, x2T, ps, w_up, w_down, g_post_mlp, x1_scr, y_prompt, y_sample):
    x2T_hi, x2T_lo = x2T
    CH = 256
    FT = CH // P
    N_CH = D_FF // CH
    UP_UNITS, DOWN_UNITS = 4, 4
    UP_GROUPS = [(f, t0, n) for f in range(FT) for t0, n in TOK_BLOCKS]
    DOWN_GROUPS = [(t, half) for t in range(TILES) for half in range(2)]
    N_UP, N_DOWN = len(UP_GROUPS), len(DOWN_GROUPS)
    UP_BANKS = 2
    DOWN_BANKS = 6
    with ExitStack() as ctx:
        sb = lambda n, s, d=F32: ctx.enter_context(nc.sbuf_tensor(n, s, d))
        sem = lambda n: top.enter_context(nc.semaphore(n))
        up_raw = sb("up_raw", [P, UP_UNITS, 2, CH])
        down_raw = sb("down_raw", [P, DOWN_UNITS, 512])
        up_hi = sb("up_hi", [P, KT, CH], F32R)
        up_lo = sb("up_lo", [P, KT, CH], F32R)
        down_hi = sb("down_hi", [P, FT, D], F32R)
        down_lo = sb("down_lo", [P, FT, D], F32R)
        hidden = sb("hidden", [P, 2, 364])
        hid_hi = sb("hid_hi", [P, FT, N_QUERY], F32R)
        hid_lo = sb("hid_lo", [P, FT, N_QUERY], F32R)
        total = sb("total", [P, TILES, D])
        x1_in = sb("x1_in", [P, 2, D])
        squares = sb("squares5", [P, D])
        gain = sb("gain5", [P, D])
        col = {n: sb("p5_" + n, [P, TILES]) for n in ("sum_sq", "std", "mean_sq", "rstd_0", "rstd", "newton")}

        up_loaded = [sem(f"p5_up_loaded{i}") for i in range(UP_UNITS)]
        down_loaded = [sem(f"p5_down_loaded{i}") for i in range(DOWN_UNITS)]
        up_hi_done, up_lo_done = sem("p5_up_hi_done"), sem("p5_up_lo_done")
        down_hi_done, down_lo_done = sem("p5_down_hi_done"), sem("p5_down_lo_done")
        up_done, relu_done, squared_done, hid_hi_done, hid_lo_done = (sem("p5_" + n) for n in ("up_done", "relu_done", "squared_done", "hid_hi_done", "hid_lo_done"))
        down_done, added, cleared = sem("p5_down_done"), sem("p5_added"), sem("p5_cleared")
        gain_loaded = sem("p5_gain_loaded")
        x1_loaded = [sem("p5_x1_loaded0"), sem("p5_x1_loaded1")]
        sq_done, std_ready, rstd_ready, refined = sem("p5_sq_done"), sem("p5_std_ready"), sem("p5_rstd_ready"), sem("p5_refined")
        scaled, y_ready, y_stored = sem("p5_scaled"), sem("p5_y_ready"), sem("p5_y_stored")

        def toks(t):
            return slice(t * P, t * P + tile_rows(t))

        up_src = w_up[0].rearrange("(u k p) f -> u p k f", k=2, p=P)

        with nc.Block() as block:

            def store_y(sp, t):
                r = tile_rows(t)
                sp.wait_ge(y_ready, t + 1)
                dst = y_prompt[0, toks(t), :] if t < SAMPLE_TILE else y_sample[0]
                sp.dma_start(dst, total[:r, t, :]).then_inc(y_stored, 16)

            @block.sync
            def _(sp):
                def load_up(j, first):
                    for u in range(UP_UNITS):
                        if not first:
                            sp.wait_ge(up_lo_done, (j - 1) * KT + (2 * u + 2))
                        sp.dma_start(up_raw[:, u], up_src[u][:, :, bass.ds(j * CH, CH)]).then_inc(up_loaded[u], 16)

                def load_down(j, first):
                    for u in range(DOWN_UNITS):
                        f, half = divmod(u, 2)
                        if not first:
                            sp.wait_ge(down_lo_done, (j - 1) * DOWN_UNITS + (u + 1))
                        src = w_down[0, bass.ds(j * CH + f * P, P), 512 * half:512 * half + 512]
                        sp.dma_start(down_raw[:, u, :], src).then_inc(down_loaded[u], 16)

                load_up(0, True)
                load_down(0, True)
                sp.dma_start(gain[:], g_post_mlp[0:1, :].to_broadcast([P, D])).then_inc(gain_loaded, 16)
                with sp.Fori(1, N_CH) as j:
                    load_up(j, False)
                    load_down(j, False)
                for t in range(TILES):
                    if t >= 2:
                        sp.wait_ge(y_ready, t - 1)
                    sp.dma_start(x1_in[:tile_rows(t), t % 2, :], x1_scr[toks(t), :]).then_inc(x1_loaded[t % 2], 16)
                    if t >= 1:
                        store_y(sp, t - 1)
                store_y(sp, TILES - 1)
                sp.wait_ge(y_stored, 16 * TILES)

            @block.gpsimd
            def _(pool):
                def split_up_lo(j):
                    for k in range(KT):
                        pool.wait_ge(up_hi_done, j * KT + (k + 1))
                        pool.tensor_tensor(up_lo[:, k, :], up_raw[:, k // 2, k % 2, :], up_hi[:, k, :].bitcast(F32),
                                           ALU.subtract).then_inc(up_lo_done, 1)

                def split_down_lo(j):
                    for u in range(DOWN_UNITS):
                        f, half = divmod(u, 2)
                        at = (slice(None), f, slice(512 * half, 512 * half + 512))
                        pool.wait_ge(down_hi_done, j * DOWN_UNITS + (u + 1))
                        pool.tensor_tensor(down_lo[at], down_raw[:, u, :], down_hi[at].bitcast(F32), ALU.subtract).then_inc(down_lo_done, 1)

                split_up_lo(0)
                with pool.Fori(0, N_CH - 1) as j:
                    split_down_lo(j)
                    split_up_lo(j + 1)
                split_down_lo(N_CH - 1)
                pool.wait_ge(down_lo_done, N_CH * DOWN_UNITS)
                for t in range(TILES):
                    r = tile_rows(t)
                    pool.wait_ge(scaled, t + 1)
                    pool.wait_ge(x1_loaded[t % 2], 16 * (t // 2 + 1))
                    pool.tensor_tensor(total[:r, t, :], total[:r, t, :], x1_in[:r, t % 2, :], ALU.add).then_inc(y_ready, 1)
                    pool.wait_ge(y_ready, t + 1)

            @block.scalar
            def _(act):
                def split_up_hi(j, first=False):
                    if not first:
                        act.wait_ge(up_done, j * N_UP)
                    for k in range(KT):
                        act.wait_ge(up_loaded[k // 2], (j + 1) * 16)
                        act.activation(up_hi[:, k, :], up_raw[:, k // 2, k % 2, :], ACT.Copy).then_inc(up_hi_done, 1)

                def chunk(j, first=False):
                    for g in range(N_UP + 1):
                        if g < DOWN_UNITS:
                            fd, half = divmod(g, 2)
                            act.wait_ge(down_done, j * N_DOWN)
                            act.wait_ge(down_loaded[g], (j + 1) * 16)
                            act.activation(down_hi[:, fd, 512 * half:512 * half + 512], down_raw[:, g, :], ACT.Copy)\
                               .then_inc(down_hi_done, 1)
                        if g < N_UP:
                            n = UP_GROUPS[g][2]
                            act.wait_ge(up_done, j * N_UP + (g + 1))
                            if g >= 2:
                                act.wait_ge(hid_lo_done, j * N_UP + (g - 1))
                            elif not first:
                                act.wait_ge(hid_lo_done, j * N_UP)
                            act.activation(hidden[:, g % 2, 0:n], ps[:, g % UP_BANKS, 0:n], ACT.Relu).then_inc(relu_done, 1)
                        if g >= 1:
                            f, t0, n = UP_GROUPS[g - 1]
                            act.wait_ge(squared_done, j * N_UP + g)
                            act.activation(hid_hi[:, f, t0:t0 + n], hidden[:, (g - 1) % 2, 0:n], ACT.Copy).then_inc(hid_hi_done, 1)

                split_up_hi(0, first=True)
                chunk(0, first=True)
                with act.Fori(1, N_CH) as j:
                    split_up_hi(j)
                    chunk(j)
                for t in range(TILES):
                    r = tile_rows(t)
                    act.wait_ge(added, (N_CH - 1) * N_DOWN + 2 * t + 2)
                    act.activation(squares[:r], total[:r, t, :], ACT.Square, accum_out=col["sum_sq"][:r, t:t + 1]).then_inc(sq_done, 1)
                    act.wait_ge(sq_done, t + 1)
                    act.activation(col["std"][:r, t:t + 1], col["sum_sq"][:r, t:t + 1], ACT.Sqrt, bias=c["eps"][:r, :],
                                   scale=1.0 / D).then_inc(std_ready, 1)

            @block.vector
            def _(dve):
                def square_hidden(j):
                    for g in range(N_UP + 1):
                        if g < N_UP:
                            h = hidden[:, g % 2, 0:UP_GROUPS[g][2]]
                            dve.wait_ge(relu_done, j * N_UP + (g + 1))
                            dve.tensor_tensor(h, h, h, ALU.mult).then_inc(squared_done, 1)
                        if g >= 1:
                            f, t0, n = UP_GROUPS[g - 1]
                            dve.wait_ge(hid_hi_done, j * N_UP + g)
                            dve.tensor_tensor(hid_lo[:, f, t0:t0 + n], hidden[:, (g - 1) % 2, 0:n],
                                              hid_hi[:, f, t0:t0 + n].bitcast(F32), ALU.subtract).then_inc(hid_lo_done, 1)

                def add_down(j, g):
                    t, half = DOWN_GROUPS[g]
                    r = tile_rows(t)
                    out = total[:r, t, 512 * half:512 * half + 512]
                    dve.wait_ge(down_done, j * N_DOWN + (g + 1))
                    dve.tensor_tensor(out, out, ps[:r, UP_BANKS + g % DOWN_BANKS, :], ALU.add).then_inc(added, 1)

                def scale_total(t):
                    r = tile_rows(t)
                    one = lambda n: col[n][:r, t:t + 1]
                    dve.wait_ge(std_ready, t + 1)
                    dve.reciprocal(one("rstd_0"), one("std")).then_inc(rstd_ready, 1)
                    dve.tensor_scalar(one("mean_sq"), one("sum_sq"), 1.0 / D, EPS, ALU.mult, ALU.add).then_inc(rstd_ready, 1)
                    dve.wait_ge(rstd_ready, 2 * t + 2)
                    refine_rstd(dve, refined, 3 * t, one("rstd"), one("rstd_0"), one("mean_sq"), one("newton"))
                    dve.scalar_tensor_tensor(out=total[:r, t, :], in0=total[:r, t, :], scalar=one("rstd"), in1=gain[:r, :],
                                             op0=ALU.mult, op1=ALU.mult).then_inc(scaled, 1)

                dve.memset(total[:], 0.0).then_inc(cleared, 1)
                dve.wait_ge(cleared, 1)
                with dve.Fori(0, N_CH - 1) as j:
                    dve.wait_ge(added, j * N_DOWN)
                    square_hidden(j)
                    for g in range(N_DOWN):
                        add_down(j, g)
                dve.wait_ge(added, (N_CH - 1) * N_DOWN)
                square_hidden(N_CH - 1)
                dve.wait_ge(gain_loaded, 16)
                for t in range(TILES):
                    add_down(N_CH - 1, 2 * t)
                    add_down(N_CH - 1, 2 * t + 1)
                    if t >= 2:
                        scale_total(t - 2)
                scale_total(TILES - 2)
                scale_total(TILES - 1)

            @block.tensor
            def _(pe):
                def chunk(j, first=False):
                    pe.wait_ge(up_lo_done, (j + 1) * KT)
                    for g, (f, t0, n) in enumerate(UP_GROUPS):
                        if g >= UP_BANKS:
                            pe.wait_ge(relu_done, j * N_UP + (g - UP_BANKS + 1))
                        elif not first:
                            pe.wait_ge(relu_done, j * N_UP - UP_BANKS + (g + 1))
                        fs = slice(f * P, (f + 1) * P)
                        for k in range(KT):
                            x_hi, x_lo = x2T_hi[:, k, t0:t0 + n], x2T_lo[:, k, t0:t0 + n]
                            for i, (a, b) in enumerate(((up_hi, x_hi), (up_hi, x_lo), (up_lo, x_hi))):
                                last = pe.matmul(ps[:, g % UP_BANKS, 0:n], a[:, k, fs], b, start=(k == 0 and i == 0),
                                                 stop=(k == KT - 1 and i == 2))
                        last.then_inc(up_done, 1)
                    pe.wait_ge(down_lo_done, (j + 1) * DOWN_UNITS)
                    for g, (t, half) in enumerate(DOWN_GROUPS):
                        r = tile_rows(t)
                        block_of = max(b for b, (t0, n) in enumerate(TOK_BLOCKS) if t0 < t * P + r)
                        if half == 0:
                            pe.wait_ge(hid_lo_done, j * N_UP + (len(TOK_BLOCKS) * (FT - 1) + block_of + 1))
                        if g >= DOWN_BANKS:
                            pe.wait_ge(added, j * N_DOWN + (g - DOWN_BANKS + 1))
                        elif not first:
                            pe.wait_ge(added, (j - 1) * N_DOWN + (N_DOWN - DOWN_BANKS + g + 1))
                        cols = slice(512 * half, 512 * half + 512)
                        for f in range(FT):
                            h_hi, h_lo = hid_hi[:, f, toks(t)], hid_lo[:, f, toks(t)]
                            for i, (a, b) in enumerate(((h_hi, down_hi), (h_hi, down_lo), (h_lo, down_hi))):
                                last = pe.matmul(ps[:r, UP_BANKS + g % DOWN_BANKS, :], a, b[:, f, cols],
                                                 start=(f == 0 and i == 0), stop=(f == FT - 1 and i == 2))
                        last.then_inc(down_done, 1)

                chunk(0, first=True)
                with pe.Fori(1, N_CH) as j:
                    chunk(j)


def streaming_step(nc, a, o):
    scratch = lambda name, shape: nc.dram_tensor(name, shape, F32).ap()
    t_scr = scratch("t_scr", (N_TOK, T_WIDTH))
    q_scr = scratch("q_scr", (2 * D + IDX_HEADS * HD, N_QUERY))
    gate_scr = scratch("gate_scr", (N_QUERY, 2 * D))
    dist_scr = scratch("dist_scr", (TILES, P, N_META + N_QUERY))
    merged_scr = scratch("merged_scr", (N_QUERY, D))
    x1_scr = scratch("x1_scr", (N_QUERY, D))
    caches = [a[n] for n in ("cache_k_a", "cache_v_a", "cache_k_b", "cache_v_b", "cache_meta")]
    with ExitStack() as top:
        c = constants(lambda n, s: top.enter_context(nc.sbuf_tensor(n, s, F32)))
        ps = top.enter_context(nc.psum_tensor("ps", [P, 8, 512], F32))
        with ExitStack() as mixers:
            sel = selection_buffers(mixers, nc)
            ctx = ExitStack()
            xT = [ctx.enter_context(nc.sbuf_tensor(n, [P, KT, N_TOK], F32R)) for n in ("xT_hi", "xT_lo")]
            input_norm(nc, top, c, xT, ps, a["x_prompt"], a["x_sample"], a["meta_tokens"], a["g_pre_mix"])
            b2 = projection_buffers(ctx, nc)
            ctx.close()
            kv = attention_buffers(mixers, top, nc)
            with ExitStack() as ctx:
                raw = operand_buffers(ctx, nc)
                projection(nc, top, c, xT, b2, sel, kv, raw, ps, a["w_in"], caches, a["cache_ki_b"], a["attn_sinks"],
                           t_scr, q_scr, gate_scr, dist_scr)
            attention(nc, top, c, ps, kv, q_scr, gate_scr, dist_scr, merged_scr, t_scr, caches, o)
        with ExitStack() as ctx:
            x2T = [ctx.enter_context(nc.sbuf_tensor(n, [P, KT, N_QUERY], F32R)) for n in ("x2T_hi", "x2T_lo")]
            output_mix(nc, top, c, x2T, ps, merged_scr, a["w_o"], a["x_prompt"], a["x_sample"], a["g_post_mix"],
                       a["g_pre_mlp"], x1_scr)
            mlp(nc, top, c, x2T, ps, a["w_up"], a["w_down"], a["g_post_mlp"], x1_scr, o["y_prompt"], o["y_sample"])


_INS = ["x_prompt", "x_sample", "cache_k_a", "cache_v_a", "cache_k_b", "cache_v_b", "cache_ki_b", "cache_meta",
        "meta_tokens", "g_pre_mix", "w_in", "attn_sinks", "w_o", "g_post_mix", "g_pre_mlp", "w_up", "w_down", "g_post_mlp"]
_OUTS = [("y_prompt", (1, N_PROMPT, D)), ("y_sample", (1, N_SAMPLE, D)),
         ("k_a_prompt", (1, 1, WINDOW, 2, HD)), ("v_a_prompt", (1, 1, WINDOW, 2, HD)),
         ("k_b_prompt", (1, 1, N_PROMPT, 1, HD)), ("v_b_prompt", (1, 1, N_PROMPT, 1, HD)),
         ("ki_b_prompt", (1, 1, N_PROMPT, HD)), ("meta_prompt", (1, 1, N_META, 6, HD)),
         ("k_a_sample", (1, 1, WINDOW, 2, HD)), ("v_a_sample", (1, 1, WINDOW, 2, HD)),
         ("k_b_sample", (1, 1, N_SAMPLE, 1, HD)), ("v_b_sample", (1, 1, N_SAMPLE, 1, HD)),
         ("ki_b_sample", (1, 1, N_SAMPLE, HD))]


def kernel(**inputs):
    import numpy as np
    import concourse.bacc as bacc
    from concourse.bass_utils import run_bass_kernel_spmd

    nc = bacc.Bacc("TRN2", target_bir_lowering=False, num_devices=1)
    arrays, a, o = {}, {}, {}
    for name in _INS:
        arrays[f"in_{name}"] = np.ascontiguousarray(inputs[name])
        a[name] = nc.dram_tensor(f"in_{name}", arrays[f"in_{name}"].shape, F32, kind="ExternalInput").ap()
    for name, shape in _OUTS:
        o[name] = nc.dram_tensor(f"out_{name}", shape, F32, kind="ExternalOutput").ap()
    streaming_step(nc, a, o)
    r = run_bass_kernel_spmd(nc, [arrays], core_ids=[0])
    return tuple(r.results[0][f"out_{name}"] for name, _ in _OUTS)
```

```python
from contextlib import ExitStack

import concourse.bass as bass
from concourse import mybir

F32 = mybir.dt.float32
F32R = mybir.dt.float32r
ALU = mybir.AluOpType
ACT = mybir.ActivationFunctionType

P = 128
D = 1024
KT = D // P
HD = 64
HEADS = 16
CHUNK = 64
N_PROMPT, N_SAMPLE, N_META = 1024, 64, 16
N_QUERY = N_PROMPT + N_SAMPLE
N_TOK = N_QUERY + N_META
TILES = 9
SAMPLE_TILE = 8
PAST = 1024
WINDOW = 128
IDX_HEADS = 8
TOPK = 256
D_FF = 4 * D
EPS = 1e-6
RAW, STAGE, BANKS, SCORES = 4, 3, 4, 4
INDEX_SCALE = (IDX_HEADS * HD) ** -0.5

QA, KA, QB, QI, KI, GA, D_IN = 0, 1024, 1280, 2432, 2944, 3016, 5064
KB = 2304
T_COLS = [(KA, 256), (KB, 128), (KI, 72)]
T_WIDTH = sum(n for _, n in T_COLS)
T_KA, T_VA, T_KB, T_VB, T_KI, T_WI = 0, 128, 256, 320, 384, 448

FAR = 1e30
TAKEN = -3.4e38
UNSEEN = -3.0e38


def slope(h):
    return 2.0 ** (-8.0 * (h + 1) / HEADS)


def tile_rows(t):
    return P if t < SAMPLE_TILE else N_SAMPLE


def tile_tokens(t):
    return P if t < SAMPLE_TILE else N_SAMPLE + N_META


def constants(sb):
    c = {}
    c["ident"] = sb("ident", [P, P])
    c["fold"] = sb("fold", [P, HD])
    c["eps"] = sb("eps", [P, 1])
    c["q_scale"] = sb("q_scale", [P, KT])
    return c


def refine_rstd(dve, step, n, out, rstd, mean_sq, work):
    dve.tensor_scalar(work, rstd, rstd, mean_sq, ALU.mult, ALU.mult).then_inc(step, 1)
    dve.wait_ge(step, n + 1)
    dve.tensor_scalar(work, work, -0.5, 1.5, ALU.mult, ALU.add).then_inc(step, 1)
    dve.wait_ge(step, n + 2)
    dve.tensor_tensor(out, rstd, work, ALU.mult).then_inc(step, 1)
    dve.wait_ge(step, n + 3)


def weight_signals(top, nc):
    sem = lambda n: top.enter_context(nc.semaphore(n))
    return {"loaded": [sem(f"p2_w_loaded{i}") for i in range(RAW)], "hi_done": sem("p2_w_hi_done"), "lo_done": sem("p2_w_lo_done")}


def load_weight_unit(act, ws, w_raw, w_in, n):
    ch, k = divmod(n, KT)
    if n >= RAW:
        act.wait_ge(ws["lo_done"], n - RAW + 1)
    col = 0
    for c0, w in CHUNKS[ch][1]:
        act.dma_start(w_raw[:, n % RAW, col:col + w], w_in[0, k * P:(k + 1) * P, c0:c0 + w]).then_inc(ws["loaded"][n % RAW], 16)
        col += w


def weight_loads(n):
    first = sum(16 * len(T_COLS) for m in range(n % RAW, min(n + 1, KT), RAW))
    return first + sum(16 for m in range(n % RAW, n + 1, RAW) if m >= KT)


def input_norm(nc, top, c, xT, b2, ws, ps, w_in, x_prompt, x_sample, meta_tokens, g_pre_mix):
    w_raw, w_hi, w_lo = b2["w_raw"], b2["w_hi"], b2["w_lo"]
    xT_hi, xT_lo = xT
    with ExitStack() as ctx:
        sb = lambda n, s, d=F32: ctx.enter_context(nc.sbuf_tensor(n, s, d))
        sem = lambda n: top.enter_context(nc.semaphore(n))
        x_in = sb("x_in", [P, 2, D])
        x_norm = sb("x_norm", [P, 2, D])
        squares = sb("squares", [P, D])
        sum_sq = sb("sum_sq", [P, TILES])
        std = sb("std", [P, TILES])
        mean_sq = sb("mean_sq", [P, TILES])
        rstd_0 = sb("rstd_0", [P, TILES])
        rstd = sb("rstd", [P, TILES])
        newton = sb("newton", [P, TILES])
        gain = sb("gain", [P, D])
        refined = sem("p1_refined")

        zeroed, const_ready = sem("p1_zeroed"), sem("p1_const_ready")
        gains_loaded = sem("p1_gains_loaded")
        x_loaded = [sem("p1_x_loaded0"), sem("p1_x_loaded1")]
        squared, std_ready, rstd_ready = sem("p1_squared"), sem("p1_std_ready"), sem("p1_rstd_ready")
        normed, transposed = sem("p1_normed"), sem("p1_transposed")
        hi_done, lo_done = sem("p1_hi_done"), sem("p1_lo_done")

        def x_loads(t):
            return 16 * (t // 2 + 1 + (t == SAMPLE_TILE))

        def toks(t):
            return slice(t * P, t * P + tile_tokens(t))

        with nc.Block() as block:

            @block.sync
            def _(sp):
                sp.dma_start(gain[:], g_pre_mix[0:1, :].to_broadcast([P, D])).then_inc(gains_loaded, 16)
                for t in range(TILES):
                    if t >= 2:
                        sp.wait_ge(normed, t - 1)
                    dst = x_in[:, t % 2, :]
                    if t < SAMPLE_TILE:
                        sp.dma_start(dst, x_prompt[0, t * P:(t + 1) * P, :]).then_inc(x_loaded[t % 2], 16)
                    else:
                        sp.dma_start(dst[0:N_SAMPLE], x_sample[0]).then_inc(x_loaded[t % 2], 16)
                        sp.dma_start(dst[N_SAMPLE:N_SAMPLE + N_META], meta_tokens).then_inc(x_loaded[t % 2], 16)

            @block.gpsimd
            def _(pool):
                pool.memset(c["ident"][:], 0.0).then_inc(zeroed, 1)
                pool.memset(c["fold"][:], 0.0).then_inc(zeroed, 1)
                pool.memset(c["eps"][:], EPS).then_inc(const_ready, 1)
                pool.wait_ge(zeroed, 2)
                pool.affine_select(out=c["ident"][:], in_=c["ident"][:], compare_op=ALU.not_equal, fill=1.0, base=0,
                                   pattern=[[-1, P]], channel_multiplier=1).then_inc(const_ready, 1)
                pool.affine_select(out=c["fold"][:], in_=c["fold"][:], compare_op=ALU.not_equal, fill=1.0, base=0,
                                   pattern=[[-1, HD]], channel_multiplier=1).then_inc(zeroed, 1)
                pool.wait_ge(zeroed, 3)
                pool.affine_select(out=c["fold"][:], in_=c["fold"][:], compare_op=ALU.not_equal, fill=1.0, base=-HD,
                                   pattern=[[-1, HD]], channel_multiplier=1).then_inc(const_ready, 1)
                for k in range(KT):
                    pool.wait_ge(ws["hi_done"], k + 1)
                    pool.tensor_tensor(w_lo[:, 0, k, 0:T_WIDTH], w_raw[:, k % RAW, 0:T_WIDTH],
                                       w_hi[:, 0, k, 0:T_WIDTH].bitcast(F32), ALU.subtract).then_inc(ws["lo_done"], 1)

            @block.scalar
            def _(act):
                def split_hi(t):
                    for g in range(2):
                        act.wait_ge(transposed, 2 * t + g + 1)
                        n = tile_tokens(t)
                        src = ps[:, (2 * t + g) % 4, :].rearrange("p (k n) -> p k n", k=4)[:, :, 0:n]
                        act.activation(xT_hi[:, 4 * g:4 * g + 4, toks(t)], src, ACT.Copy).then_inc(hi_done, 1)

                def first_weights_hi(k):
                    act.wait_ge(ws["loaded"][k % RAW], weight_loads(k))
                    act.activation(w_hi[:, 0, k, 0:T_WIDTH], w_raw[:, k % RAW, 0:T_WIDTH], ACT.Copy).then_inc(ws["hi_done"], 1)
                    if 1 <= k and k + RAW - 1 < KT:
                        load_weight_unit(act, ws, w_raw, w_in, k + RAW - 1)

                for k in range(RAW):
                    load_weight_unit(act, ws, w_raw, w_in, k)
                act.wait_ge(const_ready, 1)
                for t in range(TILES):
                    n = tile_tokens(t)
                    act.wait_ge(x_loaded[t % 2], x_loads(t))
                    act.activation(squares[:n], x_in[:n, t % 2, :], ACT.Square,
                                   accum_out=sum_sq[:n, t:t + 1]).then_inc(squared, 1)
                    act.wait_ge(squared, t + 1)
                    act.activation(std[:n, t:t + 1], sum_sq[:n, t:t + 1], ACT.Sqrt, bias=c["eps"][:n, :],
                                   scale=1.0 / D).then_inc(std_ready, 1)
                    if t >= 1:
                        split_hi(t - 1)
                        first_weights_hi(t - 1)
                split_hi(TILES - 1)

            @block.vector
            def _(dve):
                for f in range(KT):
                    for half in range(2):
                        dve.memset(c["q_scale"][half * HD:(half + 1) * HD, f:f + 1], HD ** -0.5 / slope(2 * f + half))

                def split_lo(t):
                    for g in range(2):
                        dve.wait_ge(hi_done, 2 * t + g + 1)
                        n = tile_tokens(t)
                        src = ps[:, (2 * t + g) % 4, :].rearrange("p (k n) -> p k n", k=4)[:, :, 0:n]
                        dst = (slice(None), slice(4 * g, 4 * g + 4), toks(t))
                        dve.tensor_tensor(xT_lo[dst], src, xT_hi[dst].bitcast(F32), ALU.subtract).then_inc(lo_done, 1)

                for t in range(TILES):
                    n = tile_tokens(t)
                    dve.wait_ge(std_ready, t + 1)
                    dve.reciprocal(rstd_0[:n, t:t + 1], std[:n, t:t + 1]).then_inc(rstd_ready, 1)
                    dve.tensor_scalar(mean_sq[:n, t:t + 1], sum_sq[:n, t:t + 1], 1.0 / D, EPS, ALU.mult, ALU.add).then_inc(rstd_ready, 1)
                    dve.wait_ge(rstd_ready, 2 * t + 2)
                    refine_rstd(dve, refined, 3 * t, rstd[:n, t:t + 1], rstd_0[:n, t:t + 1], mean_sq[:n, t:t + 1],
                                newton[:n, t:t + 1])
                    if t == 0:
                        dve.wait_ge(gains_loaded, 16)
                    if t >= 2:
                        dve.wait_ge(transposed, 2 * t - 2)
                    dve.scalar_tensor_tensor(out=x_norm[:n, t % 2, :], in0=x_in[:n, t % 2, :], scalar=rstd[:n, t:t + 1],
                                             in1=gain[:n, :], op0=ALU.mult, op1=ALU.mult).then_inc(normed, 1)
                    if t >= 1:
                        split_lo(t - 1)
                split_lo(TILES - 1)

            @block.tensor
            def _(pe):
                pe.wait_ge(const_ready, 2)
                for t in range(TILES):
                    n = tile_tokens(t)
                    pe.wait_ge(normed, t + 1)
                    for g in range(2):
                        u = 2 * t + g
                        if u >= 4:
                            pe.wait_ge(lo_done, u - 3)
                        for k in range(4):
                            last = pe.transpose(ps[:, u % 4, k * P:k * P + n],
                                                x_norm[:n, t % 2, (4 * g + k) * P:(4 * g + k + 1) * P],
                                                c["ident"][:n, :n])
                        last.then_inc(transposed, 1)


TOKEN_MAJOR, GATE, FEATURE_MAJOR = "token-major", "gate", "feature-major"
CHUNKS = [(TOKEN_MAJOR, T_COLS)]
CHUNKS += [(FEATURE_MAJOR, [(QI, 512)])]
CHUNKS += [(FEATURE_MAJOR, [(QB + 512 * j, 512)]) for j in range(2)]
CHUNKS += [(FEATURE_MAJOR, [(QA + 512 * j, 512)]) for j in range(2)]
CHUNKS += [(GATE, [(GA + 512 * j, 512)]) for j in range(4)]
QT_ROW = {QA: 0, QA + 512: 512, QB: 1024, QB + 512: 1536, QI: 2048}
TOK_BLOCKS = [(0, 364), (364, 362), (726, 362)]
INDEX_TILES = [8, 7, 6, 5, 4, 3, 2]
INDEX_AT = [1, 2, 3, 4, 5, 7, 8]
INDEX_CHUNK = INDEX_AT[0]
KEYS_AT, QUERIES_AT = 3, 6


def index_tile(ch):
    return INDEX_AT.index(ch) if ch in INDEX_AT else -1


def keys_seen(t):
    return P * (t + 1) if t < SAMPLE_TILE else PAST + N_SAMPLE


def groups_of(c):
    kind = CHUNKS[c][0]
    if kind == FEATURE_MAJOR:
        return [(f, t0, n) for t0, n in reversed(TOK_BLOCKS) for f in range(4)]
    rows = tile_tokens if kind == TOKEN_MAJOR else tile_rows
    return [(None, t * P, rows(t)) for t in range(TILES)]


GROUP_BASE = [sum(len(groups_of(i)) for i in range(c)) for c in range(len(CHUNKS) + 1)]


def selection_buffers(ctx, nc):
    sb = lambda n, s, d=F32: ctx.enter_context(nc.sbuf_tensor(n, s, d))
    return {
        "score": sb("score", [P, SCORES, N_META + N_QUERY]),
        "top8": sb("top8", [P, 2, 8]),
        "dist": sb("dist", [P, N_PROMPT + P]),
    }


def weight_buffers(ctx, nc, weights):
    sb = lambda n, s, d=F32: ctx.enter_context(nc.sbuf_tensor(n, s, d))
    return {"w_raw": sb("w_raw", [P, RAW, 512]), "w_hi": sb("w_hi", [P, 2, KT, 512], F32R),
            "w_lo": weights[:].rearrange("p (a k n) -> p a k n", a=2, k=KT)}


def projection_buffers(ctx, nc):
    sb = lambda n, s, d=F32: ctx.enter_context(nc.sbuf_tensor(n, s, d))
    return {
        "stage": sb("stage", [P, STAGE, 512]),
        "w_idx": sb("w_idx", [P, TILES, IDX_HEADS]),
        "kp": sb("kp", [P, 2, N_PROMPT], F32R),
        "ks": sb("ks", [P, 2, N_QUERY], F32R),
        "rel": sb("rel", [P, 2, N_QUERY]),
        "q_raw": sb("q_raw", [P, IDX_HEADS, P]),
        "q_st": sb("q_st", [P, IDX_HEADS, P], F32R),
    }


def projection(nc, top, c, xT, b2, ws, sel, kv, raw, ps, w_in, caches, cache_ki_b, attn_sinks, t_scr, q_scr, gate_scr, dist_scr):
    xT_hi, xT_lo = xT
    N_CH = len(CHUNKS)
    cache_k_a, cache_v_a, cache_k_b, cache_v_b, cache_meta = caches
    sets = operand_sets(kv, raw)
    GROUPS = key_groups(sets)
    SLOT_BASE = [sum(g[2] for g in GROUPS[:j]) for j in range(len(GROUPS))]
    sem = lambda n: top.enter_context(nc.semaphore(n))
    w_raw, w_hi, w_lo, stage, w_idx, kp, ks, rel, q_raw, q_st = (
        b2[n] for n in ("w_raw", "w_hi", "w_lo", "stage", "w_idx", "kp", "ks", "rel", "q_raw", "q_st"))
    score, top8, dist = sel["score"], sel["top8"], sel["dist"]
    k_raw = rel[:].rearrange("p a b -> p (a b)").rearrange("p (j u d) -> p j u d", u=2, d=HD)
    ps_idx = ps[:, 5:8, :].rearrange("p b n -> p (b n)")

    w_loaded, w_hi_done, w_lo_done = ws["loaded"], ws["hi_done"], ws["lo_done"]
    group_done, group_out = sem("p2_group_done"), sem("p2_group_out")
    wi_copied = sem("p2_wi_copied")
    stored = [sem(f"p2_stored{i}") for i in range(STAGE)]
    k_loaded, k_turned, k_hi_done, k_lo_done = (sem(f"p2_k_{n}") for n in ("loaded", "turned", "hi_done", "lo_done"))
    q_loaded, q_hi_done, q_lo_done = sem("p2_q_loaded"), sem("p2_q_hi_done"), sem("p2_q_lo_done")
    idx_done, rel_done, weighted, added = sem("p2_idx_done"), sem("p2_rel_done"), sem("p2_weighted"), sem("p2_added")
    dist_iota, dist_ready = sem("p2_dist_iota"), sem("p2_dist_ready")
    first_masks = sem("p2_first_masks")
    select_step = [sem("p2_select_even"), sem("p2_select_odd")]
    mask_ready = sem("p2_mask_ready")
    mask_stored = [sem(f"p2_mask_stored{i}") for i in range(SCORES)]

    def stores(u):
        return 16 * (u // STAGE + 1)

    prompt_loaded, sample_loaded = sem("p3_prompt_loaded"), sem("p3_sample_loaded")
    PROMPT_LOADS, SAMPLE_LOADS = 3, 7
    kt_hi_done, kt_lo_done, kt_turned, kt_copied = (sem(f"p3_k_{n}") for n in ("hi_done", "lo_done", "turned", "copied"))
    v_hi_done, v_lo_done = sem("p3_v_hi_done"), sem("p3_v_lo_done")
    sinks_loaded, band_iota, band_step = sem("p3_sinks_loaded"), sem("p3_band_iota"), sem("p3_band_step")

    def set_loaded(eng, s):
        eng.wait_ge(prompt_loaded, 16 * PROMPT_LOADS)
        if sets[s][3]:
            eng.wait_ge(sample_loaded, 16 * SAMPLE_LOADS)

    MASKS = 2 + len(INDEX_TILES)

    def mask_slot(n):
        return (n + 2) % SCORES

    def slot_free(eng, n):
        if n >= SCORES:
            eng.wait_ge(mask_stored[mask_slot(n)], 16 * (n // SCORES))

    def index_groups(i):
        if i == 0:
            return {g: [2 * (g - 8), 2 * (g - 8) + 1] for g in range(8, 12)}
        return {g: [g - 1] for g in range(1, IDX_HEADS + 1)}

    def unit_cols(ch):
        return sum(n for _, n in CHUNKS[ch][1])

    K_GROUPS = [(0, 4, P, kp, 0), (4, 4, P, kp, 512), (8, 4, P, ks, 0), (12, 4, P, ks, 512), (16, 1, N_SAMPLE, ks, PAST)]

    with nc.Block() as block:

        @block.sync
        def _(sp):
            def store(ch, g):
                kind, segs = CHUNKS[ch]
                f, t0, n = groups_of(ch)[g]
                u = GROUP_BASE[ch] + g
                sp.wait_ge(group_out, u + 1)
                src = stage[:, u % STAGE, :]
                if kind == TOKEN_MAJOR:
                    sp.dma_start(t_scr[t0:t0 + n, :], src[:n, 0:T_WIDTH]).then_inc(stored[u % STAGE], 16)
                elif kind == GATE:
                    col = segs[0][0] - GA
                    sp.dma_start(gate_scr[t0:t0 + n, col:col + 512], src[:n, :]).then_inc(stored[u % STAGE], 16)
                else:
                    row = QT_ROW[segs[0][0]] + f * P
                    sp.dma_start(q_scr[row:row + P, t0:t0 + n], src[:, 0:n]).then_inc(stored[u % STAGE], 16)

            def all_stored(ch):
                for u in range(GROUP_BASE[ch + 1] - STAGE, GROUP_BASE[ch + 1]):
                    sp.wait_ge(stored[u % STAGE], stores(u))

            def load_q(i):
                t = INDEX_TILES[i]
                r = tile_rows(t)
                src = q_scr[2048:2560, t * P:t * P + r].rearrange("(h d) n -> d h n", d=HD)
                for half in range(2):
                    sp.dma_start(q_raw[half * HD:(half + 1) * HD, :, 0:r], src).then_inc(q_loaded, 16)

            def store_mask(n, t):
                sp.wait_ge(mask_ready, n + 1)
                w = N_META + keys_seen(t)
                sp.dma_start(dist_scr[t, 0:tile_rows(t), 0:w], score[:tile_rows(t), mask_slot(n), 0:w])\
                  .then_inc(mask_stored[mask_slot(n)], 16)

            store_mask(0, 0)
            store_mask(1, 1)
            mask_at, LATE_MASKS = {4: [0], 6: [1], 7: [2]}, [3, 4, 5, 6]
            for ch in range(N_CH):
                for g in range(len(groups_of(ch))):
                    store(ch, g)
                    if ch == INDEX_CHUNK and g == 3:
                        for u in range(GROUP_BASE[ch] + 4 - STAGE, GROUP_BASE[ch] + 4):
                            sp.wait_ge(stored[u % STAGE], stores(u))
                        load_q(0)
                    i = index_tile(ch + 1)
                    if i >= 2 and g == 3:
                        sp.wait_ge(q_lo_done, i)
                        load_q(i)
                if ch == 0:
                    all_stored(0)
                    for half in range(2):
                        sp.dma_start(k_raw[:, 0:8, half, :],
                                     t_scr[0:N_PROMPT, T_KI:T_KI + HD].rearrange("(j p) d -> p j d", p=P)).then_inc(k_loaded, 16)
                        sp.dma_start(k_raw[:, 8:16, half, :],
                                     cache_ki_b[0, 0].rearrange("(j p) d -> p j d", p=P)).then_inc(k_loaded, 16)
                        sp.dma_start(k_raw[0:N_SAMPLE, 16, half, :],
                                     t_scr[N_PROMPT:N_QUERY, T_KI:T_KI + HD]).then_inc(k_loaded, 16)
                if ch == INDEX_CHUNK:
                    all_stored(ch)
                    sp.wait_ge(q_lo_done, 1)
                    load_q(1)
                for i in mask_at.get(ch, []):
                    store_mask(i + 2, INDEX_TILES[i])
            all_stored(N_CH - 1)
            sp.wait_ge(group_done, GROUP_BASE[N_CH])
            sp.wait_ge(added, IDX_HEADS * len(INDEX_TILES))
            new = slice(N_PROMPT, N_QUERY)
            T_KV = T_KI
            for j in range(0, 8, 4):
                sp.dma_start(raw["p"][:, j:j + 4, :], t_scr[P * j:P * (j + 4), 0:T_KV].rearrange("(j p) d -> p j d", p=P))\
                  .then_inc(prompt_loaded, 16)
            sp.dma_start(raw["m"][:], t_scr[N_QUERY:N_TOK, 0:T_KV]).then_inc(prompt_loaded, 16)
            sp.dma_start(raw["n"][0:HD], t_scr[new, 0:T_KV]).then_inc(sample_loaded, 16)
            sp.dma_start(raw["n"][HD:P], t_scr[new, 0:T_KV]).then_inc(sample_loaded, 16)
            sp.dma_start(raw["cm"][:], cache_meta[0, 0].rearrange("m s d -> m (s d)")).then_inc(sample_loaded, 16)
            for i, cache in enumerate((cache_k_a, cache_v_a)):
                sp.dma_start(raw["ca"][:, i, :], cache[0, 0].rearrange("n h d -> n (h d)")).then_inc(sample_loaded, 16)
            for i, cache in enumerate((cache_k_b, cache_v_b)):
                sp.dma_start(raw["cb"][:, i], cache[0, 0, :, 0, :].rearrange("(j p) d -> p j d", p=P)).then_inc(sample_loaded, 16)
            sp.dma_start(kv["sinks"][:], attn_sinks[0:1, :].to_broadcast([P, HEADS])).then_inc(sinks_loaded, 16)
            for i in LATE_MASKS:
                store_mask(i + 2, INDEX_TILES[i])
            for n in range(MASKS - SCORES, MASKS):
                sp.wait_ge(mask_stored[mask_slot(n)], 16 * (n // SCORES + 1))

        @block.scalar
        def _(act):
            def split_hi(n):
                ch, k = divmod(n, KT)
                w = unit_cols(ch)
                act.wait_ge(w_loaded[n % RAW], weight_loads(n))
                if ch >= 2:
                    act.wait_ge(group_done, GROUP_BASE[ch - 1])
                act.activation(w_hi[:, ch % 2, k, 0:w], w_raw[:, n % RAW, 0:w], ACT.Copy).then_inc(w_hi_done, 1)
                if n + RAW - 1 < N_CH * KT and n >= 1:
                    load_weight_unit(act, ws, w_raw, w_in, n + RAW - 1)

            def evacuate(ch, g):
                kind, segs = CHUNKS[ch]
                f, t0, n = groups_of(ch)[g]
                u = GROUP_BASE[ch] + g
                act.wait_ge(group_done, u + 1)
                if u >= STAGE:
                    act.wait_ge(stored[u % STAGE], stores(u - STAGE))
                dst = stage[:, u % STAGE, :]
                bank = ps[:, u % BANKS, :]
                if kind == TOKEN_MAJOR:
                    t = t0 // P
                    act.activation(w_idx[:n, t, :], bank[:n, T_WI:T_WI + IDX_HEADS], ACT.Copy, scale=INDEX_SCALE)\
                       .then_inc(wi_copied, 1)
                    act.activation(dst[:n, 0:T_WIDTH], bank[:n, 0:T_WIDTH], ACT.Copy).then_inc(group_out, 1)
                elif kind == GATE:
                    act.activation(dst[:n, :], bank[:n, :], ACT.Sigmoid).then_inc(group_out, 1)
                elif segs[0][0] == QI:
                    act.activation(dst[:, 0:n], bank[:, 0:n], ACT.Copy).then_inc(group_out, 1)
                else:
                    pair = (QT_ROW[segs[0][0]] % D) // P + f
                    act.activation(dst[:, 0:n], bank[:, 0:n], ACT.Copy,
                                   scale=c["q_scale"][:, pair:pair + 1]).then_inc(group_out, 1)

            def keys_hi(j):
                _, tiles, n, dst, col = K_GROUPS[j]
                act.wait_ge(k_turned, j + 1)
                act.activation(dst[:, 0, col:col + tiles * n], ps[:, 4, 0:tiles * n], ACT.Copy).then_inc(k_hi_done, 1)

            def queries_hi(i):
                r = tile_rows(INDEX_TILES[i])
                act.wait_ge(q_loaded, 32 * (i + 1))
                if i >= 1:
                    act.wait_ge(idx_done, IDX_HEADS * i)
                act.activation(q_st[:, :, 0:r], q_raw[:, :, 0:r], ACT.Copy).then_inc(q_hi_done, 1)

            def relu(i, h):
                n, r = keys_seen(INDEX_TILES[i]), tile_rows(INDEX_TILES[i])
                v = IDX_HEADS * i + h
                act.wait_ge(idx_done, v + 1)
                if v >= 2:
                    act.wait_ge(added, v - 1)
                act.activation(rel[:r, v % 2, 0:n], ps_idx[:r, 0:n], ACT.Relu).then_inc(rel_done, 1)
                if i == 0:
                    return
                act.wait_ge(rel_done, v + 1)
                act.activation(rel[:r, v % 2, 0:n], rel[:r, v % 2, 0:n], ACT.Copy,
                               scale=w_idx[:r, INDEX_TILES[i], h:h + 1]).then_inc(weighted, 1)

            for n in range(KT, KT + RAW - 1):
                load_weight_unit(act, ws, w_raw, w_in, n)
            for ch in range(N_CH):
                i = index_tile(ch)
                if 1 <= i < len(INDEX_TILES):
                    queries_hi(i)
                for g in range(len(groups_of(ch))):
                    evacuate(ch, g)
                    if g < KT and ch + 1 < N_CH:
                        split_hi((ch + 1) * KT + g)
                    if ch == INDEX_CHUNK and 0 <= g - KEYS_AT < len(K_GROUPS):
                        keys_hi(g - KEYS_AT)
                    if ch == INDEX_CHUNK and g == QUERIES_AT:
                        queries_hi(0)
                    if 0 <= i < len(INDEX_TILES):
                        for h in index_groups(i).get(g, []):
                            relu(i, h)
            for j, group in enumerate(GROUPS):
                s, first, n, rows, _ = group
                set_loaded(act, s)
                act.activation(raw["k_twice_hi"][0:rows, SLOT_BASE[j]:SLOT_BASE[j] + n], key_source(sets, group), ACT.Copy)\
                   .then_inc(kt_hi_done, 1)
            for s in range(len(sets)):
                for rows, slot, n, src in value_parts(sets, s):
                    act.activation(sets[s][1][rows, slot:slot + n, 0:HD], src, ACT.Copy).then_inc(v_hi_done, 1)
            for j, (s, first, n, rows, col) in enumerate(GROUPS):
                act.wait_ge(kt_turned, j + 1)
                act.activation(sets[s][0][:, :, col:col + n * rows], ps[:, 2 * (j % 4):2 * (j % 4) + 2, 0:n * rows], ACT.Copy)\
                   .then_inc(kt_copied, 1)

        @block.gpsimd
        def _(pool):
            def split_lo(n):
                ch, k = divmod(n, KT)
                w = unit_cols(ch)
                pool.wait_ge(w_hi_done, n + 1)
                i = index_tile(ch - 1)
                if 1 <= i < len(INDEX_TILES):
                    pool.wait_ge(added, IDX_HEADS * i + max(k - 1, 0))
                if 1 <= i < len(INDEX_TILES) or (i == 0 and k > QUERIES_AT):
                    pool.wait_ge(q_lo_done, i + 1)
                pool.tensor_tensor(w_lo[:, ch % 2, k, 0:w], w_raw[:, n % RAW, 0:w], w_hi[:, ch % 2, k, 0:w].bitcast(F32),
                                   ALU.subtract).then_inc(w_lo_done, 1)

            def queries_lo(i):
                r = tile_rows(INDEX_TILES[i])
                pool.wait_ge(q_hi_done, i + 1)
                pool.wait_ge(w_lo_done, KT * (INDEX_AT[i] + 1) + (QUERIES_AT + 1 if i == 0 else 0))
                if i >= 1:
                    pool.wait_ge(added, IDX_HEADS * i)
                pool.tensor_tensor(q_st[HD:, :, 0:r], q_raw[HD:, :, 0:r], q_st[HD:, :, 0:r].bitcast(F32),
                                   ALU.subtract).then_inc(q_lo_done, 1)

            def add_head(i, h):
                t = INDEX_TILES[i]
                n, r = keys_seen(t), tile_rows(t)
                v = IDX_HEADS * i + h
                pool.wait_ge(weighted, v + 1 - IDX_HEADS)
                pool.wait_ge(w_lo_done, KT * (INDEX_AT[i] + 1) + min(h + 2, KT))
                pool.wait_ge(q_lo_done, i + 1)
                out = score[:r, mask_slot(i + 2), N_META:N_META + n]
                if h == 0:
                    slot_free(pool, i + 2)
                    pool.tensor_copy(out, rel[:r, v % 2, 0:n]).then_inc(added, 1)
                else:
                    pool.wait_ge(added, v)
                    pool.tensor_tensor(out, out, rel[:r, v % 2, 0:n], ALU.add).then_inc(added, 1)

            pool.iota(dist[:], pattern=[[-1, N_PROMPT + P]], base=N_PROMPT, channel_multiplier=1,
                      allow_small_or_imprecise_dtypes=True).then_inc(dist_iota, 1)
            for ch in range(N_CH):
                i = index_tile(ch)
                if 1 <= i < len(INDEX_TILES):
                    queries_lo(i)
                for g in range(IDX_HEADS + 1):
                    if g < KT and ch + 1 < N_CH:
                        split_lo((ch + 1) * KT + g)
                    if i == 0 and g == QUERIES_AT:
                        queries_lo(0)
                    if 1 <= i < len(INDEX_TILES) and 1 <= g:
                        add_head(i, g - 1)
            set_loaded(pool, 0)
            for j, group in enumerate(GROUPS):
                s, first, n, rows, _ = group
                set_loaded(pool, s)
                pool.wait_ge(kt_hi_done, j + 1)
                at = (slice(0, rows), slice(SLOT_BASE[j], SLOT_BASE[j] + n))
                pool.tensor_tensor(raw["k_twice_lo"][at], key_source(sets, group), raw["k_twice_hi"][at].bitcast(F32),
                                   ALU.subtract).then_inc(kt_lo_done, 1)
            parts, shifted = 0, False
            for s in range(len(sets)):
                for rows, slot, n, src in value_parts(sets, s):
                    parts += 1
                    pool.wait_ge(v_hi_done, parts)
                    if rows.start or shifted:
                        pool.wait_ge(v_lo_done, parts - 1)
                    shifted = rows.start > 0
                    pool.tensor_tensor(sets[s][1][rows, slot:slot + n, HD:P], src,
                                       sets[s][1][rows, slot:slot + n, 0:HD].bitcast(F32), ALU.subtract).then_inc(v_lo_done, 1)
            pool.wait_ge(v_lo_done, parts)
            pool.iota(kv["dist_a"][:, N_META:], pattern=[[-1, 2 * P]], base=P, channel_multiplier=1,
                      allow_small_or_imprecise_dtypes=True).then_inc(band_iota, 1)

        @block.vector
        def _(dve):
            dve.wait_ge(dist_iota, 1)
            dve.scalar_tensor_tensor(out=dist[:], in0=dist[:], scalar=-1.0, in1=dist[:], op0=ALU.mult,
                                     op1=ALU.max).then_inc(dist_ready, 1)
            dve.memset(score[:, :, 0:N_META], 0.0).then_inc(dist_ready, 1)
            dve.wait_ge(dist_ready, 2)
            for t in range(2):
                n = keys_seen(t)
                dve.tensor_copy(score[:, mask_slot(t), N_META:N_META + n], dist[:, N_PROMPT - t * P:N_PROMPT - t * P + n]).then_inc(first_masks, 1)
                dve.wait_ge(first_masks, t + 1)
                dve.memset(score[0:CHUNK, mask_slot(t), N_META + n - CHUNK:N_META + n], FAR).then_inc(mask_ready, 1)
            for j, (_, tiles, n, dst, col) in enumerate(K_GROUPS):
                dve.wait_ge(k_hi_done, j + 1)
                dve.tensor_tensor(dst[:, 1, col:col + tiles * n], ps[:, 4, 0:tiles * n],
                                  dst[:, 0, col:col + tiles * n].bitcast(F32), ALU.subtract).then_inc(k_lo_done, 1)
            steps = [0, 0]

            def ready(i):
                t = INDEX_TILES[i]
                n, r, slot = keys_seen(t), tile_rows(t), mask_slot(i + 2)
                work = score[:r, slot, N_META:N_META + n]
                if i == 0:
                    dve.wait_ge(wi_copied, TILES)
                    for h in range(IDX_HEADS):
                        dve.wait_ge(rel_done, h + 1)
                        if h == 0:
                            dve.tensor_scalar(work, rel[:r, h % 2, 0:n], w_idx[:r, t, h:h + 1], None, ALU.mult).then_inc(added, 1)
                        else:
                            dve.wait_ge(added, h)
                            dve.scalar_tensor_tensor(out=work, in0=rel[:r, h % 2, 0:n], scalar=w_idx[:r, t, h:h + 1], in1=work,
                                                     op0=ALU.mult, op1=ALU.add).then_inc(added, 1)
                dve.wait_ge(added, IDX_HEADS * (i + 1))
                if t < SAMPLE_TILE:
                    dve.memset(score[0:CHUNK, slot, N_META + n - CHUNK:N_META + n], UNSEEN).then_inc(select_step[i % 2], 1)
                    steps[i % 2] += 1
                return work

            def finish(i, work):
                t = INDEX_TILES[i]
                n, r = keys_seen(t), tile_rows(t)
                dve.wait_ge(select_step[i % 2], steps[i % 2])
                dve.tensor_scalar(work, work, TAKEN, FAR, ALU.not_equal, ALU.mult).then_inc(select_step[i % 2], 1)
                steps[i % 2] += 1
                dve.wait_ge(select_step[i % 2], steps[i % 2])
                c0 = N_PROMPT - t * P
                dve.tensor_tensor(work, work, dist[:r, c0:c0 + n], ALU.max).then_inc(mask_ready, 1)

            ROUNDS = TOPK // 8
            first = [0, ROUNDS, ROUNDS + 12]
            while len(first) < len(INDEX_TILES):
                first.append(first[-2] + ROUNDS)
            works = {}
            for at in range(first[-1] + ROUNDS):
                live = [i for i in range(len(INDEX_TILES)) if first[i] <= at < first[i] + ROUNDS]
                for i in live:
                    if at == first[i]:
                        works[i] = ready(i)
                for i in live:
                    if steps[i % 2]:
                        dve.wait_ge(select_step[i % 2], steps[i % 2])
                    dve.max(top8[:tile_rows(INDEX_TILES[i]), i % 2], works[i]).then_inc(select_step[i % 2], 1)
                    steps[i % 2] += 1
                for i in live:
                    dve.wait_ge(select_step[i % 2], steps[i % 2])
                    dve.match_replace(works[i], top8[:tile_rows(INDEX_TILES[i]), i % 2], works[i], TAKEN)\
                       .then_inc(select_step[i % 2], 1)
                    steps[i % 2] += 1
                for i in live:
                    if at == first[i] + ROUNDS - 1:
                        finish(i, works[i])
            set_loaded(dve, len(sets) - 1)
            for s in range(len(sets)):
                if sets[s][3]:
                    dve.memset(sets[s][1][0:HD, 1 + sets[s][2], :].bitcast(F32), 0.0)
            da, da0, sinks = kv["dist_a"], kv["dist_a0"], kv["sinks"]
            dve.wait_ge(band_iota, 1)
            dve.scalar_tensor_tensor(out=da[:, N_META:], in0=da[:, N_META:], scalar=-1.0, in1=da[:, N_META:],
                                     op0=ALU.mult, op1=ALU.max).then_inc(band_step, 1)
            dve.memset(da[:, 0:N_META], 0.0).then_inc(band_step, 1)
            dve.memset(da0[:, 0:N_META], 0.0).then_inc(band_step, 1)
            dve.wait_ge(band_step, 3)
            dve.memset(da[0:CHUNK, N_META + 3 * CHUNK:N_META + 4 * CHUNK], FAR).then_inc(band_step, 1)
            dve.memset(da[CHUNK:P, N_META:N_META + CHUNK], FAR).then_inc(band_step, 1)
            dve.wait_ge(sinks_loaded, 16)
            for h in range(HEADS):
                dve.tensor_scalar(kv["sinks_scaled"][:, h:h + 1], sinks[:, h:h + 1], 1.0 / slope(h), None, ALU.mult)
            dve.wait_ge(band_step, 5)
            dve.tensor_copy(da0[:, N_META:], da[:, N_META + P:])

        @block.tensor
        def _(pe):
            def group(ch, g):
                kind = CHUNKS[ch][0]
                f, t0, n = groups_of(ch)[g]
                u = GROUP_BASE[ch] + g
                if u >= BANKS:
                    pe.wait_ge(group_out, u - BANKS + 1)
                for k in range(KT):
                    x_hi, x_lo = xT_hi[:, k, t0:t0 + n], xT_lo[:, k, t0:t0 + n]
                    if kind == FEATURE_MAJOR:
                        wh, wl = w_hi[:, ch % 2, k, f * P:(f + 1) * P], w_lo[:, ch % 2, k, f * P:(f + 1) * P]
                        out, terms = ps[:, u % BANKS, 0:n], ((wh, x_hi), (wh, x_lo), (wl, x_hi))
                    else:
                        w = unit_cols(ch)
                        wh, wl = w_hi[:, ch % 2, k, 0:w], w_lo[:, ch % 2, k, 0:w]
                        out, terms = ps[:n, u % BANKS, 0:w], ((x_hi, wh), (x_hi, wl), (x_lo, wh))
                    for j, (a, b) in enumerate(terms):
                        last = pe.matmul(out, a, b, start=(k == 0 and j == 0), stop=(k == KT - 1 and j == 2))
                last.then_inc(group_done, 1)

            def turn_keys(j):
                first, tiles, n, _, _ = K_GROUPS[j]
                if j == 0:
                    pe.wait_ge(k_loaded, 16 * 6)
                if j >= 1:
                    pe.wait_ge(k_lo_done, j)
                for a in range(tiles):
                    last = pe.transpose(ps[:, 4, a * n:(a + 1) * n],
                                        k_raw[:n, first + a, :, :].rearrange("p u d -> p (u d)"), c["ident"][:n, :n])
                last.then_inc(k_turned, 1)

            def index_scores(i, h):
                t = INDEX_TILES[i]
                n, r = keys_seen(t), tile_rows(t)
                v = IDX_HEADS * i + h
                if h == 0:
                    pe.wait_ge(q_lo_done, i + 1)
                if i == 0 and h == 0:
                    pe.wait_ge(k_lo_done, len(K_GROUPS))
                if v >= 1:
                    pe.wait_ge(rel_done, v)
                keys = kp if t < SAMPLE_TILE else ks
                for n0 in range(0, n, 512):
                    n1 = min(n, n0 + 512)
                    for part in range(2):
                        last = pe.matmul(ps_idx[:r, n0:n1], q_st[:, h, 0:r], keys[:, part, n0:n1],
                                         start=(part == 0), stop=(part == 1))
                last.then_inc(idx_done, 1)

            for ch in range(N_CH):
                pe.wait_ge(w_lo_done, KT * (ch + 1))
                i = index_tile(ch)
                for g in range(len(groups_of(ch))):
                    group(ch, g)
                    if ch == INDEX_CHUNK and 0 <= g - KEYS_AT < len(K_GROUPS):
                        turn_keys(g - KEYS_AT)
                    if 0 <= i < len(INDEX_TILES):
                        for h in index_groups(i).get(g, []):
                            index_scores(i, h)
            pe.wait_ge(group_out, GROUP_BASE[N_CH])
            for j, (s, first, n, rows, _) in enumerate(GROUPS):
                if j >= 4:
                    pe.wait_ge(kt_copied, j - 3)
                for part, (keys, split) in enumerate(((raw["k_twice_hi"], kt_hi_done), (raw["k_twice_lo"], kt_lo_done))):
                    pe.wait_ge(split, j + 1)
                    for a in range(n):
                        src = keys[0:rows, SLOT_BASE[j] + a].rearrange("p t d -> p (t d)")
                        last = pe.transpose(ps[:, 2 * (j % 4) + part, a * rows:(a + 1) * rows],
                                            src.bitcast(F32) if part == 0 else src, c["ident"][0:rows, 0:rows])
                last.then_inc(kt_turned, 1)


def band_width(t):
    return P if t == 0 else (2 * P if t < SAMPLE_TILE else WINDOW + N_SAMPLE)


def key_columns(branch, t):
    return N_META + (band_width(t) if branch == 0 else keys_seen(t))


def key_tiles(branch, t):
    w = key_columns(branch, t)
    tiles = [(0, N_META, 0)]
    if branch == 0 and t == SAMPLE_TILE:
        return tiles + [(N_META, P, 1), (w - P, P, 2)]
    if branch == 0:
        return tiles + [(N_META + P * j, P, t + j + 1 - (t > 0)) for j in range(band_width(t) // P)]
    if t == SAMPLE_TILE:
        return tiles + [(N_META + P * j, P, j + 1) for j in range(8)] + [(w - P, P, 9)]
    return tiles + [(N_META + P * j, P, j + 1) for j in range(t + 1)]


KV_COPIES = 13


def operand_buffers(ctx, nc):
    sb = lambda n, s, d=F32: ctx.enter_context(nc.sbuf_tensor(n, s, d))
    T_KV = T_KI
    return {
        "p": sb("raw_p", [P, 8, T_KV]),
        "m": sb("raw_m", [N_META, T_KV]),
        "cm": sb("raw_cm", [N_META, T_KV]),
        "n": sb("raw_n", [P, T_KV]),
        "ca": sb("raw_ca", [P, 2, 2 * HD]),
        "cb": sb("raw_cb", [P, 2, 8, HD]),
        "k_twice_hi": sb("k_twice_hi", [P, 43, 2, HD], F32R),
        "k_twice_lo": sb("k_twice_lo", [P, 43, 2, HD]),
    }


def operand_sets(kv, raw):
    sets = []

    def add_set(k, v, tiles, k_col, v_col, cached=None):
        cols = (slice(k_col, k_col + HD), slice(v_col, v_col + HD))
        if cached is None:
            sets.append((k, v, tiles, None, [(raw["m"][:, q], raw["p"][:, :, q], None) for q in cols]))
        else:
            sets.append((k, v, tiles, N_SAMPLE, [(raw["cm"][:, q], cached[i], raw["n"][:, q]) for i, q in enumerate(cols)]))

    for g in range(2):
        add_set(kv["k_a_p"][:, g], kv["v_a_p"][:, g], 8, T_KA + HD * g, T_VA + HD * g)
    add_set(kv["k_b_p"][:], kv["v_b_p"][:], 8, T_KB, T_VB)
    for g in range(2):
        add_set(kv["k_a_s"][:, g], kv["v_a_s"][:, g], 1, T_KA + HD * g, T_VA + HD * g,
                [raw["ca"][:, i:i + 1, HD * g:HD * (g + 1)] for i in range(2)])
    add_set(kv["k_b_s"][:], kv["v_b_s"][:], 8, T_KB, T_VB, [raw["cb"][:, i] for i in range(2)])
    return sets


def key_groups(sets):
    out = []
    for s, (_, _, m, last, _) in enumerate(sets):
        out.append((s, 0, 1, N_META, 0))
        for j in range(0, m, 4):
            out.append((s, 1 + j, min(4, m - j), P, N_META + P * j))
        if last:
            out.append((s, 1 + m, 1, last, N_META + P * m))
    return out


def key_source(sets, group):
    s, first, n, rows, _ = group
    k_meta, k_tiles, k_new = sets[s][4][0]
    if first == 0:
        src = k_meta.unsqueeze(1)
    elif first <= sets[s][2]:
        src = k_tiles[:, first - 1:first - 1 + n]
    else:
        src = k_new[0:rows].unsqueeze(1)
    return src.unsqueeze(2).to_broadcast([rows, n, 2, HD])


def value_parts(sets, s):
    _, _, m, last, (_, (v_meta, v_tiles, v_new)) = sets[s]
    parts = [(slice(0, N_META), 0, 1, v_meta.unsqueeze(1)), (slice(0, P), 1, m, v_tiles)]
    if last:
        parts.append((slice(HD, P), 1 + m, 1, v_new[HD:P].unsqueeze(1)))
    return parts


KV_COPIES = 13


def attention(nc, top, c, ps, kv, wo_raw, wo_loaded, w_o, q_scr, gate_scr, dist_scr, merged_scr, t_scr, caches, outs):
    with ExitStack() as ctx:
        sb = lambda n, s, d=F32: ctx.enter_context(nc.sbuf_tensor(n, s, d))
        sem = lambda n: top.enter_context(nc.semaphore(n))
        ORDER = list(range(SAMPLE_TILE - 1, -1, -1)) + [SAMPLE_TILE]
        SECTIONS = [(t, branch) for t in ORDER for branch in range(2)]
        UNITS = len(SECTIONS) * HEADS
        STEPS = UNITS + 9
        MAX_W = N_META + N_QUERY
        q_raw = sb("q_raw3", [P, HEADS, P])
        q_st = sb("q_st3", [P, 2, HEADS, P], F32R)
        probs = sb("probs", [P, 3, MAX_W])
        pt_hi = sb("pt_hi", [P, 2, 10, 2, P], F32R)
        pt_lo = sb("pt_lo", [P, 2, 10, 2, P], F32R)
        dist_b = sb("dist_b", [P, 2, MAX_W])
        top_neg = sb("top_neg", [P, 2, HEADS])
        top_val = sb("top_val", [P, 2, 3])
        top_all = sb("top_all", [P, 3])
        sums = sb("sums", [P, 2, HEADS])
        sink_e = sb("sink_e", [P, 2, HEADS])
        inv = sb("inv", [P, 2, HEADS])
        out_t = sb("out_t", [P, 2, 2 * P])
        mixed = sb("mixed", [P, 2, D])
        gates = sb("gates", [P, 2 * D])
        merged = sb("merged", [P, D])
        T_BANK, PV_BANK, O_BANK = 3, 6, 7

        q_loaded, q_hi_done, q_lo_done = sem("p3_q_loaded"), sem("p3_q_hi_done"), sem("p3_q_lo_done")
        dist_loaded = [sem("p3_dist_loaded0"), sem("p3_dist_loaded1")]
        gates_loaded = sem("p3_gates_loaded")
        scored, topped, neg_ready, exped = sem("p3_scored"), sem("p3_topped"), sem("p3_neg_ready"), sem("p3_exped")
        turned, hi_done, lo_done = sem("p3_turned"), sem("p3_hi_done"), sem("p3_lo_done")
        valued, out_copied, folded = sem("p3_valued"), sem("p3_out_copied"), sem("p3_folded")
        sink_in, sink_done, sum_ready, inv_ready = sem("p3_sink_in"), sem("p3_sink_done"), sem("p3_sum_ready"), sem("p3_inv_ready")
        normed = sem("p3_normed")
        merge_step, merged_stored = sem("p3_merge_step"), sem("p3_merged_stored")

        def section(u):
            return SECTIONS[u // HEADS]

        def tiles_of(u):
            t, branch = section(u)
            return key_tiles(branch, t)

        def groups(u):
            n = len(tiles_of(u))
            return [(a, min(4, n - a)) for a in range(0, n, 4)]

        GROUPS = [0]
        for u in range(UNITS):
            GROUPS.append(GROUPS[-1] + len(groups(u)))

        def score_chunks(u):
            t, branch = section(u)
            w = key_columns(branch, t)
            n = -(-w // 512)
            size = -(-w // (2 * n)) * 2
            return [(i, min(w, i + size)) for i in range(0, w, size)]

        CHUNK_BASE = [0]
        for u in range(UNITS):
            CHUNK_BASE.append(CHUNK_BASE[-1] + len(score_chunks(u)))

        def keys(t, branch, h):
            if branch == 1:
                k = kv["k_b_p"] if t < SAMPLE_TILE else kv["k_b_s"]
                return [(k[:], 0, 0, key_columns(1, t))]
            g = h // 8
            if t == SAMPLE_TILE:
                return [(kv["k_a_s"][:, g], 0, 0, key_columns(0, t))]
            band0 = N_META + P * max(t - 1, 0)
            return [(kv["k_a_p"][:, g], 0, 0, N_META), (kv["k_a_p"][:, g], band0, N_META, band_width(t))]

        def values(t, branch, h):
            if branch == 1:
                return kv["v_b_p"][:] if t < SAMPLE_TILE else kv["v_b_s"][:]
            return (kv["v_a_p"] if t < SAMPLE_TILE else kv["v_a_s"])[:, h // 8]

        with nc.Block() as block:

            @block.sync
            def _(sp):
                def load_q(s):
                    t, branch = SECTIONS[s]
                    r = tile_rows(t)
                    if s >= 1:
                        sp.wait_ge(q_lo_done, s)
                    src = q_scr[branch * D:(branch + 1) * D, t * P:t * P + r].rearrange("(h d) n -> d h n", d=HD)
                    for half in range(2):
                        sp.dma_start(q_raw[half * HD:(half + 1) * HD, :, 0:r], src).then_inc(q_loaded, 16)

                def load_dist(i):
                    if i >= 2:
                        sp.wait_ge(topped, CHUNK_BASE[HEADS * 2 * (i - 1)])
                    t = ORDER[i]
                    r, w = tile_rows(t), key_columns(1, t)
                    sp.dma_start(dist_b[:r, i % 2, 0:w], dist_scr[t, 0:r, 0:w]).then_inc(dist_loaded[i % 2], 16)

                def load_gates(i):
                    t = ORDER[i]
                    r = tile_rows(t)
                    sp.dma_start(gates[:r, :], gate_scr[t * P:t * P + r, :]).then_inc(gates_loaded, 16)

                def store_merged(i):
                    t = ORDER[i]
                    r = tile_rows(t)
                    sp.wait_ge(merge_step, 3 * (i + 1))
                    sp.dma_start(merged_scr[t * P:t * P + r, :], merged[:r, :]).then_inc(merged_stored, 16)

                load_q(0)
                load_dist(0)
                load_gates(0)
                copy = lambda dst, src: sp.dma_start(dst, src).then_inc(kv["stored"], 16)
                tail = slice(N_PROMPT - WINDOW, N_PROMPT)
                flat = lambda a: a[0, 0].rearrange("n h d -> n (h d)")
                copy(flat(outs["k_a_prompt"]), t_scr[tail, T_KA:T_KA + 2 * HD])
                copy(flat(outs["v_a_prompt"]), t_scr[tail, T_VA:T_VA + 2 * HD])
                copy(flat(outs["k_b_prompt"]), t_scr[0:N_PROMPT, T_KB:T_KB + HD])
                copy(flat(outs["v_b_prompt"]), t_scr[0:N_PROMPT, T_VB:T_VB + HD])
                copy(outs["ki_b_prompt"][0, 0], t_scr[0:N_PROMPT, T_KI:T_KI + HD])
                copy(flat(outs["meta_prompt"]), t_scr[N_QUERY:N_TOK, 0:T_KI])
                copy(outs["k_a_sample"][0, 0, 0:WINDOW - N_SAMPLE], caches[0][0, 0, N_SAMPLE:WINDOW])
                copy(outs["v_a_sample"][0, 0, 0:WINDOW - N_SAMPLE], caches[1][0, 0, N_SAMPLE:WINDOW])
                copy(flat(outs["k_a_sample"])[WINDOW - N_SAMPLE:], t_scr[N_PROMPT:N_QUERY, T_KA:T_KA + 2 * HD])
                copy(flat(outs["v_a_sample"])[WINDOW - N_SAMPLE:], t_scr[N_PROMPT:N_QUERY, T_VA:T_VA + 2 * HD])
                copy(flat(outs["k_b_sample"]), t_scr[N_PROMPT:N_QUERY, T_KB:T_KB + HD])
                copy(flat(outs["v_b_sample"]), t_scr[N_PROMPT:N_QUERY, T_VB:T_VB + HD])
                copy(outs["ki_b_sample"][0, 0], t_scr[N_PROMPT:N_QUERY, T_KI:T_KI + HD])
                for s in range(len(SECTIONS)):
                    i, branch = divmod(s, 2)
                    if s + 1 < len(SECTIONS):
                        load_q(s + 1)
                    if branch == 0:
                        if i >= 1:
                            store_merged(i - 1)
                            load_gates(i)
                        if i + 1 < TILES:
                            load_dist(i + 1)
                            sp.dma_start(wo_raw[:, i, :], w_o[0, i * P:(i + 1) * P, :]).then_inc(wo_loaded, 16)
                store_merged(TILES - 1)
                sp.wait_ge(merged_stored, 16 * TILES)
                sp.wait_ge(kv["stored"], 16 * KV_COPIES)
                sp.wait_ge(wo_loaded, 16 * KT)

            @block.gpsimd
            def _(pool):
                def split_queries(s):
                    t, branch = SECTIONS[s]
                    r = tile_rows(t)
                    pool.wait_ge(q_loaded, 32 * (s + 1))
                    pool.wait_ge(q_lo_done, s)
                    if s >= 2:
                        pool.wait_ge(scored, CHUNK_BASE[HEADS * (s - 1)])
                    pool.tensor_copy(q_st[:, branch, :, 0:r], q_raw[:, :, 0:r]).then_inc(q_hi_done, 1)
                    pool.wait_ge(q_hi_done, s + 1)
                    st = q_st[HD:, branch, :, 0:r]
                    pool.tensor_tensor(st, q_raw[HD:, :, 0:r], st.bitcast(F32), ALU.subtract).then_inc(q_lo_done, 1)
                    pool.wait_ge(q_lo_done, s + 1)

                def merge_first(i):
                    r = tile_rows(ORDER[i])
                    pool.wait_ge(normed, 4 * i + 2)
                    pool.wait_ge(gates_loaded, 16 * (i + 1))
                    if i >= 1:
                        pool.wait_ge(merged_stored, 16 * i)
                    pool.tensor_tensor(merged[:r, :], mixed[:r, 0, :], gates[:r, 0:D], ALU.mult).then_inc(merge_step, 1)
                    pool.wait_ge(merge_step, 3 * i + 1)

                def merge_rest(i):
                    r = tile_rows(ORDER[i])
                    pool.wait_ge(normed, 4 * (i + 1))
                    pool.tensor_tensor(mixed[:r, 1, :], mixed[:r, 1, :], gates[:r, D:], ALU.mult).then_inc(merge_step, 1)
                    pool.wait_ge(merge_step, 3 * i + 2)
                    pool.tensor_tensor(merged[:r, :], merged[:r, :], mixed[:r, 1, :], ALU.add).then_inc(merge_step, 1)
                    pool.wait_ge(merge_step, 3 * i + 3)

                for s in range(len(SECTIONS)):
                    if s + 1 < len(SECTIONS):
                        split_queries(s + 1)
                    if s % 2 == 0 and s >= 2:
                        merge_rest(s // 2 - 1)
                    if s % 2 == 1:
                        merge_first(s // 2)

            @block.scalar
            def _(act):
                def split_hi(u):
                    t, branch = section(u)
                    r = tile_rows(t)
                    if u % 2 == 0 and u >= 4:
                        act.wait_ge(valued, u // 2 - 1)
                    for j, (a, n) in enumerate(groups(u)):
                        x = GROUPS[u] + j
                        act.wait_ge(turned, x + 1)
                        src = ps[:, T_BANK + x % 3, :].rearrange("p (k n) -> p k n", k=4)[:, 0:n, 0:r]
                        act.activation(pt_hi[:, (u // 2) % 2, a:a + n, u % 2, 0:r], src, ACT.Copy).then_inc(hi_done, 1)

                def exp(u):
                    t, branch = section(u)
                    r, w, h = tile_rows(t), key_columns(branch, t), u % HEADS
                    act.wait_ge(neg_ready, u + 1)
                    act.activation(probs[:r, u % 3, 0:w], probs[:r, u % 3, 0:w], ACT.Exp, bias=top_neg[:r, branch, h:h + 1],
                                   scale=slope(h), accum_out=sums[:r, branch, h:h + 1]).then_inc(exped, 1)

                def copy_out(p):
                    r = tile_rows(section(2 * p)[0])
                    act.wait_ge(valued, p + 1)
                    if p >= 2:
                        act.wait_ge(folded, p - 1)
                    act.activation(out_t[:, p % 2, 0:2 * r], ps[:, PV_BANK, 0:2 * r], ACT.Copy).then_inc(out_copied, 1)

                def sink_exp(half, done):
                    t, _ = section(8 * half)
                    r, hs = tile_rows(t), slice(8 * (half % 2), 8 * (half % 2) + 8)
                    act.wait_ge(sink_in, done + 1)
                    act.activation(sink_e[:r, 0, hs], sink_e[:r, 0, hs], ACT.Exp).then_inc(sink_done, 1)

                r = tile_rows(ORDER[0])
                act.wait_ge(q_loaded, 32)
                act.activation(q_st[:, 0, :, 0:r], q_raw[:, :, 0:r], ACT.Copy).then_inc(q_hi_done, 1)
                sinks = 0
                for u in range(STEPS):
                    if u >= 2 and u - 2 < UNITS:
                        split_hi(u - 2)
                    if u < UNITS:
                        exp(u)
                    if u >= 5 and u % 2 == 1 and (u - 5) // 2 < UNITS // 2:
                        copy_out((u - 5) // 2)
                    if u >= 8 and u % 8 == 0 and u <= UNITS and section(u - 8)[1] == 0:
                        sink_exp(u // 8 - 1, sinks)
                        sinks += 1

            @block.vector
            def _(dve):
                def subtract_distance(u):
                    t, branch = section(u)
                    r, w, h = tile_rows(t), key_columns(branch, t), u % HEADS
                    i = u // (2 * HEADS)
                    if branch == 1 and h == 0:
                        dve.wait_ge(dist_loaded[i % 2], 16 * (i // 2 + 1))
                    if u >= 3:
                        dve.wait_ge(turned, GROUPS[u - 2])
                    if branch == 1:
                        dist, start = dist_b[:r, i % 2, :], UNSEEN
                    else:
                        dist = (kv["dist_a0"] if t == 0 else kv["dist_a"])[:r, :]
                        start = kv["sinks_scaled"][:r, h:h + 1]
                    chunks = score_chunks(u)
                    for j, (c0, c1) in enumerate(chunks):
                        x = CHUNK_BASE[u] + j
                        dve.wait_ge(scored, x + 1)
                        dve.tensor_tensor_reduce(probs[:r, u % 3, c0:c1], ps[:r, x % 3, 0:c1 - c0], dist[:, c0:c1], 1.0, start,
                                                 ALU.subtract, ALU.max, top_val[:r, u % 2, j:j + 1]).then_inc(topped, 1)
                    dve.wait_ge(topped, CHUNK_BASE[u + 1])
                    neg = top_neg[:r, branch, h:h + 1]
                    if len(chunks) == 1:
                        dve.tensor_scalar(neg, top_val[:r, u % 2, 0:1], -slope(h), None, ALU.mult).then_inc(neg_ready, 1)
                    else:
                        n = len(chunks)
                        dve.tensor_scalar(top_all[:r, 0:n], top_val[:r, u % 2, 0:n], -slope(h), None, ALU.mult, ALU.min,
                                          accum_out=neg).then_inc(neg_ready, 1)

                def split_lo(u):
                    t, branch = section(u)
                    r = tile_rows(t)
                    for j, (a, n) in enumerate(groups(u)):
                        x = GROUPS[u] + j
                        dve.wait_ge(hi_done, x + 1)
                        src = ps[:, T_BANK + x % 3, :].rearrange("p (k n) -> p k n", k=4)[:, 0:n, 0:r]
                        at = (slice(None), (u // 2) % 2, slice(a, a + n), u % 2, slice(0, r))
                        dve.tensor_tensor(pt_lo[at], src, pt_hi[at].bitcast(F32), ALU.subtract).then_inc(lo_done, 1)

                def sink_argument(half):
                    t, _ = section(8 * half)
                    r, hs = tile_rows(t), slice(8 * (half % 2), 8 * (half % 2) + 8)
                    dve.wait_ge(neg_ready, 8 * half + 8)
                    dve.tensor_tensor(sink_e[:r, 0, hs], kv["sinks"][:r, hs], top_neg[:r, 0, hs], ALU.add).then_inc(sink_in, 1)

                def invert(half, sinks):
                    t, branch = section(8 * half)
                    r, hs = tile_rows(t), slice(8 * (half % 2), 8 * (half % 2) + 8)
                    dve.wait_ge(exped, 8 * half + 8)
                    if branch == 0:
                        dve.wait_ge(sink_done, sinks)
                        dve.tensor_tensor(sums[:r, 0, hs], sums[:r, 0, hs], sink_e[:r, 0, hs], ALU.add).then_inc(sum_ready, 1)
                        dve.wait_ge(sum_ready, sinks)
                    dve.reciprocal(inv[:r, branch, hs], sums[:r, branch, hs]).then_inc(inv_ready, 1)

                def normalise(half):
                    t, branch = section(8 * half)
                    r, hs = tile_rows(t), slice(8 * (half % 2), 8 * (half % 2) + 8)
                    dve.wait_ge(folded, 4 * half + 4)
                    dve.wait_ge(inv_ready, half + 1)
                    if half >= 4:
                        dve.wait_ge(merge_step, 3 * (half // 4))
                    out = mixed[:r, branch, 512 * (half % 2):512 * (half % 2) + 512].rearrange("p (h d) -> p h d", d=HD)
                    src = ps[:r, O_BANK, :].rearrange("p (h d) -> p h d", d=HD)
                    scale = inv[:r, branch, hs].unsqueeze(2).to_broadcast([r, 8, HD])
                    dve.tensor_tensor(out, src, scale, ALU.mult).then_inc(normed, 1)

                dve.wait_ge(q_hi_done, 1)
                st = q_st[HD:, 0, :, 0:tile_rows(ORDER[0])]
                dve.tensor_tensor(st, q_raw[HD:, :, 0:tile_rows(ORDER[0])], st.bitcast(F32), ALU.subtract).then_inc(q_lo_done, 1)
                sinks = 0
                for u in range(STEPS):
                    if u < UNITS:
                        subtract_distance(u)
                    if u >= 14 and u % 8 == 6 and (u - 14) // 8 < UNITS // 8:
                        normalise((u - 14) // 8)
                    if u >= 2 and u - 2 < UNITS:
                        split_lo(u - 2)
                    if u >= 8 and u % 8 == 0 and u <= UNITS and section(u - 8)[1] == 0:
                        sink_argument(u // 8 - 1)
                        sinks += 1
                    if u >= 8 and u % 8 == 2 and (u - 10) // 8 < UNITS // 8:
                        invert((u - 10) // 8, sinks)
                r = tile_rows(ORDER[-1])
                dve.wait_ge(normed, 4 * TILES)
                dve.wait_ge(merge_step, 3 * TILES - 2)
                dve.tensor_tensor(mixed[:r, 1, :], mixed[:r, 1, :], gates[:r, D:], ALU.mult).then_inc(merge_step, 1)
                dve.wait_ge(merge_step, 3 * TILES - 1)
                dve.tensor_tensor(merged[:r, :], merged[:r, :], mixed[:r, 1, :], ALU.add).then_inc(merge_step, 1)

            @block.tensor
            def _(pe):
                def score(u):
                    t, branch = section(u)
                    r, h, s = tile_rows(t), u % HEADS, u // HEADS
                    if h == 0:
                        pe.wait_ge(q_lo_done, s + 1)
                    for j, (c0, c1) in enumerate(score_chunks(u)):
                        x = CHUNK_BASE[u] + j
                        if x >= 3:
                            pe.wait_ge(topped, x - 2)
                        for k, k0, at, n in keys(t, branch, h):
                            a, b = max(at, c0), min(at + n, c1)
                            if a >= b:
                                continue
                            for part in range(2):
                                last = pe.matmul(ps[:r, x % 3, a - c0:b - c0], q_st[:, branch, h, 0:r],
                                                 k[:, part, k0 + a - at:k0 + b - at], start=(part == 0), stop=(part == 1))
                        last.then_inc(scored, 1)

                def turn(u):
                    t, branch = section(u)
                    r, tiles = tile_rows(t), tiles_of(u)
                    pe.wait_ge(exped, u + 1)
                    for j, (a, n) in enumerate(groups(u)):
                        x = GROUPS[u] + j
                        if x >= 3:
                            pe.wait_ge(lo_done, x - 2)
                        for b in range(n):
                            col = tiles[a + b][0]
                            last = pe.transpose(ps[:, T_BANK + x % 3, b * P:b * P + r], probs[:r, u % 3, col:col + P],
                                                c["ident"][:r, :r])
                        last.then_inc(turned, 1)

                def weigh_values(p, second):
                    u = 2 * p
                    t, branch = section(u)
                    r, tiles = tile_rows(t), tiles_of(u)
                    cut = len(tiles) // 2 if branch == 1 else 0
                    if second == 0 and cut == 0:
                        return
                    if second == 0 or cut == 0:
                        pe.wait_ge(lo_done, GROUPS[u + 2])
                        if p >= 1:
                            pe.wait_ge(out_copied, p)
                    v = values(t, branch, u % HEADS)
                    for j, (_, rows, slot) in enumerate(tiles):
                        if (j >= cut) != (second == 1):
                            continue
                        for part, pt in enumerate((pt_hi, pt_lo)):
                            last = pe.matmul(ps[:, PV_BANK, 0:2 * r], v[0:rows, slot, :], pt[0:rows, p % 2, j, :, 0:r],
                                             start=(j == 0 and part == 0), stop=(j == len(tiles) - 1 and part == 1))
                    if second == 1:
                        last.then_inc(valued, 1)

                def fold(p):
                    t, _ = section(2 * p)
                    r, half = tile_rows(t), p // 4
                    pe.wait_ge(out_copied, p + 1)
                    if p % 4 == 0 and half >= 1:
                        pe.wait_ge(normed, half)
                    for b in range(2):
                        h = (2 * p + b) % 8
                        last = pe.matmul(ps[:r, O_BANK, h * HD:(h + 1) * HD], out_t[:, p % 2, b * r:(b + 1) * r],
                                         c["fold"][:], start=True, stop=True)
                    last.then_inc(folded, 1)

                score(0)
                for u in range(STEPS):
                    if u >= 2 and u - 2 < UNITS:
                        turn(u - 2)
                    if u + 1 < UNITS:
                        score(u + 1)
                    if u >= 7 and u % 2 == 1 and (u - 7) // 2 < UNITS // 2:
                        fold((u - 7) // 2)
                    if u >= 4 and (u - 4) // 2 < UNITS // 2:
                        weigh_values((u - 4) // 2, u % 2)


def attention_buffers(ctx, top, nc):
    sb = lambda n, s, d=F32: ctx.enter_context(nc.sbuf_tensor(n, s, d))
    return {
        "stored": top.enter_context(nc.semaphore("p3_kv_stored")),
        "k_b_p": sb("k_b_p", [P, 2, N_META + N_PROMPT], F32R), "k_b_s": sb("k_b_s", [P, 2, N_META + N_QUERY], F32R),
        "k_a_p": sb("k_a_p", [P, 2, 2, N_META + N_PROMPT], F32R),
        "k_a_s": sb("k_a_s", [P, 2, 2, N_META + WINDOW + N_SAMPLE], F32R),
        "v_b_p": sb("v_b_p", [P, 9, P], F32R), "v_b_s": sb("v_b_s", [P, 10, P], F32R),
        "v_a_p": sb("v_a_p", [P, 2, 9, P], F32R), "v_a_s": sb("v_a_s", [P, 2, 3, P], F32R),
        "dist_a": sb("dist_a", [P, N_META + 2 * P]), "dist_a0": sb("dist_a0", [P, N_META + P]),
        "sinks": sb("sinks", [P, HEADS]), "sinks_scaled": sb("sinks_scaled", [P, HEADS]),
    }


CH = 256
UP_UNITS = 4


def up_weights(ctx, top, nc, w_up):
    return {"raw": ctx.enter_context(nc.sbuf_tensor("up_raw", [P, UP_UNITS, 2, CH], F32)),
            "src": w_up[0].rearrange("(u k p) f -> u p k f", k=2, p=P),
            "loaded": [top.enter_context(nc.semaphore(f"p5_up_loaded{i}")) for i in range(UP_UNITS)]}


def output_mix(nc, top, c, x2T, ps, weights, wo_raw, up, merged_scr, x_prompt, x_sample, g_post_mix, g_pre_mlp, x1_scr):
    x2T_hi, x2T_lo = x2T
    UNITS = 2 * KT
    POOL_UNITS = [n for n in range(UNITS) if n % 3 == 2]
    with ExitStack() as ctx:
        sb = lambda n, s, d=F32: ctx.enter_context(nc.sbuf_tensor(n, s, d))
        sem = lambda n: top.enter_context(nc.semaphore(n))
        w_hi = sb("wo_hi", [P, KT, D], F32R)
        w_lo = weights[:].rearrange("p (k n) -> p k n", k=KT)
        m_in = sb("m_in", [P, 2, D])
        mT_hi = sb("mT_hi", [P, 2, KT, P], F32R)
        mT_lo = sb("mT_lo", [P, 2, KT, P], F32R)
        x_in = sb("x_in4", [P, 2, D])
        x1 = sb("x1", [P, 2, D])
        x_norm = sb("x_norm4", [P, 2, D])
        squares = sb("squares4", [P, D])
        g_post = sb("g_post", [P, D])
        g_pre = sb("g_pre", [P, D])
        col = {n: sb("p4_" + n, [P, 2 * TILES]) for n in ("sum_sq", "std", "mean_sq", "rstd_0", "rstd", "newton")}

        w_hi_done, w_lo_dve, w_lo_pool = sem("p4_w_hi_done"), sem("p4_w_lo_dve"), sem("p4_w_lo_pool")
        gains_loaded = sem("p4_gains_loaded")
        m_loaded = [sem("p4_m_loaded0"), sem("p4_m_loaded1")]
        x_loaded = [sem("p4_x_loaded0"), sem("p4_x_loaded1")]
        m_turned, m_hi_done, m_lo_done = sem("p4_m_turned"), sem("p4_m_hi_done"), sem("p4_m_lo_done")
        product_done = sem("p4_product_done")
        squared, std_ready, rstd_ready, refined = sem("p4_squared"), sem("p4_std_ready"), sem("p4_rstd_ready"), sem("p4_refined")
        scaled, x1_ready = sem("p4_scaled"), sem("p4_x1_ready")
        x1_stored = [sem("p4_x1_stored0"), sem("p4_x1_stored1")]
        normed, x_turned, x_hi_done, x_lo_done = sem("p4_normed"), sem("p4_x_turned"), sem("p4_x_hi_done"), sem("p4_x_lo_done")

        def toks(t):
            return slice(t * P, t * P + tile_rows(t))

        def unit(n):
            return slice(None), n // 2, slice(512 * (n % 2), 512 * (n % 2) + 512)

        def product(t):
            return ps[:, 4 + 2 * (t % 2):6 + 2 * (t % 2), :].rearrange("p b n -> p (b n)")[:tile_rows(t)]

        def four(bank, t):
            return ps[:, bank, :].rearrange("p (k n) -> p k n", k=4)[:, :, 0:tile_rows(t)]

        with nc.Block() as block:

            @block.sync
            def _(sp):
                def load_merged(t):
                    if t >= 2:
                        sp.wait_ge(m_turned, 2 * t - 2)
                    sp.dma_start(m_in[:tile_rows(t), t % 2, :], merged_scr[toks(t), :]).then_inc(m_loaded[t % 2], 16)

                def load_x(t):
                    r = tile_rows(t)
                    if t >= 2:
                        sp.wait_ge(x1_ready, t - 1)
                    src = x_prompt[0, toks(t), :] if t < SAMPLE_TILE else x_sample[0]
                    sp.dma_start(x_in[:r, t % 2, :], src).then_inc(x_loaded[t % 2], 16)

                load_merged(0)
                load_merged(1)
                load_x(0)
                load_x(1)
                for u in range(UP_UNITS):
                    sp.dma_start(up["raw"][:, u], up["src"][u][:, :, 0:CH]).then_inc(up["loaded"][u], 16)
                sp.dma_start(g_post[:], g_post_mix[0:1, :].to_broadcast([P, D])).then_inc(gains_loaded, 16)
                sp.dma_start(g_pre[:], g_pre_mlp[0:1, :].to_broadcast([P, D])).then_inc(gains_loaded, 16)
                for t in range(TILES):
                    if t + 2 < TILES:
                        load_merged(t + 2)
                    sp.wait_ge(x1_ready, t + 1)
                    sp.dma_start(x1_scr[toks(t), :], x1[:tile_rows(t), t % 2, :]).then_inc(x1_stored[t % 2], 16)
                    if t + 2 < TILES:
                        load_x(t + 2)
                sp.wait_ge(x1_stored[0], 16 * 5)
                sp.wait_ge(x1_stored[1], 16 * 4)
                for u in range(UP_UNITS):
                    sp.wait_ge(up["loaded"][u], 16)

            @block.gpsimd
            def _(pool):
                for n in POOL_UNITS:
                    pool.wait_ge(w_hi_done, n + 1)
                    pool.tensor_tensor(w_lo[unit(n)], wo_raw[unit(n)], w_hi[unit(n)].bitcast(F32), ALU.subtract)\
                        .then_inc(w_lo_pool, 1)

            @block.scalar
            def _(act):
                def norm_statistics(t, which, src):
                    j, r = 2 * t + which, tile_rows(t)
                    act.activation(squares[:r], src, ACT.Square, accum_out=col["sum_sq"][:r, j:j + 1]).then_inc(squared, 1)
                    act.wait_ge(squared, j + 1)
                    act.activation(col["std"][:r, j:j + 1], col["sum_sq"][:r, j:j + 1], ACT.Sqrt, bias=c["eps"][:r, :],
                                   scale=1.0 / D).then_inc(std_ready, 1)

                def merged_hi(t):
                    for g in range(2):
                        act.wait_ge(m_turned, 2 * t + g + 1)
                        if t >= 2:
                            act.wait_ge(product_done, t - 1)
                        act.activation(mT_hi[:, t % 2, 4 * g:4 * g + 4, 0:tile_rows(t)], four(g, t), ACT.Copy).then_inc(m_hi_done, 1)

                def normed_hi(t):
                    for g in range(2):
                        act.wait_ge(x_turned, 2 * t + g + 1)
                        act.activation(x2T_hi[:, 4 * g:4 * g + 4, toks(t)], four(2 + g, t), ACT.Copy).then_inc(x_hi_done, 1)

                for n in range(UNITS):
                    act.activation(w_hi[unit(n)], wo_raw[unit(n)], ACT.Copy).then_inc(w_hi_done, 1)
                    if n == 3:
                        merged_hi(0)
                for t in range(1, TILES + 2):
                    if t < TILES:
                        merged_hi(t)
                    if t - 1 < TILES:
                        act.wait_ge(product_done, t)
                        norm_statistics(t - 1, 0, product(t - 1))
                    if t - 1 < TILES:
                        act.wait_ge(x1_ready, t)
                        norm_statistics(t - 1, 1, x1[:tile_rows(t - 1), (t - 1) % 2, :])
                    if 0 <= t - 2:
                        normed_hi(t - 2)

            @block.vector
            def _(dve):
                def rstd(t, which):
                    j, r = 2 * t + which, tile_rows(t)
                    one = lambda n: col[n][:r, j:j + 1]
                    dve.wait_ge(std_ready, j + 1)
                    dve.reciprocal(one("rstd_0"), one("std")).then_inc(rstd_ready, 1)
                    dve.tensor_scalar(one("mean_sq"), one("sum_sq"), 1.0 / D, EPS, ALU.mult, ALU.add).then_inc(rstd_ready, 1)
                    dve.wait_ge(rstd_ready, 2 * j + 2)
                    refine_rstd(dve, refined, 3 * j, one("rstd"), one("rstd_0"), one("mean_sq"), one("newton"))
                    return one("rstd")

                def merged_lo(t):
                    for g in range(2):
                        dve.wait_ge(m_hi_done, 2 * t + g + 1)
                        at = (slice(None), t % 2, slice(4 * g, 4 * g + 4), slice(0, tile_rows(t)))
                        dve.tensor_tensor(mT_lo[at], four(g, t), mT_hi[at].bitcast(F32), ALU.subtract).then_inc(m_lo_done, 1)

                def normed_lo(t):
                    for g in range(2):
                        dve.wait_ge(x_hi_done, 2 * t + g + 1)
                        at = (slice(None), slice(4 * g, 4 * g + 4), toks(t))
                        dve.tensor_tensor(x2T_lo[at], four(2 + g, t), x2T_hi[at].bitcast(F32), ALU.subtract).then_inc(x_lo_done, 1)

                def scale_product(t):
                    r = tile_rows(t)
                    s = rstd(t, 0)
                    if t >= 2:
                        dve.wait_ge(x1_stored[t % 2], 16 * (t // 2))
                        dve.wait_ge(normed, t - 1)
                    dve.scalar_tensor_tensor(out=x1[:r, t % 2, :], in0=product(t), scalar=s, in1=g_post[:r, :],
                                             op0=ALU.mult, op1=ALU.mult).then_inc(scaled, 1)
                    dve.wait_ge(scaled, t + 1)
                    dve.wait_ge(x_loaded[t % 2], 16 * (t // 2 + 1))
                    dve.tensor_tensor(x1[:r, t % 2, :], x1[:r, t % 2, :], x_in[:r, t % 2, :], ALU.add).then_inc(x1_ready, 1)

                def norm_x1(t):
                    r = tile_rows(t)
                    s = rstd(t, 1)
                    if t >= 2:
                        dve.wait_ge(x_turned, 2 * t - 2)
                    dve.scalar_tensor_tensor(out=x_norm[:r, t % 2, :], in0=x1[:r, t % 2, :], scalar=s, in1=g_pre[:r, :],
                                             op0=ALU.mult, op1=ALU.mult).then_inc(normed, 1)

                for n in range(UNITS):
                    if n not in POOL_UNITS:
                        dve.wait_ge(w_hi_done, n + 1)
                        dve.tensor_tensor(w_lo[unit(n)], wo_raw[unit(n)], w_hi[unit(n)].bitcast(F32), ALU.subtract)\
                           .then_inc(w_lo_dve, 1)
                    if n == 4:
                        merged_lo(0)
                dve.wait_ge(gains_loaded, 32)
                for t in range(1, TILES + 2):
                    if t < TILES:
                        merged_lo(t)
                    if t - 1 < TILES:
                        scale_product(t - 1)
                    if t - 1 < TILES:
                        norm_x1(t - 1)
                    if 0 <= t - 2:
                        normed_lo(t - 2)

            @block.tensor
            def _(pe):
                def turn_merged(t):
                    pe.wait_ge(m_loaded[t % 2], 16 * (t // 2 + 1))
                    for g in range(2):
                        if t >= 1:
                            pe.wait_ge(m_lo_done, 2 * t + g - 1)
                        for k in range(4):
                            last = pe.transpose(ps[:, g, k * P:k * P + tile_rows(t)],
                                                m_in[:tile_rows(t), t % 2, (4 * g + k) * P:(4 * g + k + 1) * P],
                                                c["ident"][:tile_rows(t), :tile_rows(t)])
                        last.then_inc(m_turned, 1)

                def turn_normed(t):
                    pe.wait_ge(normed, t + 1)
                    for g in range(2):
                        if t >= 1:
                            pe.wait_ge(x_lo_done, 2 * t + g - 1)
                        for k in range(4):
                            last = pe.transpose(ps[:, 2 + g, k * P:k * P + tile_rows(t)],
                                                x_norm[:tile_rows(t), t % 2, (4 * g + k) * P:(4 * g + k + 1) * P],
                                                c["ident"][:tile_rows(t), :tile_rows(t)])
                        last.then_inc(x_turned, 1)

                def multiply(t):
                    r = tile_rows(t)
                    pe.wait_ge(m_lo_done, 2 * t + 2)
                    if t >= 2:
                        pe.wait_ge(scaled, t - 1)
                    for k in range(KT):
                        m_hi, m_lo = mT_hi[:, t % 2, k, 0:r], mT_lo[:, t % 2, k, 0:r]
                        for half in range(2):
                            if t == 0:
                                n = 2 * k + half
                                pe.wait_ge(w_lo_dve, sum(m not in POOL_UNITS for m in range(n + 1)))
                                if n >= POOL_UNITS[0]:
                                    pe.wait_ge(w_lo_pool, sum(m in POOL_UNITS for m in range(n + 1)))
                            cols = slice(512 * half, 512 * half + 512)
                            for j, (a, b) in enumerate(((m_hi, w_hi), (m_hi, w_lo), (m_lo, w_hi))):
                                last = pe.matmul(product(t)[:, cols], a, b[:, k, cols], start=(k == 0 and j == 0),
                                                 stop=(k == KT - 1 and j == 2))
                    last.then_inc(product_done, 1)

                turn_merged(0)
                for t in range(1, TILES + 2):
                    if t < TILES:
                        turn_merged(t)
                    if t - 1 < TILES:
                        multiply(t - 1)
                    if 0 <= t - 2:
                        turn_normed(t - 2)


def mlp(nc, top, c, x2T, ps, weights, up, w_down, g_post_mlp, x1_scr, y_prompt, y_sample):
    x2T_hi, x2T_lo = x2T
    FT = CH // P
    N_CH = D_FF // CH
    DOWN_UNITS = 4
    UP_GROUPS = [(f, t0, n) for f in range(FT) for t0, n in TOK_BLOCKS]
    DOWN_GROUPS = [(t, half) for t in range(TILES) for half in range(2)]
    N_UP, N_DOWN = len(UP_GROUPS), len(DOWN_GROUPS)
    UP_BANKS = 2
    DOWN_BANKS = 6
    with ExitStack() as ctx:
        sb = lambda n, s, d=F32: ctx.enter_context(nc.sbuf_tensor(n, s, d))
        sem = lambda n: top.enter_context(nc.semaphore(n))
        up_raw, up_loaded, up_src = up["raw"], up["loaded"], up["src"]
        down_raw = sb("down_raw", [P, DOWN_UNITS, 512])
        size = KT * CH
        quarter = [weights[:, i * size:(i + 1) * size] for i in range(4)]
        up_hi, up_lo = (w.rearrange("p (k n) -> p k n", k=KT) for w in quarter[:2])
        down_hi, down_lo = (w.rearrange("p (k n) -> p k n", k=FT) for w in quarter[2:])
        hidden = sb("hidden", [P, 2, 364])
        hid_hi = sb("hid_hi", [P, FT, N_QUERY], F32R)
        hid_lo = sb("hid_lo", [P, FT, N_QUERY], F32R)
        total = sb("total", [P, TILES, D])
        x1_in = sb("x1_in", [P, 2, D])
        squares = sb("squares5", [P, D])
        gain = sb("gain5", [P, D])
        col = {n: sb("p5_" + n, [P, TILES]) for n in ("sum_sq", "std", "mean_sq", "rstd_0", "rstd", "newton")}

        down_loaded = [sem(f"p5_down_loaded{i}") for i in range(DOWN_UNITS)]
        up_hi_done, up_lo_done = sem("p5_up_hi_done"), sem("p5_up_lo_done")
        down_hi_done, down_lo_done = sem("p5_down_hi_done"), sem("p5_down_lo_done")
        up_done, relu_done, squared_done, hid_hi_done, hid_lo_done = (sem("p5_" + n) for n in ("up_done", "relu_done", "squared_done", "hid_hi_done", "hid_lo_done"))
        down_done, added = sem("p5_down_done"), sem("p5_added")
        gain_loaded = sem("p5_gain_loaded")
        x1_loaded = [sem("p5_x1_loaded0"), sem("p5_x1_loaded1")]
        sq_done, std_ready, rstd_ready, refined = sem("p5_sq_done"), sem("p5_std_ready"), sem("p5_rstd_ready"), sem("p5_refined")
        scaled, y_ready, y_stored = sem("p5_scaled"), sem("p5_y_ready"), sem("p5_y_stored")

        def toks(t):
            return slice(t * P, t * P + tile_rows(t))

        FIRST_BY_DVE = range(1, KT, 2)

        with nc.Block() as block:

            def store_y(sp, t):
                r = tile_rows(t)
                sp.wait_ge(y_ready, t + 1)
                dst = y_prompt[0, toks(t), :] if t < SAMPLE_TILE else y_sample[0]
                sp.dma_start(dst, total[:r, t, :]).then_inc(y_stored, 16)

            @block.sync
            def _(sp):
                def load_up(j, all_split=False):
                    for u in range(UP_UNITS):
                        if all_split:
                            sp.wait_ge(up_lo_done, KT)
                        else:
                            sp.wait_ge(up_lo_done, (j - 1) * KT + (2 * u + 2))
                        sp.dma_start(up_raw[:, u], up_src[u][:, :, bass.ds(j * CH, CH)]).then_inc(up_loaded[u], 16)

                def load_down(j, first):
                    for u in range(DOWN_UNITS):
                        f, half = divmod(u, 2)
                        if not first:
                            sp.wait_ge(down_lo_done, (j - 1) * DOWN_UNITS + (u + 1))
                        src = w_down[0, bass.ds(j * CH + f * P, P), 512 * half:512 * half + 512]
                        sp.dma_start(down_raw[:, u, :], src).then_inc(down_loaded[u], 16)

                load_down(0, True)
                sp.dma_start(gain[:], g_post_mlp[0:1, :].to_broadcast([P, D])).then_inc(gain_loaded, 16)
                load_up(1, all_split=True)
                load_down(1, False)
                with sp.Fori(2, N_CH) as j:
                    load_up(j)
                    load_down(j, False)
                for t in range(TILES):
                    if t >= 2:
                        sp.wait_ge(y_ready, t - 1)
                    sp.dma_start(x1_in[:tile_rows(t), t % 2, :], x1_scr[toks(t), :]).then_inc(x1_loaded[t % 2], 16)
                    if t >= 1:
                        store_y(sp, t - 1)
                store_y(sp, TILES - 1)
                sp.wait_ge(y_stored, 16 * TILES)

            @block.gpsimd
            def _(pool):
                def split_up_lo(j, units=range(KT)):
                    for k in units:
                        pool.wait_ge(up_hi_done, j * KT + (k + 1))
                        pool.tensor_tensor(up_lo[:, k, :], up_raw[:, k // 2, k % 2, :], up_hi[:, k, :].bitcast(F32),
                                           ALU.subtract).then_inc(up_lo_done, 1)

                def split_down_lo(j):
                    for u in range(DOWN_UNITS):
                        f, half = divmod(u, 2)
                        at = (slice(None), f, slice(512 * half, 512 * half + 512))
                        pool.wait_ge(down_hi_done, j * DOWN_UNITS + (u + 1))
                        pool.tensor_tensor(down_lo[at], down_raw[:, u, :], down_hi[at].bitcast(F32), ALU.subtract).then_inc(down_lo_done, 1)

                split_up_lo(0, units=[k for k in range(KT) if k not in FIRST_BY_DVE])
                with pool.Fori(0, N_CH - 1) as j:
                    split_down_lo(j)
                    split_up_lo(j + 1)
                split_down_lo(N_CH - 1)
                pool.wait_ge(down_lo_done, N_CH * DOWN_UNITS)
                for t in range(TILES):
                    r = tile_rows(t)
                    pool.wait_ge(scaled, t + 1)
                    pool.wait_ge(x1_loaded[t % 2], 16 * (t // 2 + 1))
                    pool.tensor_tensor(total[:r, t, :], total[:r, t, :], x1_in[:r, t % 2, :], ALU.add).then_inc(y_ready, 1)
                    pool.wait_ge(y_ready, t + 1)

            @block.scalar
            def _(act):
                def split_up_hi(j, first=False):
                    if not first:
                        act.wait_ge(up_done, j * N_UP)
                    for k in range(KT):
                        act.wait_ge(up_loaded[k // 2], (j + 1) * 16)
                        act.activation(up_hi[:, k, :], up_raw[:, k // 2, k % 2, :], ACT.Copy).then_inc(up_hi_done, 1)

                def chunk(j, first=False):
                    for g in range(N_UP + 1):
                        if g < DOWN_UNITS:
                            fd, half = divmod(g, 2)
                            act.wait_ge(down_done, j * N_DOWN)
                            act.wait_ge(down_loaded[g], (j + 1) * 16)
                            act.activation(down_hi[:, fd, 512 * half:512 * half + 512], down_raw[:, g, :], ACT.Copy)\
                               .then_inc(down_hi_done, 1)
                        if g < N_UP:
                            n = UP_GROUPS[g][2]
                            act.wait_ge(up_done, j * N_UP + (g + 1))
                            if g >= 2:
                                act.wait_ge(hid_lo_done, j * N_UP + (g - 1))
                            elif not first:
                                act.wait_ge(hid_lo_done, j * N_UP)
                            act.activation(hidden[:, g % 2, 0:n], ps[:, g % UP_BANKS, 0:n], ACT.Relu).then_inc(relu_done, 1)
                        if g >= 1:
                            f, t0, n = UP_GROUPS[g - 1]
                            act.wait_ge(squared_done, j * N_UP + g)
                            act.activation(hid_hi[:, f, t0:t0 + n], hidden[:, (g - 1) % 2, 0:n], ACT.Copy).then_inc(hid_hi_done, 1)

                split_up_hi(0, first=True)
                chunk(0, first=True)
                with act.Fori(1, N_CH) as j:
                    split_up_hi(j)
                    chunk(j)
                for t in range(TILES):
                    r = tile_rows(t)
                    act.wait_ge(added, (N_CH - 1) * N_DOWN + 2 * t + 2)
                    act.activation(squares[:r], total[:r, t, :], ACT.Square, accum_out=col["sum_sq"][:r, t:t + 1]).then_inc(sq_done, 1)
                    act.wait_ge(sq_done, t + 1)
                    act.activation(col["std"][:r, t:t + 1], col["sum_sq"][:r, t:t + 1], ACT.Sqrt, bias=c["eps"][:r, :],
                                   scale=1.0 / D).then_inc(std_ready, 1)

            @block.vector
            def _(dve):
                def square_hidden(j):
                    for g in range(N_UP + 1):
                        if g < N_UP:
                            h = hidden[:, g % 2, 0:UP_GROUPS[g][2]]
                            dve.wait_ge(relu_done, j * N_UP + (g + 1))
                            dve.tensor_tensor(h, h, h, ALU.mult).then_inc(squared_done, 1)
                        if g >= 1:
                            f, t0, n = UP_GROUPS[g - 1]
                            dve.wait_ge(hid_hi_done, j * N_UP + g)
                            dve.tensor_tensor(hid_lo[:, f, t0:t0 + n], hidden[:, (g - 1) % 2, 0:n],
                                              hid_hi[:, f, t0:t0 + n].bitcast(F32), ALU.subtract).then_inc(hid_lo_done, 1)

                def add_down(j, g, first=False):
                    t, half = DOWN_GROUPS[g]
                    r = tile_rows(t)
                    out = total[:r, t, 512 * half:512 * half + 512]
                    dve.wait_ge(down_done, j * N_DOWN + (g + 1))
                    if first:
                        dve.tensor_copy(out, ps[:r, UP_BANKS + g % DOWN_BANKS, :]).then_inc(added, 1)
                        return
                    dve.tensor_tensor(out, out, ps[:r, UP_BANKS + g % DOWN_BANKS, :], ALU.add).then_inc(added, 1)

                def scale_total(t):
                    r = tile_rows(t)
                    one = lambda n: col[n][:r, t:t + 1]
                    dve.wait_ge(std_ready, t + 1)
                    dve.reciprocal(one("rstd_0"), one("std")).then_inc(rstd_ready, 1)
                    dve.tensor_scalar(one("mean_sq"), one("sum_sq"), 1.0 / D, EPS, ALU.mult, ALU.add).then_inc(rstd_ready, 1)
                    dve.wait_ge(rstd_ready, 2 * t + 2)
                    refine_rstd(dve, refined, 3 * t, one("rstd"), one("rstd_0"), one("mean_sq"), one("newton"))
                    dve.scalar_tensor_tensor(out=total[:r, t, :], in0=total[:r, t, :], scalar=one("rstd"), in1=gain[:r, :],
                                             op0=ALU.mult, op1=ALU.mult).then_inc(scaled, 1)

                for k in FIRST_BY_DVE:
                    dve.wait_ge(up_hi_done, k + 1)
                    dve.tensor_tensor(up_lo[:, k, :], up_raw[:, k // 2, k % 2, :], up_hi[:, k, :].bitcast(F32),
                                      ALU.subtract).then_inc(up_lo_done, 1)
                square_hidden(0)
                for g in range(N_DOWN):
                    add_down(0, g, first=True)
                with dve.Fori(1, N_CH - 1) as j:
                    dve.wait_ge(added, j * N_DOWN)
                    square_hidden(j)
                    for g in range(N_DOWN):
                        add_down(j, g)
                dve.wait_ge(added, (N_CH - 1) * N_DOWN)
                square_hidden(N_CH - 1)
                dve.wait_ge(gain_loaded, 16)
                for t in range(TILES):
                    add_down(N_CH - 1, 2 * t)
                    add_down(N_CH - 1, 2 * t + 1)
                    if t >= 2:
                        scale_total(t - 2)
                scale_total(TILES - 2)
                scale_total(TILES - 1)

            @block.tensor
            def _(pe):
                def chunk(j, first=False):
                    pe.wait_ge(up_lo_done, (j + 1) * KT)
                    for g, (f, t0, n) in enumerate(UP_GROUPS):
                        if g >= UP_BANKS:
                            pe.wait_ge(relu_done, j * N_UP + (g - UP_BANKS + 1))
                        elif not first:
                            pe.wait_ge(relu_done, j * N_UP - UP_BANKS + (g + 1))
                        fs = slice(f * P, (f + 1) * P)
                        for k in range(KT):
                            x_hi, x_lo = x2T_hi[:, k, t0:t0 + n], x2T_lo[:, k, t0:t0 + n]
                            for i, (a, b) in enumerate(((up_hi, x_hi), (up_hi, x_lo), (up_lo, x_hi))):
                                last = pe.matmul(ps[:, g % UP_BANKS, 0:n], a[:, k, fs], b, start=(k == 0 and i == 0),
                                                 stop=(k == KT - 1 and i == 2))
                        last.then_inc(up_done, 1)
                    pe.wait_ge(down_lo_done, (j + 1) * DOWN_UNITS)
                    for g, (t, half) in enumerate(DOWN_GROUPS):
                        r = tile_rows(t)
                        block_of = max(b for b, (t0, n) in enumerate(TOK_BLOCKS) if t0 < t * P + r)
                        if half == 0:
                            pe.wait_ge(hid_lo_done, j * N_UP + (len(TOK_BLOCKS) * (FT - 1) + block_of + 1))
                        if g >= DOWN_BANKS:
                            pe.wait_ge(added, j * N_DOWN + (g - DOWN_BANKS + 1))
                        elif not first:
                            pe.wait_ge(added, (j - 1) * N_DOWN + (N_DOWN - DOWN_BANKS + g + 1))
                        cols = slice(512 * half, 512 * half + 512)
                        for f in range(FT):
                            h_hi, h_lo = hid_hi[:, f, toks(t)], hid_lo[:, f, toks(t)]
                            for i, (a, b) in enumerate(((h_hi, down_hi), (h_hi, down_lo), (h_lo, down_hi))):
                                last = pe.matmul(ps[:r, UP_BANKS + g % DOWN_BANKS, :], a, b[:, f, cols],
                                                 start=(f == 0 and i == 0), stop=(f == FT - 1 and i == 2))
                        last.then_inc(down_done, 1)

                chunk(0, first=True)
                with pe.Fori(1, N_CH) as j:
                    chunk(j)


def streaming_step(nc, a, o):
    scratch = lambda name, shape: nc.dram_tensor(name, shape, F32).ap()
    t_scr = scratch("t_scr", (N_TOK, T_WIDTH))
    q_scr = scratch("q_scr", (2 * D + IDX_HEADS * HD, N_QUERY))
    gate_scr = scratch("gate_scr", (N_QUERY, 2 * D))
    dist_scr = scratch("dist_scr", (TILES, P, N_META + N_QUERY))
    merged_scr = scratch("merged_scr", (N_QUERY, D))
    x1_scr = scratch("x1_scr", (N_QUERY, D))
    caches = [a[n] for n in ("cache_k_a", "cache_v_a", "cache_k_b", "cache_v_b", "cache_meta")]
    with ExitStack() as top:
        c = constants(lambda n, s: top.enter_context(nc.sbuf_tensor(n, s, F32)))
        ps = top.enter_context(nc.psum_tensor("ps", [P, 8, 512], F32))
        with nc.sbuf_tensor("weights", [P, KT * D], F32R) as weights:
            pass
        wo_raw = top.enter_context(nc.sbuf_tensor("wo_raw", [P, KT, D], F32))
        wo_loaded = top.enter_context(nc.semaphore("wo_loaded"))
        ws = weight_signals(top, nc)
        with ExitStack() as mixers:
            ctx = ExitStack()
            xT = [ctx.enter_context(nc.sbuf_tensor(n, [P, KT, N_TOK], F32R)) for n in ("xT_hi", "xT_lo")]
            b2 = weight_buffers(ctx, nc, weights)
            input_norm(nc, top, c, xT, b2, ws, ps, a["w_in"], a["x_prompt"], a["x_sample"], a["meta_tokens"], a["g_pre_mix"])
            b2 |= projection_buffers(ctx, nc)
            sel = selection_buffers(ctx, nc)
            ctx.close()
            kv = attention_buffers(mixers, top, nc)
            with ExitStack() as ctx:
                raw = operand_buffers(ctx, nc)
                projection(nc, top, c, xT, b2, ws, sel, kv, raw, ps, a["w_in"], caches, a["cache_ki_b"], a["attn_sinks"],
                           t_scr, q_scr, gate_scr, dist_scr)
            attention(nc, top, c, ps, kv, wo_raw, wo_loaded, a["w_o"], q_scr, gate_scr, dist_scr, merged_scr, t_scr, caches, o)
        with ExitStack() as ctx:
            x2T = [ctx.enter_context(nc.sbuf_tensor(n, [P, KT, N_QUERY], F32R)) for n in ("x2T_hi", "x2T_lo")]
            up = up_weights(ctx, top, nc, a["w_up"])
            output_mix(nc, top, c, x2T, ps, weights, wo_raw, up, merged_scr, a["x_prompt"], a["x_sample"], a["g_post_mix"],
                       a["g_pre_mlp"], x1_scr)
            mlp(nc, top, c, x2T, ps, weights, up, a["w_down"], a["g_post_mlp"], x1_scr, o["y_prompt"], o["y_sample"])


_INS = ["x_prompt", "x_sample", "cache_k_a", "cache_v_a", "cache_k_b", "cache_v_b", "cache_ki_b", "cache_meta",
        "meta_tokens", "g_pre_mix", "w_in", "attn_sinks", "w_o", "g_post_mix", "g_pre_mlp", "w_up", "w_down", "g_post_mlp"]
_OUTS = [("y_prompt", (1, N_PROMPT, D)), ("y_sample", (1, N_SAMPLE, D)),
         ("k_a_prompt", (1, 1, WINDOW, 2, HD)), ("v_a_prompt", (1, 1, WINDOW, 2, HD)),
         ("k_b_prompt", (1, 1, N_PROMPT, 1, HD)), ("v_b_prompt", (1, 1, N_PROMPT, 1, HD)),
         ("ki_b_prompt", (1, 1, N_PROMPT, HD)), ("meta_prompt", (1, 1, N_META, 6, HD)),
         ("k_a_sample", (1, 1, WINDOW, 2, HD)), ("v_a_sample", (1, 1, WINDOW, 2, HD)),
         ("k_b_sample", (1, 1, N_SAMPLE, 1, HD)), ("v_b_sample", (1, 1, N_SAMPLE, 1, HD)),
         ("ki_b_sample", (1, 1, N_SAMPLE, HD))]


def kernel(**inputs):
    import numpy as np
    import concourse.bacc as bacc
    from concourse.bass_utils import run_bass_kernel_spmd

    nc = bacc.Bacc("TRN2", target_bir_lowering=False, num_devices=1)
    arrays, a, o = {}, {}, {}
    for name in _INS:
        arrays[f"in_{name}"] = np.ascontiguousarray(inputs[name])
        a[name] = nc.dram_tensor(f"in_{name}", arrays[f"in_{name}"].shape, F32, kind="ExternalInput").ap()
    for name, shape in _OUTS:
        o[name] = nc.dram_tensor(f"out_{name}", shape, F32, kind="ExternalOutput").ap()
    streaming_step(nc, a, o)
    r = run_bass_kernel_spmd(nc, [arrays], core_ids=[0])
    return tuple(r.results[0][f"out_{name}"] for name, _ in _OUTS)
```
